# Optimizing a Trainium2 kernel written in Bass

```python
import jax
import jax.numpy as jnp
from jax import lax
import numpy as np
import jax, jax.numpy as jnp

D_MODEL = 1024
BATCH = 1
SEQ = 512
DEPTH = 2

GRID_W = 64
CTX_LEN = 256
INNER = 2 * D_MODEL
NA_HEADS = 16
NA_DIM = D_MODEL // NA_HEADS
NA_WIDTH = NA_HEADS * NA_DIM
NA_WIN_H = 8
NA_WIN_W = 16
ML_HEADS = 4
ML_DIM = D_MODEL // ML_HEADS
ML_WIDTH = ML_HEADS * ML_DIM
ML_CHUNK = 64
HG_HEADS = 16
HG_KDIM = 128
HG_VDIM = INNER // HG_HEADS
HG_KW = HG_HEADS * HG_KDIM
HG_VW = HG_HEADS * HG_VDIM
HG_CHUNK = 32
ROPE_BASE = 10000.0
EPS = 1e-6
N_AB = (DEPTH + 1) // 2
N_C = DEPTH // 2
AB_SIZES = (NA_WIDTH,) * 4 + (ML_WIDTH,) * 5 + (4 * ML_HEADS,)
C_SIZES = (HG_KW, HG_KW, HG_KW, HG_VW, HG_VW)
AB_IN = sum(AB_SIZES)
C_IN = sum(C_SIZES)
F32 = jnp.float32


def _rms(x, w):
    xf = x.astype(F32)
    y = xf * lax.rsqrt(jnp.mean(xf * xf, axis=-1, keepdims=True) + EPS)
    return (y * w.astype(F32)).astype(x.dtype)

def _heads(t, n):
    return t.reshape(t.shape[:-1] + (n, t.shape[-1] // n))

def _bht(a):
    return jnp.swapaxes(a, 1, 2).astype(F32)

def _split_cols(p, sizes):
    return jnp.split(p, [int(s) for s in np.cumsum(sizes)[:-1]], axis=-1)

def _same(a):
    return a

def _flip_t(a):
    return jnp.flip(a, axis=2)

def _ada(cvec, w, b):
    m = jax.nn.silu(cvec) @ w + b
    return jnp.split(m.reshape((-1, 1, m.shape[-1])), 3, axis=-1)

def _rope_1d(x, pos):
    half = x.shape[-1] // 2
    freqs = ROPE_BASE ** (-jnp.arange(half, dtype=F32) / half)
    ang = pos.astype(F32)[:, None] * freqs[None, :]
    cos, sin = jnp.cos(ang)[:, None, :], jnp.sin(ang)[:, None, :]
    x1, x2 = x[..., :half], x[..., half:]
    return jnp.concatenate([x1 * cos - x2 * sin, x2 * cos + x1 * sin], axis=-1)

def _axial_rope(x):
    t = jnp.arange(x.shape[1])
    half = x.shape[-1] // 2
    xf = x.astype(F32)
    out = jnp.concatenate([_rope_1d(xf[..., :half], t // GRID_W),
                           _rope_1d(xf[..., half:], t % GRID_W)], axis=-1)
    return out.astype(x.dtype)

def _to_chunks(a, L):
    B, H, T = a.shape[:3]
    return jnp.moveaxis(a.reshape((B, H, T // L, L) + a.shape[3:]), 2, 0)

def _from_chunks(a):
    a = jnp.moveaxis(a, 0, 2)
    return a.reshape(a.shape[:2] + (-1,) + a.shape[4:])

def _mlstm_chunkwise(q, k, v, ig, fg, state):
    L = ML_CHUNK
    lf = jax.nn.log_sigmoid(fg)
    tri = jnp.tril(jnp.ones((L, L), bool))

    def step(carry, xs):
        C, n, m = carry
        qc, kc, vc, ic, lfc = xs
        b = jnp.cumsum(lfc, axis=-1)
        dmat = jnp.where(tri, b[..., :, None] - b[..., None, :] + ic[..., None, :], -jnp.inf)
        m_inter = b + m[..., None]
        m_t = jnp.maximum(jnp.max(dmat, axis=-1), m_inter)
        s = jnp.einsum('bhtk,bhsk->bhts', qc, kc) * jnp.exp(dmat - m_t[..., None])
        carry_w = jnp.exp(m_inter - m_t)
        num = jnp.einsum('bhts,bhsv->bhtv', s, vc) + carry_w[..., None] * jnp.einsum('bhtk,bhkv->bhtv', qc, C)
        den = jnp.sum(s, axis=-1) + carry_w * jnp.einsum('bhtk,bhk->bht', qc, n)
        h = num / jnp.maximum(jnp.abs(den), jnp.exp(-m_t))[..., None]
        bL = b[..., -1]
        g = bL[..., None] - b + ic
        m_new = jnp.maximum(bL + m, jnp.max(g, axis=-1))
        kw = kc * jnp.exp(g - m_new[..., None])[..., None]
        dec = jnp.exp(bL + m - m_new)
        C = dec[..., None, None] * C + jnp.einsum('bhsk,bhsv->bhkv', kw, vc)
        n = dec[..., None] * n + jnp.sum(kw, axis=2)
        return (C, n, m_new), h

    xs = tuple(_to_chunks(a, L) for a in (q, k, v, ig, lf))
    state, h = lax.scan(step, state, xs)
    return _from_chunks(h), state

def _mlstm_final_state(k, v, ig, fg):
    b = jnp.cumsum(jax.nn.log_sigmoid(fg), axis=-1)
    g = b[..., -1:] - b + ig
    m = jnp.max(g, axis=-1)
    kw = k * jnp.exp(g - m[..., None])[..., None]
    return (jnp.einsum('bhsk,bhsv->bhkv', kw, v), jnp.sum(kw, axis=2), m)

def _mlstm_bidir(lat, ctx, need_ctx):
    q_l, k_l, v_l, g_l = lat
    q_c, k_c, v_c, g_c = ctx
    B, H, _, dk = q_l.shape
    dv = v_l.shape[-1]
    out_l, out_c = [], []
    for d, tr in enumerate((_same, _flip_t)):
        ic, fc = tr(g_c[..., 2 * d]), tr(g_c[..., 2 * d + 1])
        il, fl = tr(g_l[..., 2 * d]), tr(g_l[..., 2 * d + 1])
        if need_ctx:
            zero = (jnp.zeros((B, H, dk, dv), F32), jnp.zeros((B, H, dk), F32), jnp.zeros((B, H), F32))
            h_c, st = _mlstm_chunkwise(tr(q_c), tr(k_c), tr(v_c), ic, fc, zero)
            out_c.append(tr(h_c))
        else:
            st = _mlstm_final_state(tr(k_c), tr(v_c), ic, fc)
        h_l, _ = _mlstm_chunkwise(tr(q_l), tr(k_l), tr(v_l), il, fl, st)
        out_l.append(tr(h_l))
    return out_l[0] + out_l[1], (out_c[0] + out_c[1] if need_ctx else None)

def _gla_chunkwise(q, k, v, lf, S):
    L = HG_CHUNK
    tri = jnp.tril(jnp.ones((L, L), bool))[..., None]

    def step(S, xs):
        qc, kc, vc, lfc = xs
        b = jnp.cumsum(lfc, axis=2)
        o = jnp.einsum('bhtk,bhkv->bhtv', qc * jnp.exp(b), S)
        pair = jnp.exp(jnp.where(tri, b[:, :, :, None, :] - b[:, :, None, :, :], -jnp.inf))
        a = jnp.einsum('bhtk,bhtsk->bhts', qc, pair * kc[:, :, None, :, :])
        o = o + jnp.einsum('bhts,bhsv->bhtv', a, vc)
        bL = b[:, :, -1:, :]
        S = jnp.exp(bL[:, :, 0])[..., None] * S + jnp.einsum('bhsk,bhsv->bhkv', kc * jnp.exp(bL - b), vc)
        return S, o

    xs = tuple(_to_chunks(a, L) for a in (q, k, v, lf))
    S, o = lax.scan(step, S, xs)
    return _from_chunks(o), S

def _gla_final_state(k, v, lf):
    b = jnp.cumsum(lf, axis=2)
    return jnp.einsum('bhsk,bhsv->bhkv', k * jnp.exp(b[:, :, -1:] - b), v)

def _gla_bidir(lat, ctx, need_ctx):
    q_l, v_l, dirs_l = lat
    q_c, v_c, dirs_c = ctx
    B, H, _, dk = q_l.shape
    dv = v_l.shape[-1]
    out_l, out_c = [], []
    for d, tr in enumerate((_same, _flip_t)):
        (k_l, lf_l), (k_c, lf_c) = dirs_l[d], dirs_c[d]
        if need_ctx:
            o_c, S = _gla_chunkwise(tr(q_c), tr(k_c), tr(v_c), tr(lf_c), jnp.zeros((B, H, dk, dv), F32))
            out_c.append(tr(o_c))
        else:
            S = _gla_final_state(tr(k_c), tr(v_c), tr(lf_c))
        o_l, _ = _gla_chunkwise(tr(q_l), tr(k_l), tr(v_l), tr(lf_l), S)
        out_l.append(tr(o_l))
    return out_l[0] + out_l[1], (out_c[0] + out_c[1] if need_ctx else None)

def _neighbourhood_attention(q, k, v, k_ctx, v_ctx, rpb):
    B, T, H, d = q.shape
    rows = T // GRID_W
    kh, kw = min(NA_WIN_H, rows), NA_WIN_W
    qg = (q * (d ** -0.5)).reshape(B, rows, GRID_W, H, d)
    kg = k.reshape(B, rows, GRID_W, H, d)
    vg = v.reshape(B, rows, GRID_W, H, d)
    col = jnp.arange(GRID_W)
    col_idx = jnp.clip(col - kw // 2, 0, GRID_W - kw)[:, None] + jnp.arange(kw)[None, :]
    col_bias = rpb[:, :, col_idx - col[:, None] + NA_WIN_W - 1]

    def one_row(r):
        r0 = jnp.clip(r - kh // 2, 0, rows - kh)
        q_r = lax.dynamic_index_in_dim(qg, r, axis=1, keepdims=False)
        k_nb = lax.dynamic_slice_in_dim(kg, r0, kh, axis=1)[:, :, col_idx]
        v_nb = lax.dynamic_slice_in_dim(vg, r0, kh, axis=1)[:, :, col_idx]
        row_off = r0 + jnp.arange(kh) - r + NA_WIN_H - 1
        bias = jnp.transpose(jnp.take(col_bias, row_off, axis=1), (0, 2, 1, 3))
        s_nb = jnp.einsum('bqhd,baqwhd->bhqaw', q_r, k_nb).astype(F32) + bias[None].astype(F32)
        s_cx = jnp.einsum('bqhd,bchd->bhqc', q_r, k_ctx).astype(F32)
        p = jax.nn.softmax(jnp.concatenate([s_nb.reshape(B, H, GRID_W, kh * kw), s_cx], axis=-1), axis=-1)
        p = p.astype(v.dtype)
        p_nb = p[..., :kh * kw].reshape(B, H, GRID_W, kh, kw)
        return (jnp.einsum('bhqaw,baqwhd->bqhd', p_nb, v_nb)
                + jnp.einsum('bhqc,bchd->bqhd', p[..., kh * kw:], v_ctx))

    out = lax.map(one_row, jnp.arange(rows))
    return jnp.moveaxis(out, 0, 1).reshape(B, T, H, d)

def _context_attention(q, k, v):
    s = jnp.einsum('bqhd,bkhd->bhqk', q, k).astype(F32) * (q.shape[-1] ** -0.5)
    p = jax.nn.softmax(s, axis=-1).astype(v.dtype)
    return jnp.einsum('bhqk,bkhd->bqhd', p, v)

def _ab_mixer(h_lat, h_ctx, w_in, b_gate, q_norm, k_norm, rpb, h_norm, w_out, need_ctx):
    def project(h, rotary):
        qa, ka, va, za, qb, kb, vb, ob, zb, g = _split_cols(h @ w_in, AB_SIZES)
        qa = _rms(_heads(qa, NA_HEADS), q_norm)
        ka = _rms(_heads(ka, NA_HEADS), k_norm)
        qb, kb = _heads(qb, ML_HEADS), _heads(kb, ML_HEADS) * (ML_DIM ** -0.5)
        if rotary:
            qb, kb = _axial_rope(qb), _axial_rope(kb)
        gates = jnp.transpose(_heads(g + b_gate, 4), (0, 3, 1, 2)).astype(F32)
        mb = (_bht(qb), _bht(kb), _bht(_heads(vb, ML_HEADS)), gates)
        return (qa, ka, _heads(va, NA_HEADS), za), mb, (ob, zb)

    (qa_l, ka_l, va_l, za_l), mb_l, (ob_l, zb_l) = project(h_lat, True)
    (qa_c, ka_c, va_c, za_c), mb_c, (ob_c, zb_c) = project(h_ctx, False)
    oa_l = _neighbourhood_attention(qa_l, ka_l, va_l, ka_c, va_c, rpb)
    hb_l, hb_c = _mlstm_bidir(mb_l, mb_c, need_ctx)

    def merge(oa, hb, za, ob, zb):
        hb = jnp.swapaxes(hb, 1, 2).astype(ob.dtype) * jax.nn.sigmoid(_heads(ob, ML_HEADS))
        hb = _rms(hb, h_norm.reshape(ML_HEADS, ML_DIM))
        ya = oa.reshape(oa.shape[:2] + (NA_WIDTH,)) * jax.nn.silu(za)
        yb = hb.reshape(hb.shape[:2] + (ML_WIDTH,)) * jax.nn.silu(zb)
        return jnp.concatenate([ya, yb], axis=-1) @ w_out

    y_lat = merge(oa_l, hb_l, za_l, ob_l, zb_l)
    y_ctx = merge(_context_attention(qa_c, ka_c, va_c), hb_c, za_c, ob_c, zb_c) if need_ctx else None
    return y_lat, y_ctx

def _c_mixer(h_lat, h_ctx, w_in, lb, h_norm, w_out, need_ctx):
    def project(h):
        q, f_fwd, f_bwd, i, z = _split_cols(h @ w_in, C_SIZES)

        def decay(f_pre):
            f = lb + (1.0 - lb) * jax.nn.sigmoid(f_pre.astype(F32))
            return _bht(_heads(1.0 - f, HG_HEADS)), _bht(_heads(jnp.log(f), HG_HEADS))

        rec = (_bht(_heads(jax.nn.silu(q), HG_HEADS)), _bht(_heads(i, HG_HEADS)), (decay(f_fwd), decay(f_bwd)))
        return rec, z

    rec_l, z_l = project(h_lat)
    rec_c, z_c = project(h_ctx)
    o_l, o_c = _gla_bidir(rec_l, rec_c, need_ctx)

    def merge(o, z):
        o = _rms(jnp.swapaxes(o, 1, 2).astype(z.dtype), h_norm.reshape(HG_HEADS, HG_VDIM))
        return (o.reshape(o.shape[:2] + (HG_VW,)) * jax.nn.silu(z)) @ w_out

    return merge(o_l, z_l), (merge(o_c, z_c) if need_ctx else None)

def _lower_bound(lb_param, layer):
    s = jax.nn.softmax(lb_param.astype(F32), axis=0)
    return (jnp.cumsum(s, axis=0) - s[0])[layer]

def first_inputs(seed: int = 0) -> dict:
    key = jax.random.key(seed)
    ks = jax.random.split(key, 22)

    def nrm(k, shape, s):
        return jax.random.normal(k, shape, F32) * s

    f_bias = jnp.linspace(3.0, 6.0, ML_HEADS, dtype=F32)
    b_gate_ab = jnp.concatenate([nrm(ks[8], (N_AB, ML_HEADS), 0.1),
                                 f_bias + nrm(ks[9], (N_AB, ML_HEADS), 0.1),
                                 nrm(ks[10], (N_AB, ML_HEADS), 0.1),
                                 f_bias + nrm(ks[11], (N_AB, ML_HEADS), 0.1)], axis=-1)
    return {
        "x": nrm(ks[0], (BATCH, SEQ, D_MODEL), 1.0),
        "c": nrm(ks[1], (BATCH, D_MODEL), 1.0),
        "ctx": nrm(ks[2], (BATCH, CTX_LEN, D_MODEL), 1.0),
        "c_ctx": nrm(ks[3], (D_MODEL,), 1.0),
        "norm_w": 1.0 + nrm(ks[4], (DEPTH, D_MODEL), 0.05),
        "w_ada": nrm(ks[5], (DEPTH, D_MODEL, 3 * D_MODEL), 0.5 * D_MODEL ** -0.5),
        "b_ada": nrm(ks[6], (DEPTH, 3 * D_MODEL), 0.02),
        "w_in_ab": nrm(ks[7], (N_AB, D_MODEL, AB_IN), D_MODEL ** -0.5),
        "b_gate_ab": b_gate_ab,
        "q_norm_a": 1.0 + nrm(ks[12], (N_AB, NA_DIM), 0.05),
        "k_norm_a": 1.0 + nrm(ks[13], (N_AB, NA_DIM), 0.05),
        "rpb_a": nrm(ks[14], (N_AB, NA_HEADS, 2 * NA_WIN_H - 1, 2 * NA_WIN_W - 1), 0.1),
        "h_norm_b": 1.0 + nrm(ks[15], (N_AB, ML_WIDTH), 0.05),
        "w_out_ab": nrm(ks[16], (N_AB, INNER, D_MODEL), INNER ** -0.5),
        "w_in_c": nrm(ks[17], (N_C, D_MODEL, C_IN), D_MODEL ** -0.5),
        "lb_c": nrm(ks[18], (DEPTH, HG_KW), 0.5),
        "h_norm_c": 1.0 + nrm(ks[19], (N_C, HG_VW), 0.05),
        "w_out_c": nrm(ks[20], (N_C, INNER, D_MODEL), INNER ** -0.5),
    }

def first_block(x, c, ctx, c_ctx, norm_w, w_ada, b_ada, w_in_ab, b_gate_ab, q_norm_a, k_norm_a, rpb_a,
              h_norm_b, w_out_ab, w_in_c, lb_c, h_norm_c, w_out_c):
    for l in range(DEPTH):
        need_ctx = l < DEPTH - 1
        shift, scale, gate = _ada(c, w_ada[l], b_ada[l])
        shift_c, scale_c, gate_c = _ada(c_ctx, w_ada[l], b_ada[l])
        h_lat = _rms(x, norm_w[l]) * (1.0 + scale) + shift
        h_ctx = _rms(ctx, norm_w[l]) * (1.0 + scale_c) + shift_c
        j = l // 2
        if l % 2 == 0:
            y_lat, y_ctx = _ab_mixer(h_lat, h_ctx, w_in_ab[j], b_gate_ab[j], q_norm_a[j], k_norm_a[j],
                                     rpb_a[j], h_norm_b[j], w_out_ab[j], need_ctx)
        else:
            y_lat, y_ctx = _c_mixer(h_lat, h_ctx, w_in_c[j], _lower_bound(lb_c, l), h_norm_c[j],
                                    w_out_c[j], need_ctx)
        x = x + gate * y_lat
        if need_ctx:
            ctx = ctx + gate_c * y_ctx
    return x


DEPTH_2 = 1

CONV_WIDTH = 512
CONV_K = 3
N_HEADS = 8
HEAD_DIM = 64
ATTN_WIDTH = N_HEADS * HEAD_DIM
Q_BLOCK = 128
N_GROUPS = 4
EXPERTS_PER_GROUP = 8
N_EXPERTS = N_GROUPS * EXPERTS_PER_GROUP
TOP_K_IN_GROUP = 2
D_EXPERT = 256
IN_COLS = 3 * CONV_WIDTH + 3 * ATTN_WIDTH + N_HEADS + 2 * D_MODEL


def rmsnorm(x, w):
    xf = x.astype(jnp.float32)
    y = xf * lax.rsqrt(jnp.mean(xf * xf, axis=-1, keepdims=True) + EPS)
    return (y * w.astype(jnp.float32)).astype(x.dtype)

def modulate(x, norm_w, shift, scale):
    return rmsnorm(x, norm_w) * (1 + scale[:, None, :]) + shift[:, None, :]

def causal_depthwise_conv(u, w):
    S = u.shape[1]
    up = jnp.pad(u, ((0, 0), (CONV_K - 1, 0), (0, 0)))
    out = w[0] * up[:, 0:S]
    for j in range(1, CONV_K):
        out = out + w[j] * up[:, j:j + S]
    return out

def forgetting_attention(q, k, v, log_f):
    B, H, S, Dh = q.shape
    nblk = S // Q_BLOCK
    F = jnp.cumsum(log_f, axis=-1)
    scale = HEAD_DIM ** -0.5
    k_pos = jnp.arange(S)
    q_blocks = q.reshape(B, H, nblk, Q_BLOCK, Dh).transpose(2, 0, 1, 3, 4)
    F_blocks = F.reshape(B, H, nblk, Q_BLOCK).transpose(2, 0, 1, 3)

    def one_block(args):
        i, q_i, F_i = args
        s = jnp.einsum('bhqd,bhkd->bhqk', q_i, k,
                       preferred_element_type=jnp.float32) * scale
        s = s + (F_i[..., :, None] - F[..., None, :])
        q_pos = i * Q_BLOCK + jnp.arange(Q_BLOCK)
        s = jnp.where(k_pos[None, :] <= q_pos[:, None], s, -jnp.inf)
        p = jax.nn.softmax(s, axis=-1)
        return jnp.einsum('bhqk,bhkd->bhqd', p.astype(v.dtype), v)

    o = lax.map(one_block, (jnp.arange(nblk), q_blocks, F_blocks))
    return o.transpose(1, 0, 3, 2, 4).reshape(B, S, H * Dh)

def hierarchical_moe(h, w_rg, b_rg, w_re, b_re, w_gate, w_up, w_down):
    B, S, _ = h.shape
    lg = (h @ w_rg).astype(jnp.float32) + b_rg.astype(jnp.float32)
    p_g = jax.nn.softmax(lg, axis=-1)
    g_idx = jnp.argmax(lg, axis=-1)
    p_sel = jnp.take_along_axis(p_g, g_idx[..., None], axis=-1)
    le = ((h @ w_re).astype(jnp.float32) + b_re.astype(jnp.float32)
          ).reshape(B, S, N_GROUPS, EXPERTS_PER_GROUP)
    le_g = jnp.take_along_axis(le, g_idx[..., None, None], axis=2)[:, :, 0]
    top_v, top_i = lax.top_k(le_g, TOP_K_IN_GROUP)
    w_k = jax.nn.softmax(top_v, axis=-1) * p_sel
    e_idx = g_idx[..., None] * EXPERTS_PER_GROUP + top_i
    comb = jnp.sum(jax.nn.one_hot(e_idx, N_EXPERTS, dtype=jnp.float32)
                   * w_k[..., None], axis=-2).astype(h.dtype)
    out = jnp.zeros_like(h)
    for e in range(N_EXPERTS):
        a = jax.nn.silu(h @ w_gate[e]) * (h @ w_up[e])
        out = out + comb[..., e:e + 1] * (a @ w_down[e])
    return out

def hybrid_layer(x, c, w_ada, b_ada, norm1_w, w_in, b_forget, conv_w,
                 q_norm_w, k_norm_w, w_out_conv, w_out_attn, w_o, norm2_w,
                 w_router_group, b_router_group, w_router_expert, b_router_expert,
                 w_gate, w_up, w_down):
    B, S, _ = x.shape
    mod = jax.nn.silu(c) @ w_ada + b_ada
    shift1, scale1, gate1, shift2, scale2, gate2 = jnp.split(mod, 6, axis=-1)

    h = modulate(x, norm1_w, shift1, scale1)
    proj = h @ w_in
    sizes = [CONV_WIDTH, CONV_WIDTH, CONV_WIDTH, ATTN_WIDTH, ATTN_WIDTH,
             ATTN_WIDTH, N_HEADS, D_MODEL]
    cuts = [int(v) for v in np.cumsum(sizes)]
    x_in, conv_b, conv_c, q, k, v, f_logit, gate_conv_l, gate_attn_l = jnp.split(
        proj, cuts, axis=-1)

    y_a = conv_b * causal_depthwise_conv(conv_c * x_in, conv_w)
    p_a = y_a @ w_out_conv

    q = rmsnorm(q.reshape(B, S, N_HEADS, HEAD_DIM), q_norm_w).transpose(0, 2, 1, 3)
    k = rmsnorm(k.reshape(B, S, N_HEADS, HEAD_DIM), k_norm_w).transpose(0, 2, 1, 3)
    v = v.reshape(B, S, N_HEADS, HEAD_DIM).transpose(0, 2, 1, 3)
    log_f = jax.nn.log_sigmoid((f_logit + b_forget).astype(jnp.float32)).transpose(0, 2, 1)
    y_b = forgetting_attention(q, k, v, log_f)
    p_b = y_b @ w_out_attn

    merged = jax.nn.sigmoid(gate_conv_l) * p_a + jax.nn.sigmoid(gate_attn_l) * p_b
    x = x + gate1[:, None, :] * (merged @ w_o)

    h2 = modulate(x, norm2_w, shift2, scale2)
    moe = hierarchical_moe(h2, w_router_group, b_router_group, w_router_expert,
                           b_router_expert, w_gate, w_up, w_down)
    return x + gate2[:, None, :] * moe

def second_inputs(seed: int = 0) -> dict:
    key = jax.random.key(seed)
    ks = jax.random.split(key, 22)
    f32 = jnp.float32
    L = DEPTH_2

    def nrm(k, shape, scale):
        return jax.random.normal(k, shape, f32) * scale

    return {
        "x": nrm(ks[0], (BATCH, SEQ, D_MODEL), 1.0),
        "c": nrm(ks[1], (BATCH, D_MODEL), 1.0),
        "w_ada": nrm(ks[2], (L, D_MODEL, 6 * D_MODEL), 0.5 * D_MODEL ** -0.5),
        "b_ada": nrm(ks[3], (L, 6 * D_MODEL), 0.02),
        "norm1_w": 1.0 + nrm(ks[4], (L, D_MODEL), 0.02),
        "w_in": nrm(ks[5], (L, D_MODEL, IN_COLS), D_MODEL ** -0.5),
        "b_forget": 4.0 + nrm(ks[6], (L, N_HEADS), 0.5),
        "conv_w": nrm(ks[7], (L, CONV_K, CONV_WIDTH), CONV_K ** -0.5),
        "q_norm_w": 1.0 + nrm(ks[8], (L, HEAD_DIM), 0.02),
        "k_norm_w": 1.0 + nrm(ks[9], (L, HEAD_DIM), 0.02),
        "w_out_conv": nrm(ks[10], (L, CONV_WIDTH, D_MODEL), CONV_WIDTH ** -0.5),
        "w_out_attn": nrm(ks[11], (L, ATTN_WIDTH, D_MODEL), ATTN_WIDTH ** -0.5),
        "w_o": nrm(ks[12], (L, D_MODEL, D_MODEL), D_MODEL ** -0.5),
        "norm2_w": 1.0 + nrm(ks[13], (L, D_MODEL), 0.02),
        "w_router_group": nrm(ks[14], (L, D_MODEL, N_GROUPS), D_MODEL ** -0.5),
        "b_router_group": nrm(ks[15], (L, N_GROUPS), 0.01),
        "w_router_expert": nrm(ks[16], (L, D_MODEL, N_EXPERTS), D_MODEL ** -0.5),
        "b_router_expert": nrm(ks[17], (L, N_EXPERTS), 0.01),
        "w_gate": nrm(ks[18], (L, N_EXPERTS, D_MODEL, D_EXPERT), D_MODEL ** -0.5),
        "w_up": nrm(ks[19], (L, N_EXPERTS, D_MODEL, D_EXPERT), D_MODEL ** -0.5),
        "w_down": nrm(ks[20], (L, N_EXPERTS, D_EXPERT, D_MODEL), D_EXPERT ** -0.5),
    }

def second_block(x, c, w_ada, b_ada, norm1_w, w_in, b_forget, conv_w, q_norm_w,
              k_norm_w, w_out_conv, w_out_attn, w_o, norm2_w, w_router_group,
              b_router_group, w_router_expert, b_router_expert, w_gate, w_up,
              w_down):
    for l in range(DEPTH_2):
        x = hybrid_layer(x, c, w_ada[l], b_ada[l], norm1_w[l], w_in[l], b_forget[l],
                         conv_w[l], q_norm_w[l], k_norm_w[l], w_out_conv[l],
                         w_out_attn[l], w_o[l], norm2_w[l], w_router_group[l],
                         b_router_group[l], w_router_expert[l], b_router_expert[l],
                         w_gate[l], w_up[l], w_down[l])
    return x


def setup_inputs(seed=0):
    out = dict(first_inputs(seed))
    for name, value in second_inputs(seed + 1).items():
        if name != "x":
            out[name + "_2"] = value
    return out


def reference(
    x, c, ctx, c_ctx, norm_w, w_ada, b_ada, w_in_ab, b_gate_ab, q_norm_a, k_norm_a, rpb_a,
    h_norm_b, w_out_ab, w_in_c, lb_c, h_norm_c, w_out_c, c_2, w_ada_2, b_ada_2, norm1_w_2,
    w_in_2, b_forget_2, conv_w_2, q_norm_w_2, k_norm_w_2, w_out_conv_2, w_out_attn_2, w_o_2,
    norm2_w_2, w_router_group_2, b_router_group_2, w_router_expert_2, b_router_expert_2,
    w_gate_2, w_up_2, w_down_2,
):
    x = first_block(
        x, c, ctx, c_ctx, norm_w, w_ada, b_ada, w_in_ab, b_gate_ab, q_norm_a, k_norm_a, rpb_a,
        h_norm_b, w_out_ab, w_in_c, lb_c, h_norm_c, w_out_c,
    )
    return second_block(
        x, c_2, w_ada_2, b_ada_2, norm1_w_2, w_in_2, b_forget_2, conv_w_2, q_norm_w_2,
        k_norm_w_2, w_out_conv_2, w_out_attn_2, w_o_2, norm2_w_2, w_router_group_2,
        b_router_group_2, w_router_expert_2, b_router_expert_2, w_gate_2, w_up_2, w_down_2,
    )


_drawn_inputs = setup_inputs


def setup_inputs(seed=0):
    import zlib

    import numpy as np

    out = dict(_drawn_inputs(seed))
    spreads = {}
    factors = {'q_norm_a': 8.0,
     'k_norm_a': 8.0,
     'rpb_a': 25.435,
     'h_norm_b': 6.044,
     'lb_c': 4.504,
     'h_norm_c': 4.923,
     'norm1_w_2': 5.942,
     'b_forget_2': 37.48,
     'q_norm_w_2': 64.0,
     'k_norm_w_2': 64.0,
     'norm2_w_2': 28.477,
     'b_router_group_2': 59.367,
     'b_router_expert_2': 64.0}
    for name, (base, spread) in spreads.items():
        noise = np.random.default_rng([zlib.crc32(name.encode()), seed]).standard_normal(out[name].shape)
        drawn = base * np.exp(spread * noise) if base else spread * noise
        out[name] = jnp.asarray(drawn.astype(out[name].dtype))
    for name, factor in factors.items():
        out[name] = (out[name] * factor).astype(out[name].dtype)
    return out
```

```python
from contextlib import ExitStack

import numpy as np

import concourse.bass as bass
from concourse import mybir

F32 = mybir.dt.float32
I32 = mybir.dt.int32
ALU = mybir.AluOpType
ACT = mybir.ActivationFunctionType
AX_X = mybir.AxisListType.X

P = 128
D = 1024
KD = D // P
SEQ, CTX = 512, 256
LT, CT = SEQ // P, CTX // P
NT = LT + CT
NTOK = SEQ + CTX
EPS = 1e-6
NEG = -1e30

GRID_W, GRID_H = 64, SEQ // 64
COLS = P // GRID_H
WIN_W = 16
NA_PAIRS = 8
NA_SCALE = 64 ** -0.5
RPB_H, RPB_W = 15, 31
RPB_PAD = 64
UK = 3 * COLS

ML_HEADS, ML_DIM = 4, 256
HG_HEADS = 16
HG_LEVELS = [1, 2, 4, 8, 16, 32, 64, 128, 256]
INNER = 2048
NE, DE = 32, 256

VECTORS = [("c", 8), ("c_ctx", 8), ("c_2", 8), ("norm_w", 16), ("norm1_w_2", 8), ("norm2_w_2", 8),
           ("h_norm_b", 8), ("h_norm_c", 16), ("lb_c", 32),
           ("conv_w_2", 12)]
ROW = {}
for _name, _n in VECTORS:
    ROW[_name] = sum(n for k, n in VECTORS if k in ROW)
    assert _n <= 32
NVEC = sum(n for _, n in VECTORS)
MOD_L0, MOD_L1, MOD_B2, NMOD = 0, 24, 48, 96


def rows128(ap):
    names = " ".join("abcd"[:len(ap.shape)])
    flat = ap.rearrange(f"{names} -> ({names})") if len(ap.shape) > 1 else ap
    return flat.rearrange("(n p) -> n p", p=P)


class Stage:

    def __init__(self, nc, name):
        self.nc, self.name, self.stack, self.sems = nc, name, ExitStack(), []

    def __enter__(self):
        self.stack.__enter__()
        return self

    def __exit__(self, *e):
        self.nc.clear_and_free_semaphores(self.sems)
        self.nc.all_engine_barrier()
        return self.stack.__exit__(*e)

    def sb(self, name, shape, dt=F32):
        return self.stack.enter_context(self.nc.sbuf_tensor(f"{self.name}_{name}", shape, dt))

    def ps(self, name, shape=(P, 512)):
        return self.stack.enter_context(self.nc.psum_tensor(f"{self.name}_{name}", list(shape), F32))

    def sem(self, name):
        self.sems.append(self.nc.alloc_semaphore(f"{self.name}_{name}"))
        return self.sems[-1]


def stage_setup(nc, a, k):
    with Stage(nc, "setup") as s:
        vrows, brows = s.sb("vrows", [P, P]), s.sb("brows", [P, P])
        vps, bps = s.ps("vps"), s.ps("bps")
        e, u = s.sb("e", [P, 24]), s.sb("u", [P, 24])
        lb_t = s.sb("lb_t", [P, 3, 16])
        rpb_rows = s.sb("rpb_rows", [16, RPB_H, RPB_PAD])
        small_in, x_in, const_in, rpb_in = s.sem("small_in"), s.sem("x_in"), s.sem("const_in"), s.sem("rpb_in")
        zeroed, turned, cols_ready, exp_ready, padded = (
            s.sem(n) for n in ("zeroed", "turned", "cols_ready", "exp_ready", "padded"))
        lbx_ready, lbe_ready = s.sem("lbx_ready"), s.sem("lbe_ready")
        with nc.Block() as block:
            @block.sync
            def _(sp):
                for name, n in VECTORS:
                    sp.dma_start(vrows[ROW[name]:ROW[name] + n, :], rows128(a[name])).then_inc(small_in, 16)
                sp.dma_start(brows[0:48, :], rows128(a["b_ada"])).then_inc(small_in, 16)
                sp.dma_start(brows[48:96, :], rows128(a["b_ada_2"])).then_inc(small_in, 16)
                sp.dma_start(k["ident"][:, :], a["ident"]).then_inc(const_in, 16)
                sp.wait_ge(zeroed, 1)
                sp.dma_start(rpb_rows[:, :, 16:16 + RPB_W], a["rpb_a"][0]).then_inc(rpb_in, 16)
                sp.dma_start(k["xs"][:, 0:LT, :], a["x"][0].rearrange("(t p) d -> p t d", p=P)).then_inc(x_in, 16)
                sp.dma_start(k["xs"][:, LT:NT, :], a["ctx"][0].rearrange("(t p) d -> p t d", p=P)).then_inc(x_in, 16)
                sp.wait_ge(rpb_in, 16)
                sp.dma_start(k["rpb_pad"], rpb_rows[:, :, :]).then_inc(padded, 16)
                sp.wait_ge(padded, 16)
                sp.wait_ge(x_in, 32)

            @block.gpsimd
            def _(pool):
                pool.memset(rpb_rows[:, :, :], 0.0).then_inc(zeroed, 1)

            @block.tensor
            def _(pe):
                pe.wait_ge(const_in, 16)
                pe.wait_ge(small_in, 16 * (len(VECTORS) + 2))
                pe.transpose(vps[:, 0:NVEC], vrows[0:NVEC, :], k["ident"][0:NVEC, 0:NVEC]).then_inc(turned, 1)
                pe.transpose(bps[:, 0:NMOD], brows[0:NMOD, :], k["ident"][0:NMOD, 0:NMOD]).then_inc(turned, 1)

            @block.vector
            def _(dve):
                dve.wait_ge(turned, 2)
                dve.tensor_copy(k["vecT"][:, :], vps[:, 0:NVEC]).then_inc(cols_ready, 1)
                dve.tensor_copy(k["biasT"][:, :], bps[:, 0:NMOD])
                dve.wait_ge(exp_ready, 1)
                dve.tensor_scalar(u[:, :], e[:, :], 1.0, None, ALU.add)
                lb = k["vecT"][:, ROW["lb_c"]:ROW["lb_c"] + 32]
                dve.tensor_tensor(lb_t[:, 2, :], lb[:, 0:16], lb[:, 16:32], ALU.max)
                dve.drain()
                dve.tensor_tensor(lb_t[:, 0, :], lb[:, 0:16], lb_t[:, 2, :], ALU.subtract)
                dve.tensor_tensor(lb_t[:, 1, :], lb[:, 16:32], lb_t[:, 2, :], ALU.subtract)
                dve.reciprocal(e[:, :], u[:, :])
                dve.drain().then_inc(lbx_ready, 1)
                dve.tensor_tensor(k["silu_c"][:, :, :], k["vecT"][:, 0:24].rearrange("p (v k) -> p k v", v=3),
                                  e[:, :].rearrange("p (v k) -> p k v", v=3), ALU.mult)
                dve.wait_ge(lbe_ready, 1)
                dve.tensor_tensor(lb_t[:, 2, :], lb_t[:, 0, :], lb_t[:, 1, :], ALU.add)
                dve.drain()
                dve.reciprocal(lb_t[:, 0, :], lb_t[:, 2, :])
                dve.drain()
                dve.tensor_tensor(k["lbT"][:, 0, :], lb_t[:, 1, :], lb_t[:, 0, :], ALU.mult)
                dve.drain()
                dve.tensor_scalar(k["lbT"][:, 1, :], k["lbT"][:, 0, :], -1.0, 1.0, ALU.mult, ALU.add)

            @block.scalar
            def _(act):
                act.preload_act_table_set("natural_log_exp_and_others")
                act.wait_ge(cols_ready, 1)
                act.activation(e[:, :], k["vecT"][:, 0:24], ACT.Exp, scale=-1.0).then_inc(exp_ready, 1)
                act.wait_ge(lbx_ready, 1)
                act.activation(lb_t[:, 0:2, :], lb_t[:, 0:2, :], ACT.Exp).then_inc(lbe_ready, 1)


def stage_modulations(nc, a, k):
    NCH = 512
    with Stage(nc, "ada") as s:
        w = [s.sb(f"w{u}", [P, KD, NCH]) for u in range(2)]
        row = [s.sb(f"row{u}", [3, NCH]) for u in range(2)]
        ps, cols = [s.ps(f"ps{u}") for u in range(2)], [s.ps(f"cols{u}") for u in range(2)]
        w_in = [s.sem(f"w_in{u}") for u in range(2)]
        products_ready, rows_ready, turned = s.sem("products_ready"), s.sem("rows_ready"), s.sem("turned")
        stored = s.sem("stored")
        parts = [(a["w_ada"][0], 0, 3), (a["w_ada"][1], 6, 3), (a["w_ada_2"][0], 12, 6)]
        with nc.Block() as block:
            @block.sync
            def _(sp):
                srcs = [wd.rearrange("(k p) n -> p k n", p=P) for wd, _, _ in parts]
                for n, (src, (_, c0, pairs)) in enumerate(zip(srcs, parts)):
                    if n == 0:
                        for u in range(2):
                            sp.dma_start(w[u][:, :, :], src[:, :, u * NCH:(u + 1) * NCH]).then_inc(w_in[u], 16)
                    with sp.Fori(0, pairs - 1) as i:
                        for u in range(2):
                            sp.wait_ge(products_ready, i * 2 + (c0 + u + 1))
                            sp.dma_start(w[u][:, :, :], src[:, :, bass.ds(i * (2 * NCH) + (u + 2) * NCH, NCH)])\
                                .then_inc(w_in[u], 16)
                    if n + 1 < len(parts):
                        for u in range(2):
                            sp.wait_ge(products_ready, c0 + 2 * pairs - 1 + u)
                            sp.dma_start(w[u][:, :, :], srcs[n + 1][:, :, u * NCH:(u + 1) * NCH]).then_inc(w_in[u], 16)

            @block.tensor
            def _(pe):
                def turn(u, i, c):
                    pe.wait_ge(rows_ready, i * 2 + (c + 1))
                    pe.wait_ge(stored, i * 2 + (c + 1))
                    pe.sem_inc(k["apart"], 1)
                    for b in range(NCH // P):
                        tr = pe.transpose(cols[u][:, 3 * b:3 * b + 3], row[u][:, b * P:(b + 1) * P],
                                          k["ident"][0:3, 0:3])
                    tr.then_inc(turned, 1)

                for wd, c0, pairs in parts:
                    with pe.Fori(0, pairs) as i:
                        for u in range(2):
                            pe.wait_ge(w_in[u], i * 16 + (c0 // 2 + 1) * 16)
                            for kk in range(KD):
                                mm = pe.matmul(ps[u][0:3, :], k["silu_c"][:, kk, :], w[u][:, kk, :],
                                               start=kk == 0, stop=kk == KD - 1)
                            mm.then_inc(products_ready, 1)
                            if u == 1:
                                turn(0, i, c0)
                        turn(1, i, c0 + 1)

            @block.scalar
            def _(act):
                for wd, c0, pairs in parts:
                    with act.Fori(0, pairs) as i:
                        for u in range(2):
                            act.wait_ge(products_ready, i * 2 + (c0 + u + 1))
                            act.activation(row[u][:, :], ps[u][0:3, :], ACT.Copy).then_inc(rows_ready, 1)

            @block.vector
            def _(dve):
                dve.drain().then_inc(stored, 1)
                dve.drain().then_inc(stored, 1)
                for wd, c0, pairs in parts:
                    with dve.Fori(0, pairs) as i:
                        for u in range(2):
                            dve.wait_ge(turned, i * 2 + (c0 + u + 1))
                            col = bass.ds(i * 8 + (4 * (c0 + u)), 4)
                            dve.tensor_tensor(k["modT"][:, col, :], cols[u][:, 0:12].rearrange("p (b v) -> p b v", v=3),
                                              k["biasT"][:, col].unsqueeze(2).to_broadcast([P, 4, 3]), ALU.add)\
                                .then_inc(stored, 1)


def stage_norm(nc, k, name, groups, xs, hT):
    with Stage(nc, name) as s:
        sq = [s.sb(f"sq{u}", [P, D]) for u in range(2)]
        xn = [s.sb(f"xn{u}", [P, D]) for u in range(2)]
        ss, ms, rstd = s.sb("ss", [P, 2]), s.sb("ms", [P, 2]), s.sb("rstd", [P, 2])
        gain = s.sb("gain", [P, len(groups), KD])
        half = s.sb("half", [P, 1])
        ps = [[s.ps(f"ps{u}{h}") for h in range(2)] for u in range(2)]
        sums_ready, rstd_ready, xn_ready, turned, stored = (
            s.sem(n) for n in ("sums_ready", "rstd_ready", "xn_ready", "turned", "stored"))
        mean_ready = s.sem("mean_ready")
        gain_ready = s.sem("gain_ready")
        KH = KD // 2
        with nc.Block() as block:
            @block.vector
            def _(dve):
                for g, (_, _, nw, mod, v) in enumerate(groups):
                    dve.tensor_scalar(gain[:, g, :], k["modT"][:, mod + 8:mod + 16, v], 1.0, None, ALU.add)
                dve.drain()
                for g, (_, _, nw, mod, v) in enumerate(groups):
                    dve.tensor_tensor(gain[:, g, :], gain[:, g, :], k["vecT"][:, nw:nw + 8], ALU.mult)
                dve.drain().then_inc(gain_ready, 1)
                for g, (t0, n, nw, mod, v) in enumerate(groups):
                    with dve.Fori(0, n // 2) as i:
                        for u in range(2):
                            dve.wait_ge(sums_ready, i * 2 + (t0 + u + 1))
                            dve.tensor_scalar(ms[:, u:u + 1], ss[:, u:u + 1], 1.0 / D, EPS, ALU.mult, ALU.add)\
                                .then_inc(mean_ready, 1)
                        for u in range(2):
                            dve.wait_ge(turned, i * 2 + (t0 + u + 1))
                            for b in range(KH):
                                ev = dve.tensor_scalar(hT[:, b, bass.ds(i * 256 + (t0 + u) * P, P)], ps[u][0][:, b * P:(b + 1) * P],
                                                       gain[:, g, b:b + 1], k["modT"][:, mod + b:mod + b + 1, v],
                                                       ALU.mult, ALU.add)
                            ev.then_inc(stored, 1)

            @block.gpsimd
            def _(pool):
                pool.memset(half[:, :], -0.5)
                pool.drain()
                for g, (t0, n, nw, mod, v) in enumerate(groups):
                    with pool.Fori(0, n // 2) as i:
                        for u in range(2):
                            pool.wait_ge(mean_ready, i * 2 + (t0 + u + 1))
                            pool.tensor_tensor(rstd[:, u:u + 1], ms[:, u:u + 1], half[:, :], ALU.pow)\
                                .then_inc(rstd_ready, 1)

            @block.scalar
            def _(act):
                act.wait_ge(gain_ready, 1)
                for g, (t0, n, nw, mod, v) in enumerate(groups):
                    with act.Fori(0, n // 2) as i:
                        for u in range(2):
                            act.activation(sq[u][:, :], xs[:, bass.ds(i * 2 + (t0 + u), 1), :].squeeze(1), ACT.Square,
                                           accum_out=ss[:, u:u + 1]).then_inc(sums_ready, 1)
                        for u in range(2):
                            act.wait_ge(rstd_ready, i * 2 + (t0 + u + 1))
                            act.sem_inc(k["apart"], 1)
                            act.activation(xn[u][:, :], xs[:, bass.ds(i * 2 + (t0 + u), 1), :].squeeze(1), ACT.Copy,
                                           scale=rstd[:, u:u + 1]).then_inc(xn_ready, 1)
                        for u in range(2):
                            act.wait_ge(turned, i * 2 + (t0 + u + 1))
                            act.sem_inc(k["apart"], 1)
                            for b in range(KH):
                                act.activation(hT[:, KH + b, bass.ds(i * 256 + (t0 + u) * P, P)],
                                               ps[u][1][:, b * P:(b + 1) * P], ACT.Identity,
                                               scale=gain[:, g, KH + b:KH + b + 1],
                                               bias=k["modT"][:, mod + KH + b:mod + KH + b + 1, v])

            @block.tensor
            def _(pe):
                for g, (t0, n, nw, mod, v) in enumerate(groups):
                    with pe.Fori(0, n // 2) as i:
                        for u in range(2):
                            pe.wait_ge(xn_ready, i * 2 + (t0 + u + 1))
                            for b in range(KD):
                                tr = pe.transpose(ps[u][b // KH][:, (b % KH) * P:(b % KH + 1) * P],
                                                  xn[u][:, b * P:(b + 1) * P], k["ident"][:, :])
                            tr.then_inc(turned, 1)


def stage_attention_a(nc, a, k, yT):
    HD, W4 = 64, 512
    KINDS = {0: (0, (1, 2)), 1: (256, (0, 1, 2)), 2: (256, (0, 1, 2)), 3: (640, (0, 1))}
    units = [(t, h) for t in range(NT) for h in range(2)]
    NU = len(units)

    def key_tiles(t):
        near = list(range(max(0, t - 1), min(LT, t + 2))) if t < LT else []
        return near, near + list(range(LT, NT))

    with Stage(nc, "na") as s:
        w = s.sb("w", [P, KD, 4, P])
        h_cols = s.sb("h_cols", [P, KD, SEQ])
        squares, qkn = s.sb("squares", [P, 4, HD]), [s.sb(f"qkn{u}", [P, 4, HD]) for u in range(2)]
        ss, ms, rstd, half = (s.sb(n, [P, 4]) for n in ("ss", "ms", "rstd", "half"))
        qw, kw = s.sb("qw", [P, 1]), s.sb("kw", [P, 1])
        qT, kT = s.sb("qT", [P, NTOK]), s.sb("kT", [P, NTOK])
        v, zs = s.sb("v", [P, NT, P]), s.sb("zs", [P, NT, P])
        ez, uz, rz = s.sb("ez", [P, P]), s.sb("uz", [P, P]), s.sb("rz", [P, P])
        flip, mask = s.sb("flip", [P, P]), s.sb("mask", [P, 896])
        u_rev, bias = s.sb("u_rev", [P, 2, GRID_H, UK]), s.sb("bias", [P, 2, 896])
        sc, p = s.sb("sc", [P, UK * GRID_H]), [s.sb(f"p{u}", [P, 640]) for u in range(2)]
        pT = [s.sb(f"pT{u}", [P, 640]) for u in range(2)]
        m1, m2, nm = (s.sb(n, [P, NU]) for n in ("m1", "m2", "nm"))
        sums, total, rinv = s.sb("sums", [P, 2, NU]), s.sb("total", [P, NU]), s.sb("rinv", [P, NU])
        minus = s.sb("minus", [P, 1])
        y = s.sb("y", [P, 2, P])
        banks = [s.ps(f"bank{n}") for n in range(8)]
        proj, qk_ps, near_ps, ctx_ps, pT_ps = banks[0:2], banks[2:4], banks[4], banks[5], banks[6:8]
        o_ps, yT_ps = banks[0:2], banks[2:4]

        regrouped = s.sem("regrouped")
        w_in, u_in, const_in = s.sem("w_in"), s.sem("u_in"), s.sem("const_in")
        (proj_ready, squares_ready, means_ready, rstd_ready, qk_normed, qk_turned, qk_stored, consts_ready,
         u_flipped, bias_ready, scores_ready, max_ready, exp_ready, pT_ready, pT_stored_dve, pT_stored_act, pv_ready,
         y_ready, yT_ready) = (s.sem(n) for n in (
             "proj_ready", "squares_ready", "means_ready", "rstd_ready", "qk_normed", "qk_turned", "qk_stored",
             "consts_ready", "u_flipped", "bias_ready", "scores_ready", "max_ready", "exp_ready", "pT_ready",
             "pT_stored_dve", "pT_stored_act", "pv_ready", "y_ready", "yT_ready"))

        def bank_of(b, n):
            first = 3 if n > 3 else 1
            return (0, b * P) if b < first else (1, (b - first) * P)

        def regroup(eng, kk):
            src = k["hT"][:, kk, 0:SEQ].rearrange("p (r t c) -> p t r c", r=GRID_H, t=LT)
            for t in range(LT):
                dst = h_cols[:, kk, t * P:(t + 1) * P].rearrange("p (r c) -> p r c", r=GRID_H)
                if eng is nc.scalar:
                    ins = eng.activation(dst, src[:, t], ACT.Copy)
                else:
                    ins = eng.tensor_copy(dst, src[:, t])
            ins.then_inc(regrouped, 1)

        def token_tile(kk, j):
            if j < LT:
                return h_cols[:, kk, j * P:(j + 1) * P]
            return k["hT"][:, kk, j * P:(j + 1) * P]

        def turn_y(pe, i, t):
            pe.wait_ge(y_ready, i * NU + (2 * t + 2))
            pe.transpose(yT_ps[t % 2][:, 0:P], y[:, t % 2, :], k["ident"][:, :]).then_inc(yT_ready, 1)

        def store_yT(act, i, t):
            dst = yT[:, bass.ds(i, 1), :].squeeze(1)
            if t < LT:
                dst = dst[:, 0:SEQ].rearrange("p (r c) -> p r c", c=GRID_W)[:, :, COLS * t:COLS * (t + 1)]
                act.activation(dst, yT_ps[t % 2][:, 0:P].rearrange("p (r c) -> p r c", c=COLS), ACT.Copy)
            else:
                act.activation(dst[:, t * P:(t + 1) * P], yT_ps[t % 2][:, 0:P], ACT.Copy)

        with nc.Block() as block:
            @block.sync
            def _(sp):
                for dst, src in ((qw, "q_norm_a"), (kw, "k_norm_a")):
                    for h in range(2):
                        sp.dma_start(dst[h * HD:(h + 1) * HD, :], a[src].rearrange("a d -> d a")).then_inc(const_in, 16)
                sp.dma_start(flip[:, :], a["flip"]).then_inc(const_in, 16)
                sp.dma_start(mask[:, :], a["na_mask"]).then_inc(const_in, 16)
                src = a["w_in_ab"][0].rearrange("(k p) n -> p k n", p=P)

                def load(pair):
                    for seg in range(4):
                        sp.dma_start(w[:, :, seg, :], src[:, :, bass.ds(pair * P + seg * D, P)]).then_inc(w_in, 16)

                def load_bias(pair):
                    for h in range(2):
                        for r in range(GRID_H):
                            at = (pair * 2 + h) * (RPB_H * RPB_PAD) + r * RPB_PAD
                            sp.dma_start(u_rev[r * COLS:(r + 1) * COLS, h, :, :],
                                         bass.AP(k["rpb_pad"].tensor, at, [[1, COLS], [RPB_PAD, GRID_H], [1, UK]]))\
                                .then_inc(u_in, 16)

                load(0)
                load_bias(0)
                with sp.Fori(0, NA_PAIRS - 1) as i:
                    sp.wait_ge(proj_ready, i * NT + NT)
                    load(i + 1)
                    sp.wait_ge(u_flipped, i * 2 + 2)
                    load_bias(i + 1)

            @block.tensor
            def _(pe):
                pe.wait_ge(const_in, 16 * 6)
                pe.wait_ge(regrouped, KD)
                with pe.Fori(0, NA_PAIRS) as i:
                    def turn_qk(j):
                        pe.wait_ge(qk_normed, i * NT + (j + 1))
                        for b in range(2):
                            tr = pe.transpose(qk_ps[j % 2][:, b * P:(b + 1) * P],
                                              qkn[j % 2][:, 2 * b:2 * b + 2, :], k["ident"][:, :])
                        tr.then_inc(qk_turned, 1)

                    pe.wait_ge(w_in, i * 64 + 64)
                    for j in range(NT):
                        if j >= 2:
                            pe.wait_ge(qk_normed, i * NT + (j - 1))
                        for kk in range(KD):
                            mm = pe.matmul(proj[j % 2][:, :], token_tile(kk, j), w[:, kk, :, :],
                                           start=kk == 0, stop=kk == KD - 1)
                        mm.then_inc(proj_ready, 1)
                        if j >= 1:
                            if j >= 3:
                                pe.wait_ge(qk_stored, i * NT + (j - 2))
                            turn_qk(j - 1)
                    pe.wait_ge(qk_stored, i * NT + (NT - 2))
                    turn_qk(NT - 1)
                    pe.wait_ge(u_in, i * 256 + 256)
                    for h, ps in enumerate((near_ps, ctx_ps)):
                        pe.matmul(ps[:, 0:384], flip[:, :], u_rev[:, h, :, :], start=True, stop=True)\
                            .then_inc(u_flipped, 1)
                    pe.wait_ge(qk_stored, i * NT + NT)
                    pe.wait_ge(bias_ready, i + 1)
                    for n in range(NU + 3):
                        if n < NU:
                            t, h = units[n]
                            near, _ = key_tiles(t)
                            hs = slice(h * HD, (h + 1) * HD)
                            if n >= 1:
                                pe.wait_ge(exp_ready, i * NU + n)
                            if near:
                                pe.matmul(near_ps[:, 0:len(near) * P], qT[hs, t * P:(t + 1) * P],
                                          kT[hs, near[0] * P:(near[-1] + 1) * P], start=True, stop=True)
                            pe.matmul(ctx_ps[:, 0:CTX], qT[hs, t * P:(t + 1) * P], kT[hs, SEQ:NTOK],
                                      start=True, stop=True).then_inc(scores_ready, 1)
                        if n == NU:
                            pe.wait_ge(exp_ready, i * NU + n)
                        if n >= 2 and n - 2 < NU:
                            pe.wait_ge(pT_stored_dve, i * NU + (n - 1))
                            pe.wait_ge(pT_stored_act, i * NU + (n - 1))
                        if 1 <= n <= NU:
                            _, keys = key_tiles(units[n - 1][0])
                            for b in range(len(keys)):
                                bank, col = bank_of(b, len(keys))
                                tr = pe.transpose(pT_ps[bank][:, col:col + P],
                                    p[(n - 1) % 2][:, b * P:(b + 1) * P], k["ident"][:, :])
                            tr.then_inc(pT_ready, 1)
                        if n >= 2 and n - 2 < NU:
                            t, h = units[n - 2]
                            _, keys = key_tiles(t)
                            for b, kt in enumerate(keys):
                                mm = pe.matmul(o_ps[n % 2][:, 0:HD], pT[n % 2][:, b * P:(b + 1) * P],
                                               v[:, kt, h * HD:(h + 1) * HD], start=b == 0, stop=b == len(keys) - 1)
                            mm.then_inc(pv_ready, 1)
                        if n >= 4 and n % 2 == 0:
                            turn_y(pe, i, n // 2 - 2)

            @block.scalar
            def _(act):
                for kk in (0, 1, 2):
                    regroup(nc.scalar, kk)
                act.wait_ge(consts_ready, 1)
                with act.Fori(0, NA_PAIRS) as i:
                    def store_qk(j):
                        act.wait_ge(qk_turned, i * NT + (j + 1))
                        act.activation(qT[:, j * P:(j + 1) * P], qk_ps[j % 2][:, 0:P], ACT.Copy, scale=qw[:, 0:1])
                        act.activation(kT[:, j * P:(j + 1) * P], qk_ps[j % 2][:, P:2 * P], ACT.Copy, scale=kw[:, 0:1])\
                            .then_inc(qk_stored, 1)

                    for j in range(NT):
                        act.wait_ge(proj_ready, i * NT + (j + 1))
                        if j >= 1:
                            act.wait_ge(qk_normed, i * NT + j)
                        act.activation(v[:, j, :], proj[j % 2][:, 256:384], ACT.Copy)
                        act.activation(ez[:, :], proj[j % 2][:, 384:512], ACT.Exp, scale=-1.0)
                        act.activation(squares[:, :, :], proj[j % 2][:, 0:256].rearrange("p (h d) -> p h d", d=HD),
                                       ACT.Square).then_inc(squares_ready, 1)
                        if j >= 1:
                            store_qk(j - 1)
                    store_qk(NT - 1)
                    for n in range(NU + 3):
                        if n < NU:
                            t, h = units[n]
                            near, _ = key_tiles(t)
                            nw = len(near) * P
                            act.wait_ge(max_ready, i * NU + (n + 1))
                            if near:
                                act.activation(p[n % 2][:, 0:nw], sc[:, 0:nw], ACT.Exp, bias=nm[:, n:n + 1],
                                               accum_out=sums[:, 0, n:n + 1])
                            act.activation(p[n % 2][:, nw:nw + CTX], ctx_ps[:, 0:CTX], ACT.Exp, bias=nm[:, n:n + 1],
                                           accum_out=sums[:, 1, n:n + 1])
                            act.drain().then_inc(exp_ready, 1)
                        if 1 <= n <= NU:
                            _, keys = key_tiles(units[n - 1][0])
                            act.wait_ge(pT_ready, i * NU + n)
                            if len(keys) > 3:
                                st = act.activation(pT[(n - 1) % 2][:, 384:len(keys) * P],
                                                    pT_ps[1][:, 0:(len(keys) - 3) * P], ACT.Copy)
                            else:
                                st = act.activation(pT[(n - 1) % 2][:, P:2 * P], pT_ps[1][:, 0:P], ACT.Copy)
                            st.then_inc(pT_stored_act, 1)
                        if n >= 4 and n % 2 == 0:
                            t = n // 2 - 2
                            act.wait_ge(yT_ready, i * NT + (t + 1))
                            act.sem_inc(k["apart"], 1)
                            store_yT(act, i, t)

            @block.gpsimd
            def _(pool):
                pool.memset(half[:, :], -0.5)
                for kk in (3, 4):
                    regroup(nc.gpsimd, kk)
                pool.drain()
                with pool.Fori(0, NA_PAIRS) as i:
                    for j in range(NT):
                        pool.wait_ge(means_ready, i * NT + (j + 1))
                        pool.tensor_tensor(rstd[:, :], ms[:, :], half[:, :], ALU.pow).then_inc(rstd_ready, 1)

            @block.vector
            def _(dve):
                dve.memset(minus[:, :], -1.0)
                for kk in (5, 6, 7):
                    regroup(nc.vector, kk)
                dve.wait_ge(const_in, 16 * 6)
                dve.tensor_scalar(qw[:, :], qw[:, :], NA_SCALE, None, ALU.mult).then_inc(consts_ready, 1)
                with dve.Fori(0, NA_PAIRS) as i:
                    for j in range(NT):
                        qkvz = proj[j % 2]
                        dve.wait_ge(squares_ready, i * NT + (j + 1))
                        dve.tensor_reduce(ss[:, :], squares[:, :, :], AX_X, ALU.add)
                        dve.tensor_scalar(uz[:, :], ez[:, :], 1.0, None, ALU.add)
                        dve.drain()
                        dve.tensor_scalar(ms[:, :], ss[:, :], 1.0 / HD, EPS, ALU.mult, ALU.add).then_inc(means_ready, 1)
                        dve.reciprocal(rz[:, :], uz[:, :])
                        dve.drain()
                        dve.tensor_tensor(zs[:, j, :], qkvz[:, 384:512], rz[:, :], ALU.mult)
                        dve.wait_ge(rstd_ready, i * NT + (j + 1))
                        dve.tensor_tensor(qkn[j % 2][:, :, :], qkvz[:, 0:256].rearrange("p (h d) -> p h d", d=HD),
                                          rstd[:, :].unsqueeze(2).to_broadcast([P, 4, HD]), ALU.mult)\
                            .then_inc(qk_normed, 1)
                    dve.wait_ge(u_flipped, i * 2 + 2)
                    for h, ps in enumerate((near_ps, ctx_ps)):
                        u = ps[:, 0:384].rearrange("p (a t c) -> p t a c", a=GRID_H, t=3)
                        for t in (0, 1, 3):
                            off, tiles = KINDS[t]
                            shape = dict(t=len(tiles), a=GRID_H)
                            for x, dt in enumerate(tiles):
                                at = slice(off + x * P, off + (x + 1) * P)
                                ad = dve.tensor_tensor(
                                    bias[:, h, at].rearrange("p (a c) -> p a c", a=GRID_H), u[:, dt, :, :],
                                    mask[:, at].rearrange("p (a c) -> p a c", a=GRID_H), ALU.add)
                    ad.then_inc(bias_ready, 1)
                    dve.drain()
                    for n in range(NU + 2):
                        if n < NU:
                            t, h = units[n]
                            near, _ = key_tiles(t)
                            nw = len(near) * P
                            dve.wait_ge(scores_ready, i * NU + (n + 1))
                            dve.tensor_reduce(m2[:, n:n + 1], ctx_ps[:, 0:CTX], AX_X, ALU.max)
                            if near:
                                dve.tensor_tensor_reduce(sc[:, 0:nw], near_ps[:, 0:nw],
                                                         bias[:, h, KINDS[t][0]:KINDS[t][0] + nw], 1.0, -3e38,
                                                         ALU.add, ALU.max, m1[:, n:n + 1])
                            dve.drain()
                            if near:
                                dve.scalar_tensor_tensor(out=nm[:, n:n + 1], in0=m1[:, n:n + 1], scalar=m2[:, n:n + 1],
                                                         in1=minus[:, :], op0=ALU.max, op1=ALU.mult)\
                                    .then_inc(max_ready, 1)
                            else:
                                dve.tensor_scalar(nm[:, n:n + 1], m2[:, n:n + 1], -1.0, None, ALU.mult)\
                                    .then_inc(max_ready, 1)
                        if 1 <= n <= NU:
                            _, keys = key_tiles(units[n - 1][0])
                            first = 3 if len(keys) > 3 else 1
                            dve.wait_ge(pT_ready, i * NU + n)
                            dve.tensor_copy(pT[(n - 1) % 2][:, 0:first * P], pT_ps[0][:, 0:first * P])\
                                .then_inc(pT_stored_dve, 1)
                        if n >= 2:
                            t, h = units[n - 2]
                            c = slice(n - 2, n - 1)
                            if t < LT:
                                dve.tensor_tensor(total[:, c], sums[:, 0, c], sums[:, 1, c], ALU.add)
                                dve.drain()
                                dve.reciprocal(rinv[:, c], total[:, c])
                            else:
                                dve.reciprocal(rinv[:, c], sums[:, 1, c])
                            dve.drain()
                            dve.wait_ge(pv_ready, i * NU + (n - 1))
                            dve.scalar_tensor_tensor(out=y[:, t % 2, h * HD:(h + 1) * HD], in0=o_ps[n % 2][:, 0:HD],
                                                     scalar=rinv[:, c], in1=zs[:, t, h * HD:(h + 1) * HD],
                                                     op0=ALU.mult, op1=ALU.mult).then_inc(y_ready, 1)


SEQ_TILE = [j + CT if j < LT else j - LT for j in range(NT)]


def stage_gates(nc, a, k):
    with Stage(nc, "gates") as s:
        wg, bg = s.sb("wg", [P, KD, P]), s.sb("bg", [P, 1])
        g, t0, t1 = s.sb("g", [P, NTOK]), s.sb("t0", [P, NTOK]), s.sb("t1", [P, NTOK])
        r_lf, r_i, b, m, ones = (s.sb(n, [36, NTOK]) for n in ("r_lf", "r_i", "b", "m", "ones"))
        a_out, rows = s.sb("a_out", [36, NTOK]), s.sb("rows", [P, NTOK])
        ps0, ps1 = s.ps("ps0"), s.ps("ps1")
        col_ps = [s.ps(f"col_ps{n}") for n in range(2)]
        zeroed, w_in, a_saved = s.sem("zeroed"), s.sem("w_in"), s.sem("a_saved")
        (products_ready, g_ready, ef_ready, one_ready, ln_ready, a_ready, bm_ready, em_ready, rows_ready, turned,
         stored) = (s.sem(n) for n in ("products_ready", "g_ready", "ef_ready", "one_ready", "ln_ready", "a_ready",
                                       "bm_ready", "em_ready", "rows_ready", "turned", "stored"))

        def in_order(dst, src, d0, s0, back):
            for n, (at, to) in enumerate(((slice(SEQ, NTOK), slice(0, CTX)), (slice(0, SEQ), slice(CTX, NTOK)))):
                x = src[s0:s0 + 4, at]
                ins = nc.vector.tensor_copy(dst[d0:d0 + 4, to], x[:, ::-1] if back else x)
            return ins

        with nc.Block() as block:
            @block.sync
            def _(sp):
                sp.wait_ge(zeroed, 2)
                w = a["w_in_ab"][0][:, 9 * D:9 * D + 16].rearrange("(k p) n -> p k n", p=P)
                bias = a["b_gate_ab"].rearrange("a n -> n a")
                for q in range(4):
                    sp.dma_start(wg[:, :, 32 * q:32 * q + 4], w[:, :, 4 * q:4 * q + 4]).then_inc(w_in, 16)
                    sp.dma_start(bg[32 * q:32 * q + 4, :], bias[4 * q:4 * q + 4, :]).then_inc(w_in, 16)
                sp.wait_ge(a_ready, 1)
                for d in range(2):
                    sp.dma_start(k["a_rows"][d], a_out[32 * d:32 * d + 4, :]).then_inc(a_saved, 16)
                sp.wait_ge(a_saved, 32)

            @block.gpsimd
            def _(pool):
                pool.memset(wg[:, :, :], 0.0).then_inc(zeroed, 1)
                pool.memset(bg[:, :], 0.0).then_inc(zeroed, 1)
                pool.memset(ones[:, :], 1.0)
                pool.memset(r_lf[:, :], 0.0)
                pool.memset(r_i[:, :], 0.0)
                pool.memset(rows[:, :], 0.0)
                pool.drain().then_inc(zeroed, 1)

            @block.tensor
            def _(pe):
                pe.wait_ge(w_in, 16 * 8)
                for ps, c0, n in ((ps0, 0, SEQ), (ps1, SEQ, CTX)):
                    for kk in range(KD):
                        mm = pe.matmul(ps[:, 0:n], wg[:, kk, :], k["hT"][:, kk, c0:c0 + n],
                                       start=kk == 0, stop=kk == KD - 1)
                mm.then_inc(products_ready, 1)
                pe.wait_ge(rows_ready, 1)
                for t in range(NT):
                    tr = pe.transpose(col_ps[t // 3][:, t % 3 * P:t % 3 * P + P], rows[:, t * P:(t + 1) * P],
                                      k["ident"][:, :])
                tr.then_inc(turned, 1)

            @block.scalar
            def _(act):
                act.wait_ge(g_ready, 1)
                act.activation(t0[:, :], g[:, :], ACT.Abs)
                act.drain()
                act.activation(t1[:, :], t0[:, :], ACT.Exp, scale=-1.0)
                act.drain()
                act.activation(t0[:, :], t1[:, :], ACT.Ln, bias=1.0).then_inc(ln_ready, 1)
                act.wait_ge(bm_ready, 1)
                act.activation(r_i[:, :], b[:, :], ACT.Exp, scale=-1.0).then_inc(em_ready, 1)

            @block.vector
            def _(dve):
                dve.wait_ge(zeroed, 3)
                dve.wait_ge(products_ready, 1)
                dve.tensor_scalar(g[:, 0:SEQ], ps0[:, :], bg[:, 0:1], None, ALU.add)
                dve.tensor_scalar(g[:, SEQ:NTOK], ps1[:, 0:CTX], bg[:, 0:1], None, ALU.add).then_inc(g_ready, 1)
                dve.wait_ge(ln_ready, 1)
                dve.drain()
                dve.scalar_tensor_tensor(out=t1[:, :], in0=g[:, :], scalar=0.0, in1=t0[:, :], op0=ALU.min,
                                         op1=ALU.subtract)
                dve.drain()
                for d in range(2):
                    in_order(r_lf, t1, 32 * d, 32 + 64 * d, d == 1)
                    in_order(r_i, g, 32 * d, 64 * d, d == 1)
                dve.drain()
                dve.tensor_tensor_scan(b[:, :], ones[:, :], r_lf[:, :], 0.0, ALU.mult, ALU.add)
                dve.drain()
                dve.tensor_tensor(r_lf[:, :], r_i[:, :], b[:, :], ALU.subtract)
                dve.drain()
                dve.tensor_tensor_scan(m[:, :], r_lf[:, :], r_lf[:, :], 0.0, ALU.max, ALU.max)
                dve.tensor_copy(a_out[0:4, :], r_lf[0:4, :])
                for at in (slice(0, CTX), slice(CTX, NTOK)):
                    cp = dve.tensor_copy(a_out[32:36, at], r_lf[32:36, at][:, ::-1])
                cp.then_inc(a_ready, 1)
                dve.drain()
                dve.tensor_tensor(b[:, :], b[:, :], m[:, :], ALU.add)
                dve.tensor_scalar(r_lf[:, :], m[:, :], -1.0, None, ALU.mult)
                dve.drain().then_inc(bm_ready, 1)
                dve.wait_ge(em_ready, 1)
                for q, src in enumerate((r_lf, r_i)):
                    dve.tensor_copy(rows[64 * q:64 * q + 4, :], src[0:4, :])
                    for at in (slice(0, CTX), slice(CTX, NTOK)):
                        cp = dve.tensor_copy(rows[64 * q + 32:64 * q + 36, at], src[32:36, at][:, ::-1])
                cp.then_inc(rows_ready, 1)
                dve.wait_ge(turned, 1)
                for n in range(2):
                    dve.tensor_copy(k["m_cols"][:, 3 * n:3 * n + 3, :, :],
                                    col_ps[n][:, 0:3 * P].rearrange("p (t q c) -> p t q c", t=3, q=4)[:, :, :, 0:4])


def stage_mlstm(nc, a, k, yT):
    DH, KB = ML_DIM, ML_DIM // P
    NU = NT

    def fwd_range(t):
        return (0, (t + 1) * P)

    def bwd_ranges(t):
        if t < CT:
            return [(t * P, CTX)]
        return [(0, NTOK)] if t == CT else [(0, CTX), (t * P, NTOK)]

    def keys_of(t):
        return CT if t < CT else NT

    with Stage(nc, "ml") as s:
        w = [s.sb(f"w{u}", [P, KD, 512]) for u in range(2)]
        cos, sin = s.sb("cos", [P, LT, 2, 64]), s.sb("sin", [P, LT, 2, 64])
        qk, rot = [s.sb(f"qk{u}", [P, 2, DH]) for u in range(2)], s.sb("rot", [P, 2, 2, 64])
        qT, kT = s.sb("qT", [P, KB, NTOK]), s.sb("kT", [P, KB, NTOK])
        v, so, sz = s.sb("v", [P, NT, DH]), s.sb("so", [P, NT, DH]), s.sb("sz", [P, NT, DH])
        ex, rx = s.sb("ex", [P, DH]), s.sb("rx", [P, DH])
        ab = [s.sb(f"ab{d}", [P, NTOK]) for d in range(2)]
        abd = [s.sb(f"abd{d}", [P, NTOK]) for d in range(2)]
        tri = s.sb("tri", [P, 2, P])
        e = [[s.sb(f"e{u}{d}", [P, NTOK]) for d in range(2)] for u in range(2)]
        pT = [s.sb(f"pT{u}", [P, NTOK]) for u in range(2)]
        hcols, hn = s.sb("hcols", [P, NT, 4]), s.sb("hn", [P, KB])
        den, rden = s.sb("den", [P, NU, 2]), s.sb("rden", [P, NU, 2])
        gated, y = [s.sb(f"gated{u}", [P, DH]) for u in range(2)], [s.sb(f"y{u}", [P, DH]) for u in range(2)]
        ss, ms, rstd, half = (s.sb(n, [P, NU]) for n in ("ss", "ms", "rstd", "half"))
        banks = [s.ps(f"bank{n}") for n in range(5)]
        s_ps = s.ps("s_ps", (P, 1024))
        pT_ps = [s.ps("pT_ps"), banks[0]]
        proj, turn_ps, o_ps = banks[0:3], banks[3:5], banks[1:3]

        const_in, a_in = s.sem("const_in"), s.sem("a_in")
        w_in = [s.sem(f"w_in{u}") for u in range(3)]
        (proj_ready, cols_ready, rotated, qk_turned, qk_stored, vo_exp, vo_done, z_exp, z_done, diag_ready,
         scores_ready, exp_ready, den_ready, wb_scaled, w_ready, pT_ready, pT_stored_dve, pT_stored_act, pv_ready,
         gated_ready, squares_ready, means_ready, rstd_ready, y_ready, y_turned, yT_stored) = (s.sem(n) for n in (
             "proj_ready", "cols_ready", "rotated", "qk_turned", "qk_stored", "vo_exp", "vo_done",
             "z_exp", "z_done", "diag_ready", "scores_ready", "exp_ready", "den_ready", "wb_scaled", "w_ready",
             "pT_ready", "pT_stored_dve", "pT_stored_act", "pv_ready", "gated_ready", "squares_ready",
             "means_ready", "rstd_ready", "y_ready", "y_turned", "yT_stored"))

        def h_tile(kk, j):
            return k["hT"][:, kk, j * P:(j + 1) * P]

        with nc.Block() as block:
            @block.sync
            def _(sp):
                sp.dma_start(cos[:, :, :, :], a["rope_cos"]).then_inc(const_in, 16)
                sp.dma_start(sin[:, :, :, :], a["rope_sin"]).then_inc(const_in, 16)
                sp.dma_start(tri[:, :, :], a["tri"]).then_inc(const_in, 16)
                src = a["w_in_ab"][0].rearrange("(k p) n -> p k n", p=P)

                def load(head, piece):
                    parts = ((4, 5), (6, 7), (8,))[piece]
                    for n, x in enumerate(parts):
                        sp.dma_start(w[piece % 2][:, :, n * DH:(n + 1) * DH],
                                     src[:, :, bass.ds(head * DH + x * D, DH)]).then_inc(w_in[piece], 16)

                def load_a(head):
                    for d in range(2):
                        sp.dma_start(ab[d][:, :], k["a_rows"][d, bass.ds(head, 1), :].to_broadcast([P, NTOK]))\
                            .then_inc(a_in, 16)

                load(0, 0)
                load(0, 1)
                load_a(0)
                with sp.Fori(0, ML_HEADS - 1) as i:
                    sp.wait_ge(proj_ready, i * 18 + NT)
                    load(i, 2)
                    sp.wait_ge(proj_ready, i * 18 + 2 * NT)
                    load(i + 1, 1)
                    sp.wait_ge(proj_ready, i * 18 + 3 * NT)
                    load(i + 1, 0)
                    sp.wait_ge(exp_ready, i * NU + NU)
                    load_a(i + 1)
                sp.wait_ge(proj_ready, (ML_HEADS - 1) * 18 + NT)
                load(ML_HEADS - 1, 2)

            @block.tensor
            def _(pe):
                with pe.Fori(0, ML_HEADS) as i:
                    def project(j, u, width):
                        for kk in range(KD):
                            mm = pe.matmul(proj[j % 3][:, 0:width], h_tile(kk, j), w[u][:, kk, 0:width],
                                           start=kk == 0, stop=kk == KD - 1)
                        mm.then_inc(proj_ready, 1)

                    def turn_qk(j):
                        pe.wait_ge(rotated, i * NT + (j + 1))
                        if j >= 2:
                            pe.wait_ge(qk_stored, i * NT + (j - 1))
                        for x in range(2):
                            for b in range(KB):
                                tr = pe.transpose(turn_ps[j % 2][:, (2 * x + b) * P:(2 * x + b + 1) * P],
                                                  qk[j % 2][:, x, b * P:(b + 1) * P], k["ident"][:, :])
                        tr.then_inc(qk_turned, 1)

                    pe.wait_ge(w_in[0], i * 32 + 32)
                    for j in range(NT):
                        if j >= 3:
                            pe.wait_ge(rotated, i * NT + (j - 2))
                        project(j, 0, 512)
                        if j >= 2:
                            turn_qk(j - 2)
                    pe.wait_ge(w_in[1], i * 32 + 32)
                    for j in range(NT):
                        if j < 3:
                            pe.wait_ge(rotated, i * NT + (j + 4))
                        else:
                            pe.wait_ge(vo_exp, i * NT + (j - 2))
                        project(j, 1, 512)
                        if j < 2:
                            turn_qk(j + 4)
                    pe.wait_ge(w_in[2], i * 16 + 16)
                    for j in range(NT):
                        if j < 3:
                            pe.wait_ge(vo_exp, i * NT + (j + 4))
                        else:
                            pe.wait_ge(z_done, i * NT + (j - 2))
                        project(j, 0, 256)
                    pe.wait_ge(qk_stored, i * NT + NT)
                    pe.wait_ge(z_done, i * NT + NT)
                    for n in range(NU + 4):
                        if n < NU:
                            if n >= 1:
                                pe.wait_ge(den_ready, i * NU + n)
                            for c0 in range(0, keys_of(n) * P, 512):
                                c1 = min(c0 + 512, keys_of(n) * P)
                                for b in range(KB):
                                    mm = pe.matmul(s_ps[:, c0:c1], qT[:, b, n * P:(n + 1) * P], kT[:, b, c0:c1],
                                                   start=b == 0, stop=b == KB - 1)
                            mm.then_inc(scores_ready, 1)
                        if 2 <= n < NU + 2:
                            pe.wait_ge(pT_stored_dve, i * NU + (n - 1))
                            pe.wait_ge(pT_stored_act, i * NU + (n - 1))
                        if 1 <= n <= NU:
                            t = n - 1
                            pe.wait_ge(w_ready, i * NU + n)
                            for b in range(keys_of(t)):
                                src = e[t % 2][1 if b > t else 0]
                                hf = keys_of(t) // 2
                                tr = pe.transpose(pT_ps[b // hf][:, b % hf * P:b % hf * P + P],
                                                  src[:, b * P:(b + 1) * P], k["ident"][:, :])
                            tr.then_inc(pT_ready, 1)
                        if 2 <= n < NU + 2:
                            t = n - 2
                            for b in range(keys_of(t)):
                                mm = pe.matmul(o_ps[t % 2][:, 0:DH], pT[t % 2][:, b * P:(b + 1) * P], v[:, b, :],
                                               start=b == 0, stop=b == keys_of(t) - 1)
                            mm.then_inc(pv_ready, 1)
                        if n >= 4:
                            t = n - 4
                            pe.wait_ge(y_ready, i * NU + (t + 1))
                            if t >= 2:
                                pe.wait_ge(yT_stored, i * NU + (t - 1))
                            for b in range(KB):
                                tr = pe.transpose(turn_ps[t % 2][:, b * P:(b + 1) * P], y[t % 2][:, b * P:(b + 1) * P],
                                                  k["ident"][:, :])
                            tr.then_inc(y_turned, 1)
                    pe.wait_ge(yT_stored, i * NU + NU)

            @block.scalar
            def _(act):
                with act.Fori(0, ML_HEADS) as i:
                    def store_qk(j):
                        at = slice(SEQ_TILE[j] * P, SEQ_TILE[j] * P + P)
                        ps = turn_ps[j % 2][:, :].rearrange("p (x b c) -> p x b c", x=2, b=KB)
                        act.wait_ge(qk_turned, i * NT + (j + 1))
                        act.activation(qT[:, :, at], ps[:, 0], ACT.Copy)
                        act.activation(kT[:, :, at], ps[:, 1], ACT.Copy, scale=DH ** -0.5).then_inc(qk_stored, 1)

                    for j in range(NT):
                        store_qk(j)
                    for j in range(NT):
                        act.wait_ge(proj_ready, i * 18 + (NT + j + 1))
                        act.activation(v[:, SEQ_TILE[j], :], proj[j % 3][:, 0:DH], ACT.Copy)
                        if j >= 1:
                            act.wait_ge(vo_done, i * NT + j)
                        act.activation(ex[:, :], proj[j % 3][:, DH:2 * DH], ACT.Exp, scale=-1.0).then_inc(vo_exp, 1)
                    act.wait_ge(vo_done, i * NT + NT)
                    for j in range(NT):
                        act.wait_ge(proj_ready, i * 18 + (2 * NT + j + 1))
                        if j >= 1:
                            act.wait_ge(z_done, i * NT + j)
                        act.activation(ex[:, :], proj[j % 3][:, 0:DH], ACT.Exp, scale=-1.0).then_inc(z_exp, 1)
                    act.wait_ge(cols_ready, i + 1)
                    act.wait_ge(diag_ready, i * 2 + 2)
                    for n in range(NU + 4):
                        if n < NU:
                            if n >= 2:
                                act.wait_ge(pT_ready, i * NU + (n - 1))
                            st, dg = n, slice(n * P, (n + 1) * P)
                            for d, ranges in enumerate(([fwd_range(n)], bwd_ranges(n))):
                                bias = hcols[:, n, d:d + 1]
                                for lo, hi in ranges:
                                    for c0, c1, src in ((lo, min(hi, n * P), ab[d]),
                                                        (max(lo, n * P), min(hi, (n + 1) * P), abd[d]),
                                                        (max(lo, (n + 1) * P), hi, ab[d])):
                                        if c0 < c1:
                                            act.activation(e[n % 2][d][:, c0:c1], src[:, c0:c1], ACT.Exp, bias=bias)
                            act.drain().then_inc(exp_ready, 1)
                            act.wait_ge(den_ready, i * NU + (n + 1))
                            for lo, hi in bwd_ranges(n):
                                act.activation(e[n % 2][1][:, lo:hi], e[n % 2][1][:, lo:hi], ACT.Copy,
                                               scale=rden[:, n, 1:2])
                            act.drain().then_inc(wb_scaled, 1)
                        if 1 <= n <= NU:
                            t = n - 1
                            hf = keys_of(t) // 2
                            act.wait_ge(pT_ready, i * NU + n)
                            act.activation(pT[t % 2][:, hf * P:2 * hf * P], pT_ps[1][:, 0:hf * P], ACT.Copy)\
                                .then_inc(pT_stored_act, 1)
                        if 2 <= n < NU + 2:
                            t = n - 2
                            act.wait_ge(gated_ready, i * NU + (t + 1))
                            act.activation(ex[:, :], gated[t % 2][:, :], ACT.Square, accum_out=ss[:, t:t + 1])\
                                .then_inc(squares_ready, 1)
                        if n >= 4:
                            t = n - 4
                            act.wait_ge(y_turned, i * NU + (t + 1))
                            act.sem_inc(k["apart"], 1)
                            tok = (t - CT) * P if t >= CT else SEQ + t * P
                            for b in range(KB):
                                st_ = act.activation(yT[:, bass.ds(i * KB + (KD + b), 1), tok:tok + P].squeeze(1),
                                                     turn_ps[t % 2][:, b * P:(b + 1) * P], ACT.Copy,
                                                     scale=hn[:, b:b + 1])
                            st_.then_inc(yT_stored, 1)

            @block.gpsimd
            def _(pool):
                pool.memset(half[:, :], -0.5)
                pool.wait_ge(const_in, 48)
                with pool.Fori(0, ML_HEADS) as i:
                    pool.wait_ge(a_in, i * 32 + 32)
                    pool.sem_inc(k["apart"], 1)
                    for d in range(2):
                        pool.tensor_tensor(abd[d][:, :].rearrange("p (t c) -> p t c", c=P),
                                           ab[d][:, :].rearrange("p (t c) -> p t c", c=P),
                                           tri[:, d, :].unsqueeze(1).to_broadcast([P, NT, P]), ALU.add)\
                            .then_inc(diag_ready, 1)
                    for t in range(NU):
                        pool.wait_ge(means_ready, i * NU + (t + 1))
                        pool.tensor_tensor(rstd[:, t:t + 1], ms[:, t:t + 1], half[:, 0:1], ALU.pow)\
                            .then_inc(rstd_ready, 1)

            @block.vector
            def _(dve):
                dve.wait_ge(const_in, 48)
                with dve.Fori(0, ML_HEADS) as i:
                    for j in range(NT):
                        dve.wait_ge(proj_ready, i * 18 + (j + 1))
                        if j >= 2:
                            dve.wait_ge(qk_turned, i * NT + (j - 1))
                        if j >= LT:
                            dve.tensor_copy(qk[j % 2][:, :, :], proj[j % 3][:, :].rearrange("p (x d) -> p x d", x=2))\
                                .then_inc(rotated, 1)
                            continue
                        for x in range(2):
                            src = proj[j % 3][:, x * DH:(x + 1) * DH].rearrange("p (h r f) -> p h r f", h=2, r=2)
                            dst = qk[j % 2][:, x, :].rearrange("p (h r f) -> p h r f", h=2, r=2)
                            dve.tensor_tensor(dst, src, cos[:, j, :, :].unsqueeze(2).to_broadcast([P, 2, 2, 64]), ALU.mult)
                            for r in range(2):
                                dve.tensor_tensor(rot[:, :, r, :], src[:, :, 1 - r, :], sin[:, j, :, :], ALU.mult)
                            dve.drain()
                            for r, op in enumerate((ALU.subtract, ALU.add)):
                                last = dve.tensor_tensor(dst[:, :, r, :], dst[:, :, r, :], rot[:, :, r, :], op)
                            if x == 0:
                                dve.drain()
                        last.then_inc(rotated, 1)
                        dve.drain()
                    for j in range(NT):
                        dve.wait_ge(vo_exp, i * NT + (j + 1))
                        dve.tensor_scalar(rx[:, :], ex[:, :], 1.0, None, ALU.add).then_inc(vo_done, 1)
                        dve.drain()
                        dve.reciprocal(so[:, SEQ_TILE[j], :], rx[:, :])
                        dve.drain()
                    dve.tensor_copy(hcols[:, :, :], k["m_cols"][:, :, :, bass.ds(i, 1)].squeeze(3))
                    dve.tensor_copy(hn[:, :], k["vecT"][:, bass.ds(i * KB + ROW["h_norm_b"], KB)]).then_inc(cols_ready, 1)
                    for j in range(NT):
                        dve.wait_ge(z_exp, i * NT + (j + 1))
                        dve.tensor_scalar(rx[:, :], ex[:, :], 1.0, None, ALU.add)
                        dve.drain()
                        dve.reciprocal(sz[:, SEQ_TILE[j], :], rx[:, :])
                        dve.drain()
                        dve.tensor_tensor(sz[:, SEQ_TILE[j], :], proj[j % 3][:, 0:DH], sz[:, SEQ_TILE[j], :], ALU.mult)\
                            .then_inc(z_done, 1)
                    for n in range(NU + 3):
                        if n >= 3:
                            t = n - 3
                            dve.wait_ge(squares_ready, i * NU + (t + 1))
                            dve.tensor_scalar(ms[:, t:t + 1], ss[:, t:t + 1], 1.0 / DH, EPS, ALU.mult, ALU.add)\
                                .then_inc(means_ready, 1)
                        if n < NU:
                            ef, eb = e[n % 2]
                            dve.wait_ge(exp_ready, i * NU + (n + 1))
                            dve.wait_ge(scores_ready, i * NU + (n + 1))
                            lo, hi = fwd_range(n)
                            dve.tensor_tensor_reduce(ef[:, lo:hi], s_ps[:, lo:hi], ef[:, lo:hi], 1.0, 0.0, ALU.mult,
                                                     ALU.add, den[:, n, 0:1])
                            for x, (lo, hi) in enumerate(bwd_ranges(n)):
                                if x:
                                    dve.drain()
                                dve.tensor_tensor_reduce(eb[:, lo:hi], s_ps[:, lo:hi], eb[:, lo:hi], 1.0,
                                                         den[:, n, 1:2] if x else 0.0, ALU.mult, ALU.add,
                                                         den[:, n, 1:2])
                            dve.drain()
                            dve.scalar_tensor_tensor(out=den[:, n, :], in0=den[:, n, :], scalar=-1.0,
                                                     in1=den[:, n, :], op0=ALU.mult, op1=ALU.max)
                            dve.drain()
                            dve.tensor_tensor(den[:, n, :], den[:, n, :], hcols[:, n, 2:4], ALU.max)
                            dve.drain()
                            dve.reciprocal(rden[:, n, :], den[:, n, :]).then_inc(den_ready, 1)
                            dve.drain()
                            dve.wait_ge(wb_scaled, i * NU + (n + 1))
                            both = [(n * P, (n + 1) * P)] if n < CT else (
                                [(0, CTX), (n * P, (n + 1) * P)])
                            for lo, hi in both:
                                dve.scalar_tensor_tensor(out=ef[:, lo:hi], in0=ef[:, lo:hi], scalar=rden[:, n, 0:1],
                                                         in1=eb[:, lo:hi], op0=ALU.mult, op1=ALU.add)
                            lo, hi = (0, n * P) if n < CT else (CTX, n * P)
                            if lo < hi:
                                dve.tensor_scalar(ef[:, lo:hi], ef[:, lo:hi], rden[:, n, 0:1], None, ALU.mult)
                            dve.drain().then_inc(w_ready, 1)
                        if 1 <= n <= NU:
                            t = n - 1
                            hf = keys_of(t) // 2
                            dve.wait_ge(pT_ready, i * NU + n)
                            dve.tensor_copy(pT[t % 2][:, 0:hf * P], pT_ps[0][:, 0:hf * P]).then_inc(pT_stored_dve, 1)
                        if 2 <= n < NU + 2:
                            t = n - 2
                            dve.wait_ge(pv_ready, i * NU + (t + 1))
                            dve.tensor_tensor(gated[t % 2][:, :], o_ps[t % 2][:, 0:DH], so[:, t, :], ALU.mult)\
                                .then_inc(gated_ready, 1)
                        if n >= 3:
                            t = n - 3
                            if t >= 2:
                                dve.wait_ge(y_turned, i * NU + (t - 1))
                            dve.wait_ge(rstd_ready, i * NU + (t + 1))
                            dve.scalar_tensor_tensor(out=y[t % 2][:, :], in0=gated[t % 2][:, :], scalar=rstd[:, t:t + 1],
                                                     in1=sz[:, t, :], op0=ALU.mult, op1=ALU.mult).then_inc(y_ready, 1)
                            dve.drain()


def stage_output(nc, k, name, lhs, w_dram, chunks, tiles, gates, dst=None):
    NW = 256
    with Stage(nc, name) as s:
        w = [s.sb(f"w{u}", [P, chunks, NW]) for u in range(2)]
        ones, diag = s.sb("ones", [P, P]), s.sb("diag", [P, len(gates), KD, P])
        gate = s.sb("gate", [P, len(gates), D])
        t = [s.sb(f"t{u}", [P, NW]) for u in range(2)]
        banks = [s.ps(f"bank{n}") for n in range(4)]
        w_in = [s.sem(f"w_in{u}") for u in range(2)]
        diag_ready, spread, stored, products_ready, added = (
            s.sem(n) for n in ("diag_ready", "spread", "stored", "products_ready", "added"))
        n_t = len(tiles)
        half = KD // 2
        with nc.Block() as block:
            @block.sync
            def _(sp):
                src = w_dram.rearrange("(k p) n -> p k n", p=P)
                for u in range(2):
                    sp.dma_start(w[u][:, :, :], src[:, :, u * NW:(u + 1) * NW]).then_inc(w_in[u], 16)
                for u in range(2):
                    sp.wait_ge(products_ready, n_t * (u + 1))
                    sp.dma_start(w[u][:, :, :], src[:, :, (u + 2) * NW:(u + 3) * NW]).then_inc(w_in[u], 16)

            @block.tensor
            def _(pe):
                pe.wait_ge(diag_ready, 1)
                for g in range(len(gates)):
                    for h in range(2):
                        n = 2 * g + h
                        pe.matmul(banks[n % 4][:, :], ones[:, :], diag[:, g, h * half:(h + 1) * half, :],
                                  start=True, stop=True).then_inc(spread, 1)
                pe.wait_ge(stored, 2 * len(gates))
                with pe.Fori(0, 2) as i:
                    for u in range(2):
                        pe.wait_ge(w_in[u], i * 16 + 16)
                        for x, j in enumerate(tiles):
                            pe.wait_ge(added, i * (2 * n_t) + (u * n_t + x + 1))
                            bank = banks[(u * n_t + x) % 4]
                            for c in range(chunks):
                                mm = pe.matmul(bank[:, 0:NW], lhs(c, j), w[u][:, c, :],
                                               start=c == 0, stop=c == chunks - 1)
                            mm.then_inc(products_ready, 1)

            @block.vector
            def _(dve):
                dve.memset(ones[:, :], 1.0)
                for g, (mod, v, _, _) in enumerate(gates):
                    dve.tensor_tensor(diag[:, g, :, :], k["ident"][:, :].unsqueeze(1).to_broadcast([P, KD, P]),
                                      k["modT"][:, mod:mod + KD, v:v + 1].to_broadcast([P, KD, P]), ALU.mult)
                dve.drain().then_inc(diag_ready, 1)
                for n in range(2 * len(gates)):
                    dve.wait_ge(spread, n + 1)
                    dve.tensor_copy(gate[:, n // 2, (n % 2) * 512:(n % 2) * 512 + 512], banks[n % 4][:, :])\
                        .then_inc(stored, 1)
                for _ in range(4):
                    dve.drain().then_inc(added, 1)
                with dve.Fori(0, 2) as i:
                    for u in range(2):
                        for x, j in enumerate(tiles):
                            g = [n for n, (_, _, t0, nt) in enumerate(gates) if t0 <= j < t0 + nt][0]
                            at = bass.ds(i * (2 * NW) + u * NW, NW)
                            dve.wait_ge(products_ready, i * (2 * n_t) + (u * n_t + x + 1))
                            dve.tensor_tensor(t[x % 2][:, :], banks[(u * n_t + x) % 4][:, 0:NW], gate[:, g, at], ALU.mult)\
                                .then_inc(added, 1)
                            dve.drain()
                            dve.tensor_tensor(k["xs"][:, j, at], k["xs"][:, j, at], t[x % 2][:, :], ALU.add)
                            dve.drain()


def stage_gla(nc, a, k, yT):
    SMALL = [w for w in HG_LEVELS if w < P]
    NL = len(HG_LEVELS)
    with Stage(nc, "gla") as s:
        w = s.sb("w", [P, KD, 5, P])
        lbh, hn, tiny, half = s.sb("lbh", [P, 2]), s.sb("hn", [P, 1]), s.sb("tiny", [P, 1]), s.sb("half", [P, LT])
        f = [s.sb("f_ctx", [P, 2, CTX]), s.sb("f_fwd", [P, SEQ]), s.sb("f_bwd", [P, SEQ])]
        u = [s.sb("u_ctx", [P, 2, CTX]), s.sb("u_fwd", [P, SEQ]), s.sb("u_bwd", [P, SEQ])]
        kk_ = [s.sb("k_ctx", [P, 2, CTX]), s.sb("k_fwd", [P, SEQ]), s.sb("k_bwd", [P, SEQ])]
        q, eq, uq, kd0 = (s.sb(n, [P, SEQ]) for n in ("q", "eq", "uq", "kd0"))
        arr = [s.sb(f"arr{d}", [P, SEQ + 1]) for d in range(2)]
        arc = [s.sb(f"arc{d}", [P, CTX + 1]) for d in range(2)]
        ones = s.sb("ones", [P, SEQ])
        xy = [s.sb(f"xy{n}", [P, 2, SEQ]) for n in range(2)]
        qk = [s.sb(f"qk{n}", [P, 2, SEQ]) for n in range(2)]
        xq, xc = s.sb("xq", [P, 2, SEQ]), s.sb("xc", [P, 2, CTX])
        masks = s.sb("masks", [P, len(SMALL), P], I32)
        own, near, far = s.sb("own", [P, SEQ]), s.sb("near", [P, SEQ]), s.sb("far", [P, LT, 2 * P])
        v, zs = s.sb("v", [P, NT, P]), s.sb("zs", [P, LT, P])
        ez, uz, rz = s.sb("ez", [P, P]), s.sb("uz", [P, P]), s.sb("rz", [P, P])
        kdT, st = s.sb("kdT", [P, 4, P]), s.sb("st", [P, 2, P])
        ss, ms, rstd = s.sb("ss", [P, LT]), s.sb("ms", [P, LT]), s.sb("rstd", [P, LT])
        sq, y = s.sb("sq", [P, P]), s.sb("y", [P, LT, P])
        b = [s.ps(f"bank{n}") for n in range(8)]
        f_ps, q_ps, iz_ps = [b[2], b[1], b[3]], b[0], [b[4], b[5]]
        w_in, const_in, pool_consts = s.sem("w_in"), s.sem("const_in"), s.sem("pool_consts")
        (f_ready, q_ready, iz_ready, ef_ready, eq_ready, iz_exp, iz_used, f_stored, k_stored, lf_stored, sums_ready,
         q_stored, xy_ready, xy_exp, qk_ready, level_ready, own_stored, near_stored, far_stored, xc_ready, xc_exp,
         kd_ready, kd_turned, kdT_stored, st_ready, st_stored, xq_ready, xq_exp, qp_ready, o_ready, squares_ready,
         means_ready, rstd_ready, y_ready, y_turned, yT_stored, k_diag) = (s.sem(n) for n in (
             "f_ready", "q_ready", "iz_ready", "ef_ready", "eq_ready", "iz_exp", "iz_used", "f_stored", "k_stored",
             "lf_stored", "sums_ready", "q_stored", "xy_ready", "xy_exp", "qk_ready", "level_ready", "own_stored",
             "near_stored", "far_stored", "xc_ready", "xc_exp", "kd_ready", "kd_turned", "kdT_stored", "st_ready",
             "st_stored", "xq_ready", "xq_exp", "qp_ready", "o_ready", "squares_ready", "means_ready", "rstd_ready",
             "y_ready", "y_turned", "yT_stored", "k_diag"))

        def halves(x, wd):
            return x.rearrange("p (n h w) -> p n h w", h=2, w=wd)

        with nc.Block() as block:
            @block.sync
            def _(sp):
                sp.dma_start(masks[:, :, :], a["level_masks"]).then_inc(const_in, 16)
                src = a["w_in_c"][0].rearrange("(k p) n -> p k n", p=P)

                def load(head):
                    for x in range(5):
                        sp.dma_start(w[:, :, x, :], src[:, :, bass.ds(head * P + x * INNER, P)]).then_inc(w_in, 16)

                load(0)
                with sp.Fori(0, HG_HEADS - 1) as i:
                    sp.wait_ge(iz_ready, i * NT + NT)
                    load(i + 1)

            @block.tensor
            def _(pe):
                with pe.Fori(0, HG_HEADS) as i:
                    def project(out, x, c0, n):
                        for c in range(KD):
                            mm = pe.matmul(out, w[:, c, x, :], k["hT"][:, c, c0:c0 + n], start=c == 0, stop=c == KD - 1)
                        return mm

                    pe.wait_ge(w_in, i * 80 + 80)
                    for x in range(2):
                        mm = project(f_ps[0][:, x * CTX:(x + 1) * CTX], 1 + x, SEQ, CTX)
                    mm.then_inc(f_ready, 1)
                    for x in range(2):
                        project(f_ps[1 + x][:, :], 1 + x, 0, SEQ).then_inc(f_ready, 1)
                    project(q_ps[:, :], 0, 0, SEQ).then_inc(q_ready, 1)
                    for j in range(NT):
                        n = 2 * P if j < LT else P
                        if j >= 2:
                            pe.wait_ge(iz_used, i * NT + (j - 1))
                        for c in range(KD):
                            mm = pe.matmul(iz_ps[j % 2][:, 0:n], k["hT"][:, c, j * P:(j + 1) * P],
                                           w[:, c, 3:3 + n // P, :], start=c == 0, stop=c == KD - 1)
                        mm.then_inc(iz_ready, 1)
                    pe.wait_ge(kd_ready, i * 2 + 2)
                    pe.wait_ge(iz_used, i * NT + NT)
                    for d in range(2):
                        for t in range(CT):
                            tr = pe.transpose(b[4][:, (2 * d + t) * P:(2 * d + t + 1) * P],
                                              kk_[0][:, d, t * P:(t + 1) * P], k["ident"][:, :])
                    tr.then_inc(kd_turned, 1)
                    for n in range(len(SMALL) + 1):
                        if n == 0:
                            pe.wait_ge(k_diag, i + 1)
                            pe.wait_ge(q_stored, i + 1)
                            kl, ql = kd0, q
                        else:
                            pe.wait_ge(qk_ready, i * NL + n)
                            kl, ql = qk[(n - 1) % 2][:, 1, :], qk[(n - 1) % 2][:, 0, :]
                        if n >= 2:
                            pe.wait_ge(own_stored, i * (len(SMALL) + 1) + (n - 1))
                        for t in range(LT):
                            at = slice(t * P, (t + 1) * P)
                            mm = pe.matmul(b[n % 2][:, at], kl[:, at], ql[:, at], start=True, stop=True)
                        mm.then_inc(level_ready, 1)
                        if n == 1:
                            pe.wait_ge(kdT_stored, i + 1)
                            for d in range(2):
                                for t in range(CT):
                                    mm = pe.matmul(b[5][:, d * P:(d + 1) * P], kdT[:, 2 * d + t, :], v[:, LT + t, :],
                                                   start=t == 0, stop=t == CT - 1)
                            mm.then_inc(st_ready, 1)
                    pe.wait_ge(qk_ready, i * NL + len(SMALL) + 1)
                    x = qk[len(SMALL) % 2]
                    pe.wait_ge(own_stored, i * (len(SMALL) + 1) + len(SMALL))
                    for t in range(LT):
                        o = t ^ 1
                        mm = pe.matmul(b[0][:, t * P:(t + 1) * P], x[:, 1, o * P:(o + 1) * P], x[:, 0, t * P:(t + 1) * P],
                                       start=True, stop=True)
                    mm.then_inc(level_ready, 1)
                    pe.wait_ge(qk_ready, i * NL + len(SMALL) + 2)
                    x = qk[(len(SMALL) + 1) % 2]
                    for t in range(LT):
                        to = 2 * P if t < 2 else 0
                        mm = pe.matmul(b[2 + t // 2][:, t % 2 * 256:t % 2 * 256 + 256], x[:, 1, t * P:(t + 1) * P],
                                       x[:, 0, to:to + 256], start=True, stop=True)
                    mm.then_inc(level_ready, 1)
                    pe.wait_ge(st_stored, i + 1)
                    pe.wait_ge(qp_ready, i * 2 + 2)
                    pe.wait_ge(own_stored, i * (len(SMALL) + 1) + len(SMALL) + 1)
                    pe.wait_ge(near_stored, i + 1)
                    pe.wait_ge(far_stored, i + 1)
                    for t in range(LT):
                        at = slice(t * P, (t + 1) * P)
                        s0 = 2 if t < 2 else 0
                        fc = slice(t % 2 * P, t % 2 * P + P)
                        parts = [(own[:, at], v[:, t, :]), (near[:, at], v[:, t ^ 1, :]),
                                 (far[:, s0, fc], v[:, s0, :]), (far[:, s0 + 1, fc], v[:, s0 + 1, :]),
                                 (xq[:, 0, at], st[:, 0, :]), (xq[:, 1, at], st[:, 1, :])]
                        for n, (l, r) in enumerate(parts):
                            mm = pe.matmul(b[6][:, at], l, r, start=n == 0, stop=n == len(parts) - 1)
                    mm.then_inc(o_ready, 1)
                    pe.wait_ge(y_ready, i + 1)
                    for t in range(LT):
                        tr = pe.transpose(b[7][:, t * P:(t + 1) * P], y[:, t, :], k["ident"][:, :])
                    tr.then_inc(y_turned, 1)

            @block.scalar
            def _(act):
                act.wait_ge(pool_consts, 1)
                with act.Fori(0, HG_HEADS) as i:
                    for g in range(3):
                        act.wait_ge(f_ready, i * 3 + (g + 1))
                        act.activation(u[g][:, :, :] if g == 0 else u[g][:, :],
                                       f_ps[g][:, :].rearrange("p (d t) -> p d t", d=2) if g == 0 else f_ps[g][:, :],
                                       ACT.Exp, scale=-1.0).then_inc(ef_ready, 1)
                    act.wait_ge(q_ready, i + 1)
                    act.activation(eq[:, :], q_ps[:, :], ACT.Exp, scale=-1.0).then_inc(eq_ready, 1)
                    for g in range(3):
                        act.wait_ge(f_stored, i * 3 + (g + 1))
                        fx = f[g][:, :, :] if g == 0 else f[g][:, :]
                        ux = u[g][:, :, :] if g == 0 else u[g][:, :]
                        act.activation(ux, fx, ACT.Ln, bias=tiny[:, 0:1]).then_inc(lf_stored, 1)
                    for j in range(NT):
                        act.wait_ge(iz_ready, i * NT + (j + 1))
                        cp = act.activation(v[:, j, :], iz_ps[j % 2][:, 0:P], ACT.Copy)
                        if j < LT:
                            if j >= 1:
                                act.wait_ge(iz_used, i * NT + j)
                            act.activation(ez[:, :], iz_ps[j % 2][:, P:2 * P], ACT.Exp, scale=-1.0).then_inc(iz_exp, 1)
                        else:
                            cp.then_inc(iz_exp, 1)
                    act.wait_ge(xc_ready, i + 1)
                    act.activation(xc[:, :, :], xc[:, :, :], ACT.Exp).then_inc(xc_exp, 1)
                    act.wait_ge(xq_ready, i + 1)
                    act.activation(xq[:, :, :], xq[:, :, :], ACT.Exp).then_inc(xq_exp, 1)
                    for n in range(NL):
                        act.wait_ge(xy_ready, i * NL + (n + 1))
                        act.activation(xy[n % 2][:, :, :], xy[n % 2][:, :, :], ACT.Exp).then_inc(xy_exp, 1)
                        if n == 1:
                            act.wait_ge(kd_turned, i + 1)
                            act.activation(kdT[:, :, :], b[4][:, :].rearrange("p (x c) -> p x c", x=4), ACT.Copy)\
                                .then_inc(kdT_stored, 1)
                        if n == 3:
                            act.wait_ge(st_ready, i + 1)
                            act.activation(st[:, :, :], b[5][:, 0:2 * P].rearrange("p (x c) -> p x c", x=2), ACT.Copy)\
                                .then_inc(st_stored, 1)
                    act.wait_ge(level_ready, i * (NL + 1) + (NL + 1))
                    for h in range(2):
                        fs = act.activation(far[:, 2 * h:2 * h + 2, :], b[2 + h][:, :].rearrange("p (x c) -> p x c", x=2),
                                            ACT.Copy)
                    fs.then_inc(far_stored, 1)
                    act.wait_ge(o_ready, i + 1)
                    for t in range(LT):
                        act.activation(sq[:, :], b[6][:, t * P:(t + 1) * P], ACT.Square, accum_out=ss[:, t:t + 1])
                        act.drain()
                    act.drain().then_inc(squares_ready, 1)
                    act.wait_ge(y_turned, i + 1)
                    act.sem_inc(k["apart"], 1)
                    act.activation(yT[:, bass.ds(i, 1), 0:SEQ].squeeze(1), b[7][:, :], ACT.Copy, scale=hn[:, 0:1])\
                        .then_inc(yT_stored, 1)

            @block.gpsimd
            def _(pool):
                pool.memset(half[:, :], -0.5)
                pool.memset(tiny[:, :], 2.0 ** -64)
                pool.memset(ones[:, :], 1.0)
                for x in (*arr, *arc):
                    pool.memset(x[:, 0:1], 0.0)
                pool.drain().then_inc(pool_consts, 1)
                with pool.Fori(0, HG_HEADS) as i:
                    for g in range(3):
                        pool.wait_ge(f_stored, i * 3 + (g + 1))
                        pool.sem_inc(k["apart"], 1)
                        fx = f[g][:, :, :] if g == 0 else f[g][:, :]
                        kx = kk_[g][:, :, :] if g == 0 else kk_[g][:, :]
                        pool.tensor_scalar(kx, fx, -1.0, 1.0, ALU.mult, ALU.add).then_inc(k_stored, 1)
                    pool.drain()
                    pool.tensor_tensor(kd0[:, :], kk_[1][:, :], kk_[2][:, :], ALU.add).then_inc(k_diag, 1)
                    pool.wait_ge(sums_ready, i * 4 + 2)
                    pool.tensor_tensor(xc[:, 0, :], arc[0][:, CTX:CTX + 1].to_broadcast([P, CTX]), arc[0][:, 1:CTX + 1],
                                       ALU.subtract)
                    pool.tensor_copy(xc[:, 1, :], arc[1][:, 0:CTX])
                    pool.drain().then_inc(xc_ready, 1)
                    pool.wait_ge(sums_ready, i * 4 + 4)
                    pool.tensor_tensor(xq[:, 1, :], arr[1][:, SEQ:SEQ + 1].to_broadcast([P, SEQ]), arr[1][:, 0:SEQ],
                                       ALU.subtract)
                    pool.tensor_copy(xq[:, 0, :], arr[0][:, 1:SEQ + 1])
                    pool.drain().then_inc(xq_ready, 1)
                    for n, wd in enumerate(HG_LEVELS):
                        if n >= 2:
                            pool.wait_ge(qk_ready, i * NL + (n - 1))
                        nb = SEQ // (2 * wd)
                        pf, ef = halves(arr[0][:, 1:SEQ + 1], wd), halves(arr[0][:, 0:SEQ], wd)
                        eb = halves(arr[1][:, 0:SEQ], wd)
                        rf, rb = (e[:, :, 1, 0:1].to_broadcast([P, nb, wd]) for e in (ef, eb))
                        x, yb = halves(xy[n % 2][:, 0, :], wd), halves(xy[n % 2][:, 1, :], wd)
                        pool.tensor_tensor(x[:, :, 0, :], rf, pf[:, :, 0, :], ALU.subtract)
                        pool.tensor_tensor(x[:, :, 1, :], pf[:, :, 1, :], rf, ALU.subtract)
                        pool.tensor_tensor(yb[:, :, 0, :], rb, eb[:, :, 0, :], ALU.subtract)
                        pool.tensor_tensor(yb[:, :, 1, :], eb[:, :, 1, :], rb, ALU.subtract)
                        pool.drain().then_inc(xy_ready, 1)
                    pool.wait_ge(means_ready, i + 1)
                    pool.tensor_tensor(rstd[:, :], ms[:, :], half[:, :], ALU.pow).then_inc(rstd_ready, 1)

            @block.vector
            def _(dve):
                dve.wait_ge(const_in, 16)
                dve.wait_ge(pool_consts, 1)
                with dve.Fori(0, HG_HEADS) as i:
                    dve.tensor_copy(lbh[:, :], k["lbT"][:, :, bass.ds(i, 1)].squeeze(2))
                    dve.drain()
                    for g in range(3):
                        ux, fx = (z[g][:, :, :] if g == 0 else z[g][:, :] for z in (u, f))
                        dve.wait_ge(ef_ready, i * 3 + (g + 1))
                        dve.tensor_scalar(fx, ux, 1.0, None, ALU.add)
                        dve.drain()
                        dve.reciprocal(fx, fx)
                        dve.drain()
                        dve.tensor_scalar(fx, fx, lbh[:, 1:2], lbh[:, 0:1], ALU.mult, ALU.add).then_inc(f_stored, 1)
                    dve.wait_ge(eq_ready, i + 1)
                    dve.tensor_scalar(uq[:, :], eq[:, :], 1.0, None, ALU.add)
                    dve.drain()
                    dve.reciprocal(uq[:, :], uq[:, :])
                    dve.drain()
                    dve.tensor_tensor(q[:, :], q_ps[:, :], uq[:, :], ALU.mult).then_inc(q_stored, 1)
                    dve.wait_ge(lf_stored, i * 3 + 1)
                    for d in range(2):
                        dve.tensor_tensor_scan(arc[d][:, 1:CTX + 1], ones[:, 0:CTX], u[0][:, d, :], 0.0, ALU.mult,
                                               ALU.add).then_inc(sums_ready, 1)
                    for d in range(2):
                        dve.wait_ge(lf_stored, i * 3 + (2 + d))
                        dve.tensor_tensor_scan(arr[d][:, 1:SEQ + 1], ones[:, :], u[1 + d][:, :], 0.0, ALU.mult, ALU.add)\
                            .then_inc(sums_ready, 1)
                    for j in range(NT):
                        dve.wait_ge(iz_exp, i * NT + (j + 1))
                        dve.sem_inc(k["apart"], 1)
                        if j >= LT:
                            dve.drain().then_inc(iz_used, 1)
                            continue
                        dve.tensor_scalar(uz[:, :], ez[:, :], 1.0, None, ALU.add)
                        dve.drain()
                        dve.reciprocal(rz[:, :], uz[:, :])
                        dve.drain()
                        dve.tensor_tensor(zs[:, j, :], iz_ps[j % 2][:, P:2 * P], rz[:, :], ALU.mult).then_inc(iz_used, 1)
                    dve.wait_ge(xc_exp, i + 1)
                    for d in range(2):
                        dve.tensor_tensor(kk_[0][:, d, :], kk_[0][:, d, :], xc[:, d, :], ALU.mult).then_inc(kd_ready, 1)
                    dve.wait_ge(xq_exp, i + 1)
                    for d in range(2):
                        dve.tensor_tensor(xq[:, d, :], xq[:, d, :], q[:, :], ALU.mult).then_inc(qp_ready, 1)

                    def collect(n):
                        dve.wait_ge(level_ready, i * (NL + 1) + (n + 1))
                        dve.sem_inc(k["apart"], 1)
                        if n == 0:
                            cp = dve.tensor_copy(own[:, :], b[0][:, :])
                        else:
                            cp = dve.copy_predicated(own[:, :].rearrange("p (t c) -> p t c", t=LT),
                                                     masks[:, n - 1, :].unsqueeze(1).to_broadcast([P, LT, P]),
                                                     b[n % 2][:, :].rearrange("p (t c) -> p t c", t=LT))
                        cp.then_inc(own_stored, 1)
                        dve.drain()

                    for n, wd in enumerate(HG_LEVELS):
                        dve.wait_ge(xy_exp, i * NL + (n + 1))
                        if n >= 2:
                            dve.wait_ge(level_ready, i * (NL + 1) + n)
                        x, yb = halves(xy[n % 2][:, 0, :], wd), halves(xy[n % 2][:, 1, :], wd)
                        ql, kl = halves(qk[n % 2][:, 0, :], wd), halves(qk[n % 2][:, 1, :], wd)
                        qh, kf, kb = halves(q[:, :], wd), halves(kk_[1][:, :], wd), halves(kk_[2][:, :], wd)
                        dve.tensor_tensor(ql[:, :, 0, :], qh[:, :, 0, :], yb[:, :, 0, :], ALU.mult)
                        dve.tensor_tensor(ql[:, :, 1, :], qh[:, :, 1, :], x[:, :, 1, :], ALU.mult)
                        dve.tensor_tensor(kl[:, :, 0, :], kf[:, :, 0, :], x[:, :, 0, :], ALU.mult)
                        dve.tensor_tensor(kl[:, :, 1, :], kb[:, :, 1, :], yb[:, :, 1, :], ALU.mult)
                        dve.drain().then_inc(qk_ready, 1)
                        if n <= len(SMALL):
                            collect(n)
                    dve.wait_ge(level_ready, i * (NL + 1) + (len(SMALL) + 2))
                    dve.tensor_copy(near[:, :], b[0][:, :]).then_inc(near_stored, 1)
                    dve.wait_ge(squares_ready, i + 1)
                    dve.tensor_scalar(ms[:, :], ss[:, :], 1.0 / P, EPS, ALU.mult, ALU.add).then_inc(means_ready, 1)
                    dve.tensor_copy(hn[:, :], k["vecT"][:, bass.ds(i + ROW["h_norm_c"], 1)])
                    dve.wait_ge(rstd_ready, i + 1)
                    for t in range(LT):
                        dve.scalar_tensor_tensor(out=y[:, t, :], in0=b[6][:, t * P:(t + 1) * P], scalar=rstd[:, t:t + 1],
                                                 in1=zs[:, t, :], op0=ALU.mult, op1=ALU.mult)
                    dve.drain().then_inc(y_ready, 1)


def stage_conv(nc, a, k, yaT, f_rows):
    CH = 512 // P
    with Stage(nc, "conv") as s:
        w = [s.sb(f"w{n}", [P, KD, 3, P]) for n in range(2)]
        wf, bf = s.sb("wf", [P, KD, 8]), s.sb("bf", [8, 1])
        g, t0, t1, cum, ones = (s.sb(n, [8, SEQ]) for n in ("g", "t0", "t1", "cum", "ones"))
        c = [s.sb(f"c{n}", [P, SEQ]) for n in range(2)]
        u = s.sb("u", [P, SEQ + 2])
        taps = s.sb("taps", [P, 3, 1])
        s0, s1 = s.sb("s0", [P, SEQ]), s.sb("s1", [P, SEQ])
        ps = [[s.ps(f"ps_{n}{h}") for n in ("x", "b", "c")] for h in range(2)]
        f_ps = s.ps("f_ps")
        w_in, f_in = [s.sem(f"w_in{n}") for n in range(2)], s.sem("f_in")
        (f_ready, g_ready, ln_ready, f_rows_ready, f_saved, products_ready, c_stored, chunk_done) = (
            s.sem(n) for n in ("f_ready", "g_ready", "ln_ready", "f_rows_ready", "f_saved", "products_ready",
                               "c_stored", "chunk_done"))
        with nc.Block() as block:
            @block.sync
            def _(sp):
                src = a["w_in_2"][0].rearrange("(k p) n -> p k n", p=P)

                def load(n, col):
                    for x in range(3):
                        sp.dma_start(w[n][:, :, x, :], src[:, :, bass.ds(col + x * 512, P)]).then_inc(w_in[n], 16)

                sp.dma_start(wf[:, :, :], src[:, :, 3072:3080]).then_inc(f_in, 16)
                sp.dma_start(bf[:, :], a["b_forget_2"].rearrange("a n -> n a")).then_inc(f_in, 16)
                for n in range(2):
                    load(n, n * P)
                for n in range(2):
                    sp.wait_ge(products_ready, n + 1)
                    load(n, (n + 2) * P)
                sp.wait_ge(f_rows_ready, 1)
                sp.dma_start(f_rows, cum[:, :]).then_inc(f_saved, 16)
                sp.wait_ge(f_saved, 16)

            @block.tensor
            def _(pe):
                pe.wait_ge(f_in, 32)
                for kk in range(KD):
                    mm = pe.matmul(f_ps[0:8, :], wf[:, kk, :], k["hT"][:, kk, 0:SEQ], start=kk == 0, stop=kk == KD - 1)
                mm.then_inc(f_ready, 1)
                with pe.Fori(0, CH // 2) as i:
                    for n in range(2):
                        pe.wait_ge(w_in[n], i * 48 + 48)
                        pe.wait_ge(chunk_done, i * 2 + (n + 1))
                        for x in range(3):
                            for kk in range(KD):
                                mm = pe.matmul(ps[n][x][:, :], w[n][:, kk, x, :], k["hT"][:, kk, 0:SEQ],
                                               start=kk == 0, stop=kk == KD - 1)
                        mm.then_inc(products_ready, 1)

            @block.scalar
            def _(act):
                act.wait_ge(g_ready, 1)
                act.activation(t0[:, :], g[:, :], ACT.Abs)
                act.drain()
                act.activation(t1[:, :], t0[:, :], ACT.Exp, scale=-1.0)
                act.drain()
                act.activation(t0[:, :], t1[:, :], ACT.Ln, bias=1.0).then_inc(ln_ready, 1)
                with act.Fori(0, CH // 2) as i:
                    for n in range(2):
                        act.wait_ge(products_ready, i * 2 + (n + 1))
                        act.activation(c[n][:, :], ps[n][2][:, :], ACT.Copy).then_inc(c_stored, 1)

            @block.vector
            def _(dve):
                dve.memset(ones[:, :], 1.0)
                dve.memset(u[:, 0:2], 0.0)
                dve.drain().then_inc(chunk_done, 1)
                dve.drain().then_inc(chunk_done, 1)
                dve.wait_ge(f_ready, 1)
                dve.tensor_scalar(g[:, :], f_ps[0:8, :], bf[:, 0:1], None, ALU.add).then_inc(g_ready, 1)
                dve.wait_ge(ln_ready, 1)
                dve.drain()
                dve.tensor_scalar(t1[:, :], g[:, :], 0.0, None, ALU.min)
                dve.drain()
                dve.tensor_tensor(g[:, :], t0[:, :], t1[:, :], ALU.subtract)
                dve.drain()
                dve.tensor_tensor_scan(cum[:, :], ones[:, :], g[:, :], 0.0, ALU.mult, ALU.add).then_inc(f_rows_ready, 1)
                table = k["vecT"][:, ROW["conv_w_2"]:ROW["conv_w_2"] + 12].rearrange("p (j c) -> p j c", c=CH)
                with dve.Fori(0, CH // 2) as i:
                    for n in range(2):
                        dve.drain()
                        dve.tensor_copy(taps[:, :, :], table[:, :, bass.ds(i * 2 + n, 1)])
                        dve.wait_ge(c_stored, i * 2 + (n + 1))
                        dve.tensor_tensor(u[:, 2:SEQ + 2], ps[n][0][:, :], c[n][:, :], ALU.mult)
                        dve.drain()
                        dve.tensor_scalar(s0[:, :], u[:, 0:SEQ], taps[:, 0, :], None, ALU.mult)
                        dve.drain()
                        dve.scalar_tensor_tensor(out=s1[:, :], in0=u[:, 1:SEQ + 1], scalar=taps[:, 1, :], in1=s0[:, :],
                                                 op0=ALU.mult, op1=ALU.add)
                        dve.drain()
                        dve.scalar_tensor_tensor(out=s0[:, :], in0=u[:, 2:SEQ + 2], scalar=taps[:, 2, :], in1=s1[:, :],
                                                 op0=ALU.mult, op1=ALU.add)
                        dve.drain()
                        dve.tensor_tensor(yaT[:, bass.ds(i * 2 + n, 1), 0:SEQ].squeeze(1), s0[:, :], ps[n][1][:, :],
                                          ALU.mult).then_inc(chunk_done, 1)


def stage_attention_2(nc, a, k, ybT, f_rows):
    HD, PAIRS = 64, 4
    OFF = [0, 1, 3, 6]
    PACK = 10 * P
    units = [(t, h) for t in range(LT) for h in range(2)]
    NU = len(units)
    with Stage(nc, "att") as s:
        w = s.sb("w", [P, KD, 3, P])
        squares, qkn = s.sb("squares", [P, 4, HD]), [s.sb(f"qkn{u}", [P, 4, HD]) for u in range(2)]
        ss, ms, rstd, half = (s.sb(n, [P, 4]) for n in ("ss", "ms", "rstd", "half"))
        qw, kw = s.sb("qw", [P, 1]), s.sb("kw", [P, 1])
        qT, kT = s.sb("qT", [P, SEQ]), s.sb("kT", [P, SEQ])
        v = s.sb("v", [P, LT, P])
        mask, fb = s.sb("mask", [P, PACK]), [s.sb(f"fb{h}", [P, SEQ]) for h in range(2)]
        bias = s.sb("bias", [P, 2, PACK])
        sc, p = [s.sb(f"sc{u}", [P, SEQ]) for u in range(3)], [s.sb(f"p{u}", [P, SEQ]) for u in range(3)]
        pT = [s.sb(f"pT{u}", [P, SEQ]) for u in range(2)]
        m, nm, sums, rinv = (s.sb(n, [P, NU]) for n in ("m", "nm", "sums", "rinv"))
        y = s.sb("y", [P, 2, P])
        banks = [s.ps(f"bank{n}") for n in range(8)]
        proj, qk_ps, pT_ps = banks[0:4], banks[4:6], banks[6:8]
        s_ps, o_ps, yT_ps = banks[0:2], banks[2:4], banks[4:6]
        w_in, f_in, const_in = s.sem("w_in"), s.sem("f_in"), s.sem("const_in")
        (consts_ready, proj_ready, squares_ready, means_ready, rstd_ready, qk_normed, qk_turned, qk_stored,
         bias_ready, scores_ready, max_ready, exp_ready, pT_ready, pT_stored, pv_ready, y_ready, y_turned,
         yT_stored) = (s.sem(n) for n in (
             "consts_ready", "proj_ready", "squares_ready", "means_ready", "rstd_ready", "qk_normed", "qk_turned",
             "qk_stored", "bias_ready", "scores_ready", "max_ready", "exp_ready", "pT_ready", "pT_stored", "pv_ready",
             "y_ready", "y_turned", "yT_stored"))

        def n_keys(t):
            return (t + 1) * P

        with nc.Block() as block:
            @block.sync
            def _(sp):
                for dst, src in ((qw, "q_norm_w_2"), (kw, "k_norm_w_2")):
                    for h in range(2):
                        sp.dma_start(dst[h * HD:(h + 1) * HD, :], a[src].rearrange("a d -> d a")).then_inc(const_in, 16)
                sp.dma_start(mask[:, :], a["causal"]).then_inc(const_in, 16)
                src = a["w_in_2"][0].rearrange("(k p) n -> p k n", p=P)

                def load(pair):
                    for x in range(3):
                        sp.dma_start(w[:, :, x, :], src[:, :, bass.ds(pair * P + (1536 + x * 512), P)])\
                            .then_inc(w_in, 16)
                    for h in range(2):
                        sp.dma_start(fb[h][:, :], f_rows[bass.ds(pair * 2 + h, 1), :].to_broadcast([P, SEQ]))\
                            .then_inc(f_in, 16)

                load(0)
                with sp.Fori(0, PAIRS - 1) as i:
                    sp.wait_ge(proj_ready, i * LT + LT)
                    sp.sem_inc(k["apart"], 1)
                    sp.wait_ge(bias_ready, i + 1)
                    sp.sem_inc(k["apart"], 1)
                    load(i + 1)

            @block.tensor
            def _(pe):
                pe.wait_ge(const_in, 16 * 5)
                with pe.Fori(0, PAIRS) as i:
                    def turn_qk(j):
                        pe.wait_ge(qk_normed, i * LT + (j + 1))
                        if j >= 2:
                            pe.wait_ge(qk_stored, i * LT + (j - 1))
                        for b in range(2):
                            tr = pe.transpose(qk_ps[j % 2][:, b * P:(b + 1) * P],
                                              qkn[j % 2][:, 2 * b:2 * b + 2, :], k["ident"][:, :])
                        tr.then_inc(qk_turned, 1)

                    pe.wait_ge(w_in, i * 48 + 48)
                    for j in range(LT):
                        for kk in range(KD):
                            mm = pe.matmul(proj[j][:, 0:384], k["hT"][:, kk, j * P:(j + 1) * P], w[:, kk, :, :],
                                           start=kk == 0, stop=kk == KD - 1)
                        mm.then_inc(proj_ready, 1)
                        if j >= 1:
                            turn_qk(j - 1)
                    turn_qk(LT - 1)
                    pe.wait_ge(qk_stored, i * LT + LT)
                    for n in range(NU + 4):
                        if n < NU:
                            t, h = units[n]
                            hs = slice(h * HD, (h + 1) * HD)
                            if n >= 2:
                                pe.wait_ge(max_ready, i * NU + (n - 1))
                            pe.matmul(s_ps[n % 2][:, 0:n_keys(t)], qT[hs, t * P:(t + 1) * P], kT[hs, 0:n_keys(t)],
                                      start=True, stop=True).then_inc(scores_ready, 1)
                        if 2 <= n < NU + 2:
                            x = n - 2
                            pe.wait_ge(exp_ready, i * NU + (x + 1))
                            if x >= 2:
                                pe.wait_ge(pT_stored, i * NU + (x - 1))
                            for b in range(units[x][0] + 1):
                                tr = pe.transpose(pT_ps[x % 2][:, b * P:(b + 1) * P], p[x % 3][:, b * P:(b + 1) * P],
                                                  k["ident"][:, :])
                            tr.then_inc(pT_ready, 1)
                        if 3 <= n < NU + 3:
                            x = n - 3
                            t, h = units[x]
                            pe.wait_ge(pT_stored, i * NU + (x + 1))
                            if x >= 2:
                                pe.wait_ge(y_ready, i * NU + (x - 1))
                            for b in range(t + 1):
                                mm = pe.matmul(o_ps[x % 2][:, 0:HD], pT[x % 2][:, b * P:(b + 1) * P],
                                               v[:, b, h * HD:(h + 1) * HD], start=b == 0, stop=b == t)
                            mm.then_inc(pv_ready, 1)
                        if n >= 5 and n % 2 == 1:
                            t = (n - 5) // 2
                            pe.wait_ge(y_ready, i * NU + (2 * t + 2))
                            if t >= 2:
                                pe.wait_ge(yT_stored, i * LT + (t - 1))
                            pe.transpose(yT_ps[t % 2][:, 0:P], y[:, t % 2, :], k["ident"][:, :]).then_inc(y_turned, 1)

            @block.scalar
            def _(act):
                act.wait_ge(consts_ready, 1)
                with act.Fori(0, PAIRS) as i:
                    def store_qk(j):
                        act.wait_ge(qk_turned, i * LT + (j + 1))
                        act.activation(qT[:, j * P:(j + 1) * P], qk_ps[j % 2][:, 0:P], ACT.Copy, scale=qw[:, 0:1])
                        act.activation(kT[:, j * P:(j + 1) * P], qk_ps[j % 2][:, P:2 * P], ACT.Copy, scale=kw[:, 0:1])\
                            .then_inc(qk_stored, 1)

                    def store_y(t):
                        act.wait_ge(y_turned, i * LT + (t + 1))
                        act.sem_inc(k["apart"], 1)
                        act.activation(ybT[:, bass.ds(i, 1), t * P:(t + 1) * P].squeeze(1), yT_ps[t % 2][:, 0:P], ACT.Copy)\
                            .then_inc(yT_stored, 1)

                    for j in range(LT):
                        act.wait_ge(proj_ready, i * LT + (j + 1))
                        if j >= 1:
                            act.wait_ge(qk_normed, i * LT + j)
                        act.activation(v[:, j, :], proj[j][:, 256:384], ACT.Copy)
                        act.activation(squares[:, :, :], proj[j][:, 0:256].rearrange("p (h d) -> p h d", d=HD),
                                       ACT.Square).then_inc(squares_ready, 1)
                        if j >= 1:
                            store_qk(j - 1)
                    store_qk(LT - 1)
                    for n in range(NU + 3):
                        if n < NU:
                            nk = n_keys(units[n][0])
                            act.wait_ge(max_ready, i * NU + (n + 1))
                            if n >= 3:
                                act.wait_ge(pT_ready, i * NU + (n - 2))
                            act.activation(p[n % 3][:, 0:nk], sc[n % 3][:, 0:nk], ACT.Exp, bias=nm[:, n:n + 1],
                                           accum_out=sums[:, n:n + 1]).then_inc(exp_ready, 1)
                        if 2 <= n < NU + 2:
                            x = n - 2
                            nk = n_keys(units[x][0])
                            act.wait_ge(pT_ready, i * NU + (x + 1))
                            if x >= 2:
                                act.wait_ge(pv_ready, i * NU + (x - 1))
                            act.activation(pT[x % 2][:, 0:nk], pT_ps[x % 2][:, 0:nk], ACT.Copy).then_inc(pT_stored, 1)
                        if n >= 7 and n % 2 == 1:
                            store_y((n - 7) // 2)
                    for t in range((NU + 2 - 7) // 2 + 1, LT):
                        store_y(t)

            @block.gpsimd
            def _(pool):
                pool.memset(half[:, :], -0.5)
                pool.drain()
                pool.wait_ge(const_in, 16 * 5)
                with pool.Fori(0, PAIRS) as i:
                    for j in range(LT):
                        pool.wait_ge(means_ready, i * LT + (j + 1))
                        pool.tensor_tensor(rstd[:, :], ms[:, :], half[:, :], ALU.pow).then_inc(rstd_ready, 1)
                    pool.wait_ge(f_in, i * 32 + 32)
                    pool.sem_inc(k["apart"], 1)
                    for h in range(2):
                        for t in range(LT):
                            at = slice(OFF[t] * P, OFF[t] * P + n_keys(t))
                            pool.tensor_tensor(bias[:, h, at], mask[:, at], fb[h][:, 0:n_keys(t)], ALU.add)
                    pool.drain().then_inc(bias_ready, 1)

            @block.vector
            def _(dve):
                dve.wait_ge(const_in, 16 * 5)
                dve.tensor_scalar(qw[:, :], qw[:, :], HD ** -0.5, None, ALU.mult).then_inc(consts_ready, 1)
                with dve.Fori(0, PAIRS) as i:
                    for j in range(LT):
                        dve.wait_ge(squares_ready, i * LT + (j + 1))
                        dve.tensor_reduce(ss[:, :], squares[:, :, :], AX_X, ALU.add)
                        dve.drain()
                        dve.tensor_scalar(ms[:, :], ss[:, :], 1.0 / HD, EPS, ALU.mult, ALU.add).then_inc(means_ready, 1)
                        dve.wait_ge(rstd_ready, i * LT + (j + 1))
                        if j >= 2:
                            dve.wait_ge(qk_turned, i * LT + (j - 1))
                        dve.tensor_tensor(qkn[j % 2][:, :, :], proj[j][:, 0:256].rearrange("p (h d) -> p h d", d=HD),
                                          rstd[:, :].unsqueeze(2).to_broadcast([P, 4, HD]), ALU.mult)\
                            .then_inc(qk_normed, 1)
                    dve.wait_ge(bias_ready, i + 1)
                    dve.sem_inc(k["apart"], 1)
                    for n in range(NU + 3):
                        if n >= 3:
                            x = n - 3
                            dve.wait_ge(exp_ready, i * NU + (x + 1))
                            dve.reciprocal(rinv[:, x:x + 1], sums[:, x:x + 1])
                        if n < NU:
                            t, h = units[n]
                            nk = n_keys(t)
                            dve.wait_ge(scores_ready, i * NU + (n + 1))
                            dve.sem_inc(k["apart"], 1)
                            dve.tensor_tensor_reduce(sc[n % 3][:, 0:nk], s_ps[n % 2][:, 0:nk],
                                                     bias[:, h, OFF[t] * P:OFF[t] * P + nk], 1.0, -3e38,
                                                     ALU.add, ALU.max, m[:, n:n + 1])
                        dve.drain()
                        if n < NU:
                            dve.tensor_scalar(nm[:, n:n + 1], m[:, n:n + 1], -1.0, None, ALU.mult).then_inc(max_ready, 1)
                        if n >= 3:
                            t, h = units[x]
                            dve.wait_ge(pv_ready, i * NU + (x + 1))
                            if t >= 2 and h == 0:
                                dve.wait_ge(y_turned, i * LT + (t - 1))
                            dve.tensor_scalar(y[:, t % 2, h * HD:(h + 1) * HD], o_ps[x % 2][:, 0:HD], rinv[:, x:x + 1],
                                              None, ALU.mult).then_inc(y_ready, 1)


def stage_merge(nc, a, k, yaT, ybT, mergedT):
    with Stage(nc, "merge") as s:
        wg = [s.sb(f"wg{n}", [P, 2, KD, P]) for n in range(2)]
        wo = [s.sb(f"wo{n}", [P, 2, 4, P]) for n in range(2)]
        e, r = s.sb("e", [P, 2, SEQ]), s.sb("r", [P, 2, SEQ])
        t = s.sb("t", [P, 2, SEQ])
        ps = [[s.ps(f"{n}{h}") for n in ("gc", "ga", "pa", "pb")] for h in range(2)]
        w_in = [s.sem(f"w_in{n}") for n in range(2)]
        gates_ready, products_ready, exp_ready, e_read, merged = (
            s.sem(n) for n in ("gates_ready", "products_ready", "exp_ready", "e_read", "merged"))
        with nc.Block() as block:
            @block.sync
            def _(sp):
                src = a["w_in_2"][0].rearrange("(k p) n -> p k n", p=P)
                outs = [a[n][0].rearrange("(k p) n -> p k n", p=P) for n in ("w_out_conv_2", "w_out_attn_2")]

                def load(n, chunk):
                    for x in range(2):
                        sp.dma_start(wg[n][:, x, :, :], src[:, :, bass.ds(chunk * P + (3080 + x * D), P)])\
                            .then_inc(w_in[n], 16)
                        sp.dma_start(wo[n][:, x, :, :], outs[x][:, :, bass.ds(chunk * P, P)]).then_inc(w_in[n], 16)

                for n in range(2):
                    load(n, n)
                with sp.Fori(0, KD // 2 - 1) as i:
                    for n in range(2):
                        sp.wait_ge(products_ready, i * 2 + (n + 1))
                        load(n, i * 2 + (n + 2))

            @block.tensor
            def _(pe):
                with pe.Fori(0, KD // 2) as i:
                    for n in range(2):
                        pe.wait_ge(w_in[n], i * 64 + 64)
                        pe.wait_ge(merged, i * 2 + (n + 1))
                        for x in range(2):
                            for kk in range(KD):
                                mm = pe.matmul(ps[n][x][:, :], wg[n][:, x, kk, :], k["hT"][:, kk, 0:SEQ],
                                               start=kk == 0, stop=kk == KD - 1)
                        mm.then_inc(gates_ready, 1)
                        for x, yy in enumerate((yaT, ybT)):
                            for kk in range(4):
                                mm = pe.matmul(ps[n][2 + x][:, :], wo[n][:, x, kk, :], yy[:, kk, 0:SEQ],
                                               start=kk == 0, stop=kk == 3)
                        mm.then_inc(products_ready, 1)

            @block.scalar
            def _(act):
                with act.Fori(0, KD // 2) as i:
                    for n in range(2):
                        act.wait_ge(gates_ready, i * 2 + (n + 1))
                        act.wait_ge(e_read, i * 2 + (n + 1))
                        act.activation(e[:, 0, :], ps[n][0][:, :], ACT.Exp, scale=-1.0)
                        act.activation(e[:, 1, :], ps[n][1][:, :], ACT.Exp, scale=-1.0).then_inc(exp_ready, 1)

            @block.vector
            def _(dve):
                dve.drain().then_inc(merged, 1)
                dve.drain().then_inc(merged, 1)
                dve.drain().then_inc(e_read, 1)
                with dve.Fori(0, KD // 2) as i:
                    for n in range(2):
                        dve.wait_ge(exp_ready, i * 2 + (n + 1))
                        dve.tensor_scalar(r[:, :, :], e[:, :, :], 1.0, None, ALU.add).then_inc(e_read, 1)
                        dve.drain()
                        dve.reciprocal(r[:, :, :], r[:, :, :])
                        dve.drain()
                        dve.wait_ge(products_ready, i * 2 + (n + 1))
                        for x in range(2):
                            dve.tensor_tensor(t[:, x, :], ps[n][2 + x][:, :], r[:, x, :], ALU.mult)
                        dve.drain()
                        dve.tensor_tensor(mergedT[:, bass.ds(i * 2 + n, 1), 0:SEQ].squeeze(1), t[:, 0, :], t[:, 1, :],
                                          ALU.add).then_inc(merged, 1)


def stage_router(nc, a, k, comb):
    NG, EG = 4, 8
    NL = NG + NE
    with Stage(nc, "router") as s:
        w, bias = s.sb("w", [P, KD, NL]), s.sb("bias", [P, NL])
        lg, le = s.sb("lg", [P, LT, NG]), s.sb("le", [P, LT, NG, EG])
        picked = s.sb("picked", [P, LT, NG, EG])
        ex_g, leg, leg2 = s.sb("ex_g", [P, LT, NG]), s.sb("leg", [P, LT, EG]), s.sb("leg2", [P, LT, EG])
        iota = s.sb("iota", [P, EG])
        val, low = s.sb("val", [P, LT, EG]), s.sb("low", [P, LT])
        sel, first, second = s.sb("sel", [P, LT, NG]), s.sb("first", [P, LT, EG]), s.sb("second", [P, LT, EG])
        mg, v1, v2, dv, ex, sg, rg, w1, w2 = (s.sb(n, [P, LT]) for n in ("mg", "v1", "v2", "dv", "ex", "sg", "rg",
                                                                         "w1", "w2"))
        t0, t1 = s.sb("t0", [P, LT, EG]), s.sb("t1", [P, LT, EG])
        ps = s.ps("ps")
        w_in, bias_in, products_ready = s.sem("w_in"), s.sem("bias_in"), s.sem("products_ready")
        diff_ready, exp_ready, group_ready, group_exp = (
            s.sem(n) for n in ("diff_ready", "exp_ready", "group_ready", "group_exp"))
        with nc.Block() as block:
            @block.sync
            def _(sp):
                for src, c0, n in (("w_router_group_2", 0, NG), ("w_router_expert_2", NG, NE)):
                    sp.dma_start(w[:, :, c0:c0 + n], a[src][0].rearrange("(k p) n -> p k n", p=P)).then_inc(w_in, 16)
                for src, c0, n in (("b_router_group_2", 0, NG), ("b_router_expert_2", NG, NE)):
                    sp.dma_start(bias[:, c0:c0 + n], a[src].to_broadcast([P, n])).then_inc(bias_in, 16)
                sp.dma_start(iota[:, :], a["iota8"]).then_inc(bias_in, 16)

            @block.tensor
            def _(pe):
                pe.wait_ge(w_in, 32)
                for j in range(LT):
                    for kk in range(KD):
                        mm = pe.matmul(ps[:, j * 64:j * 64 + NL], k["hT"][:, kk, j * P:(j + 1) * P], w[:, kk, :],
                                       start=kk == 0, stop=kk == KD - 1)
                mm.then_inc(products_ready, 1)

            @block.scalar
            def _(act):
                act.wait_ge(group_ready, 1)
                act.activation(ex_g[:, :, :], ex_g[:, :, :], ACT.Exp).then_inc(group_exp, 1)
                act.wait_ge(diff_ready, 1)
                act.activation(ex[:, :], dv[:, :], ACT.Exp).then_inc(exp_ready, 1)

            @block.vector
            def _(dve):
                def bc(x, n):
                    return x[:, :].unsqueeze(2).to_broadcast([P, LT, n])

                def pick_first(out, x, top, n):
                    dve.tensor_tensor(out[:, :, :], x[:, :, :], bc(top, n), ALU.is_equal)
                    dve.drain()
                    dve.scalar_tensor_tensor(out=val[:, :, 0:n], in0=out[:, :, :], scalar=-100.0,
                                             in1=iota[:, 0:n].unsqueeze(1).to_broadcast([P, LT, n]),
                                             op0=ALU.mult, op1=ALU.add)
                    dve.drain()
                    dve.tensor_reduce(low[:, :], val[:, :, 0:n], AX_X, ALU.min)
                    dve.drain()
                    dve.tensor_tensor(out[:, :, :], val[:, :, 0:n], bc(low, n), ALU.is_equal)
                    dve.drain()

                dve.wait_ge(bias_in, 48)
                dve.wait_ge(products_ready, 1)
                logits = ps[:, 0:LT * 64].rearrange("p (t n) -> p t n", t=LT)
                dve.tensor_tensor(lg[:, :, :], logits[:, :, 0:NG],
                                  bias[:, 0:NG].unsqueeze(1).to_broadcast([P, LT, NG]), ALU.add)
                for t in range(LT):
                    dve.tensor_tensor(le[:, t, :, :].rearrange("p g e -> p (g e)"), logits[:, t, NG:NL],
                                      bias[:, NG:NL], ALU.add)
                dve.drain()
                dve.tensor_reduce(mg[:, :], lg[:, :, :], AX_X, ALU.max)
                dve.drain()
                dve.tensor_tensor(ex_g[:, :, :], lg[:, :, :], bc(mg, NG), ALU.subtract).then_inc(group_ready, 1)
                pick_first(sel, lg, mg, NG)
                for t in range(LT):
                    dve.tensor_tensor(picked[:, t, :, :], le[:, t, :, :],
                                      sel[:, t, :].unsqueeze(2).to_broadcast([P, NG, EG]), ALU.mult)
                dve.drain()
                for t in range(LT):
                    dve.tensor_reduce(leg[:, t, :], picked[:, t, :, :].rearrange("p g e -> p e g"), AX_X, ALU.add)
                dve.drain()
                dve.tensor_reduce(v1[:, :], leg[:, :, :], AX_X, ALU.max)
                dve.drain()
                pick_first(first, leg, v1, EG)
                dve.scalar_tensor_tensor(out=leg2[:, :, :], in0=first[:, :, :], scalar=NEG, in1=leg[:, :, :],
                                         op0=ALU.mult, op1=ALU.add)
                dve.drain()
                dve.tensor_reduce(v2[:, :], leg2[:, :, :], AX_X, ALU.max)
                dve.drain()
                dve.tensor_tensor(dv[:, :], v2[:, :], v1[:, :], ALU.subtract).then_inc(diff_ready, 1)
                pick_first(second, leg2, v2, EG)
                dve.wait_ge(group_exp, 1)
                dve.tensor_reduce(sg[:, :], ex_g[:, :, :], AX_X, ALU.add)
                dve.wait_ge(exp_ready, 1)
                dve.tensor_scalar(w1[:, :], ex[:, :], 1.0, None, ALU.add)
                dve.drain()
                dve.reciprocal(rg[:, :], sg[:, :])
                dve.reciprocal(w2[:, :], w1[:, :])
                dve.drain()
                dve.tensor_tensor(w1[:, :], w2[:, :], rg[:, :], ALU.mult)
                dve.drain()
                dve.tensor_tensor(w2[:, :], w1[:, :], ex[:, :], ALU.mult)
                dve.tensor_tensor(t0[:, :, :], first[:, :, :], bc(w1, EG), ALU.mult)
                dve.drain()
                dve.tensor_tensor(t1[:, :, :], second[:, :, :], bc(w2, EG), ALU.mult)
                dve.drain()
                dve.tensor_tensor(leg[:, :, :], t0[:, :, :], t1[:, :, :], ALU.add)
                dve.drain()
                for t in range(LT):
                    dve.tensor_tensor(comb[:, t, :].rearrange("p (g e) -> p g e", g=NG),
                                      leg[:, t, :].unsqueeze(1).to_broadcast([P, NG, EG]),
                                      sel[:, t, :].unsqueeze(2).to_broadcast([P, NG, EG]), ALU.mult)


def stage_moe(nc, a, k, comb):
    FC = DE // P
    with Stage(nc, "moe") as s:
        wgu = [s.sb(f"wgu{n}", [P, 2, KD, DE]) for n in range(2)]
        wd = [s.sb(f"wd{n}", [P, FC, D]) for n in range(2)]
        e, r = s.sb("e", [P, FC, SEQ]), s.sb("r", [P, FC, SEQ])
        aT = [s.sb(f"aT{n}", [P, FC, SEQ]) for n in range(2)]
        acc, gate, ones, diag = s.sb("acc", [P, LT, D]), s.sb("gate", [P, D]), s.sb("ones", [P, P]), s.sb("diag", [P, KD, P])
        gu = [[s.ps(f"{n}{f}") for f in range(FC)] for n in ("g", "u")]
        down = [s.ps(f"down{n}") for n in range(4)]
        gu_in, d_in = [s.sem(f"gu_in{n}") for n in range(2)], [s.sem(f"d_in{n}") for n in range(2)]
        (diag_ready, spread, gate_ready, gu_ready, exp_ready, a_ready, down_ready, added, out_ready, out_saved) = (
            s.sem(n) for n in ("diag_ready", "spread", "gate_ready", "gu_ready", "exp_ready", "a_ready", "down_ready",
                               "added", "out_ready", "out_saved"))
        ND = LT * 2
        with nc.Block() as block:
            @block.sync
            def _(sp):
                def load_gu(n, x):
                    for y, name in enumerate(("w_gate_2", "w_up_2")):
                        sp.dma_start(wgu[n][:, y, :, :],
                                     a[name][0, bass.ds(x, 1), :, :].squeeze(0).rearrange("(k p) n -> p k n", p=P))\
                            .then_inc(gu_in[n], 16)

                def load_d(n, x):
                    sp.dma_start(wd[n][:, :, :],
                                 a["w_down_2"][0, bass.ds(x, 1), :, :].squeeze(0).rearrange("(k p) n -> p k n", p=P))\
                        .then_inc(d_in[n], 16)

                for n in range(2):
                    load_gu(n, n)
                    load_d(n, n)
                with sp.Fori(0, NE // 2 - 1) as i:
                    for n in range(2):
                        sp.wait_ge(gu_ready, i * 2 + (n + 1))
                        load_gu(n, i * 2 + (n + 2))
                        sp.wait_ge(down_ready, i * (2 * ND) + (n + 1) * ND)
                        load_d(n, i * 2 + (n + 2))
                for t in range(LT):
                    sp.wait_ge(out_ready, t + 1)
                    sp.dma_start(a["out"][0, t * P:(t + 1) * P, :], acc[:, t, :]).then_inc(out_saved, 16)
                sp.wait_ge(out_saved, 16 * LT)

            @block.tensor
            def _(pe):
                pe.wait_ge(diag_ready, 1)
                for h in range(2):
                    mm = pe.matmul(down[h][:, :], ones[:, :], diag[:, h * 4:h * 4 + 4, :], start=True, stop=True)
                mm.then_inc(spread, 1)

                def gate_up(n, i):
                    pe.wait_ge(gu_in[n], i * 32 + 32)
                    pe.wait_ge(a_ready, i * 2 + (n + 1))
                    for y in range(2):
                        for f in range(FC):
                            for kk in range(KD):
                                mm = pe.matmul(gu[y][f][:, :], wgu[n][:, y, kk, f * P:(f + 1) * P],
                                               k["hT"][:, kk, 0:SEQ], start=kk == 0, stop=kk == KD - 1)
                    mm.then_inc(gu_ready, 1)

                def project_down(n, i, count):
                    pe.wait_ge(d_in[n], i * 16 + 16)
                    pe.wait_ge(a_ready, i * 2 + (n + 2))
                    for x in range(ND):
                        pe.wait_ge(added, i * (2 * ND) + (n * ND + x + 1))
                        t, h = x // 2, x % 2
                        for f in range(FC):
                            mm = pe.matmul(down[x % 4][:, :], aT[n][:, f, t * P:(t + 1) * P],
                                           wd[n][:, f, h * 512:(h + 1) * 512], start=f == 0, stop=f == FC - 1)
                        mm.then_inc(down_ready, 1)

                pe.wait_ge(gate_ready, 1)
                gate_up(0, 0)
                with pe.Fori(0, NE // 2 - 1) as i:
                    gate_up(1, i)
                    project_down(0, i, 0)
                    gate_up(0, i + 1)
                    project_down(1, i, 0)
                gate_up(1, NE // 2 - 1)
                project_down(0, NE // 2 - 1, 0)
                project_down(1, NE // 2 - 1, 0)

            @block.scalar
            def _(act):
                with act.Fori(0, NE) as i:
                    act.wait_ge(gu_ready, i + 1)
                    for f in range(FC):
                        ex = act.activation(e[:, f, :], gu[0][f][:, :], ACT.Silu)
                    ex.then_inc(exp_ready, 1)

            @block.vector
            def _(dve):
                dve.memset(ones[:, :], 1.0)
                dve.memset(acc[:, :, :], 0.0)
                dve.tensor_tensor(diag[:, :, :], k["ident"][:, :].unsqueeze(1).to_broadcast([P, KD, P]),
                                  k["modT"][:, MOD_B2 + 40:MOD_B2 + 48, 2:3].to_broadcast([P, KD, P]), ALU.mult)
                dve.drain().then_inc(diag_ready, 1)
                dve.wait_ge(spread, 1)
                for h in range(2):
                    dve.tensor_copy(gate[:, h * 512:(h + 1) * 512], down[h][:, :])
                dve.drain().then_inc(gate_ready, 1)
                dve.drain().then_inc(a_ready, 1)
                for _ in range(4):
                    dve.drain().then_inc(added, 1)

                def activations(n, i):
                    dve.wait_ge(exp_ready, i * 2 + (n + 1))
                    for f in range(FC):
                        tt = dve.tensor_tensor(aT[n][:, f, :], e[:, f, :], gu[1][f][:, :], ALU.mult)
                    tt.then_inc(a_ready, 1)

                def add(n, i):
                    for x in range(ND):
                        t, h = x // 2, x % 2
                        at = acc[:, t, h * 512:(h + 1) * 512]
                        dve.wait_ge(down_ready, i * (2 * ND) + (n * ND + x + 1))
                        dve.scalar_tensor_tensor(out=at, in0=down[x % 4][:, :], scalar=comb[:, t, bass.ds(i * 2 + n, 1)],
                                                 in1=at, op0=ALU.mult, op1=ALU.add).then_inc(added, 1)
                    dve.drain()

                activations(0, 0)
                with dve.Fori(0, NE // 2 - 1) as i:
                    activations(1, i)
                    add(0, i)
                    activations(0, i + 1)
                    add(1, i)
                activations(1, NE // 2 - 1)
                add(0, NE // 2 - 1)
                add(1, NE // 2 - 1)
                for t in range(LT):
                    dve.tensor_tensor(acc[:, t, :], acc[:, t, :], gate[:, :], ALU.mult)
                dve.drain()
                for t in range(LT):
                    dve.tensor_tensor(acc[:, t, :], acc[:, t, :], k["xs"][:, t, :], ALU.add).then_inc(out_ready, 1)


def stages(nc, a, k):
    norm = lambda name, groups: stage_norm(nc, k, name, groups, k["xs"], k["hT"])
    y_tile = lambda c, j: k["yT"][:, c, j * P:(j + 1) * P]
    comb = k["yT"][:, 0:LT, 0:NE]
    return [
        lambda: stage_setup(nc, a, k),
        lambda: stage_modulations(nc, a, k),
        lambda: norm("norm_a", [(0, LT, ROW["norm_w"], MOD_L0, 0), (LT, CT, ROW["norm_w"], MOD_L0, 1)]),
        lambda: stage_attention_a(nc, a, k, k["yT"]),
        lambda: stage_gates(nc, a, k),
        lambda: stage_mlstm(nc, a, k, k["yT"]),
        lambda: stage_output(nc, k, "out_a", y_tile, a["w_out_ab"][0], INNER // P, range(NT),
                             [(MOD_L0 + 16, 0, 0, LT), (MOD_L0 + 16, 1, LT, CT)]),
        lambda: norm("norm_c", [(0, LT, ROW["norm_w"] + KD, MOD_L1, 0), (LT, CT, ROW["norm_w"] + KD, MOD_L1, 1)]),
        lambda: stage_gla(nc, a, k, k["yT"]),
        lambda: stage_output(nc, k, "out_c", y_tile, a["w_out_c"][0], INNER // P, range(LT),
                             [(MOD_L1 + 16, 0, 0, LT)]),
        lambda: norm("norm_1", [(0, LT, ROW["norm1_w_2"], MOD_B2, 2)]),
        lambda: stage_conv(nc, a, k, k["yT"][:, 0:4, :], k["f_rows"]),
        lambda: stage_attention_2(nc, a, k, k["yT"][:, 4:8, :], k["f_rows"]),
        lambda: stage_merge(nc, a, k, k["yT"][:, 0:4, :], k["yT"][:, 4:8, :], k["yT"][:, 8:16, :]),
        lambda: stage_output(nc, k, "out_2", lambda c, j: y_tile(8 + c, j), a["w_o_2"][0], KD, range(LT),
                             [(MOD_B2 + 16, 2, 0, LT)]),
        lambda: norm("norm_2", [(0, LT, ROW["norm2_w_2"], MOD_B2 + 24, 2)]),
        lambda: stage_router(nc, a, k, comb),
        lambda: stage_moe(nc, a, k, comb),
    ]


def constants():
    f = np.float32
    c = {"ident": np.eye(P, dtype=f), "flip": np.ascontiguousarray(np.eye(P, dtype=f)[::-1])}
    col = np.arange(GRID_W)
    start = np.clip(col - WIN_W // 2, 0, GRID_W - WIN_W)
    kinds = []
    for t in (0, 1, 3):
        keys = range(max(0, t - 1), min(LT, t + 2))
        m = np.zeros((GRID_H, COLS, len(keys), GRID_H, COLS), f)
        for ci in range(COLS):
            q = COLS * t + ci
            for n, kt in enumerate(keys):
                kc = COLS * kt + np.arange(COLS)
                ok = (kc >= start[q]) & (kc < start[q] + WIN_W)
                m[:, ci, n, :, ~ok] = NEG
        kinds.append(m.reshape(P, -1))
    c["na_mask"] = np.concatenate(kinds, axis=1)
    freqs = (f(10000.0) ** (-np.arange(64, dtype=f) / f(64))).astype(f)
    t = np.arange(SEQ)
    ang = np.stack([(t // GRID_W).astype(f)[:, None] * freqs, (t % GRID_W).astype(f)[:, None] * freqs], axis=1)
    tiles = ang.reshape(LT, P, 2, 64).transpose(1, 0, 2, 3)
    c["rope_cos"] = np.cos(tiles).astype(f)
    c["rope_sin"] = np.sin(tiles).astype(f)
    i = np.arange(P)
    c["tri"] = np.stack([np.where(i[None] > i[:, None], NEG, 0), np.where(i[None] < i[:, None], NEG, 0)], axis=1).astype(f)
    d = i[:, None] ^ i[None]
    c["level_masks"] = np.stack([(d >= w) & (d < 2 * w) for w in HG_LEVELS if w < P], axis=1).astype(np.int32)
    c["causal"] = np.concatenate([np.where(np.arange((n + 1) * P)[None] > n * P + i[:, None], NEG, 0)
                                  for n in range(LT)], axis=1).astype(f)
    c["iota8"] = np.tile(np.arange(8, dtype=f), (P, 1))
    return c


def program(nc, a):
    with ExitStack() as ctx:
        def sb(name, shape, dt=F32):
            return ctx.enter_context(nc.sbuf_tensor(name, shape, dt))

        k = {"xs": sb("xs", [P, NT, D]), "hT": sb("hT", [P, KD, NTOK]), "ident": sb("ident", [P, P]),
             "vecT": sb("vecT", [P, NVEC]), "biasT": sb("biasT", [P, NMOD]), "modT": sb("modT", [P, NMOD, 3]),
             "silu_c": sb("silu_c", [P, KD, 3]), "lbT": sb("lbT", [P, 2, HG_HEADS]),
             "yT": sb("yT", [P, INNER // P, NTOK]),
             "m_cols": sb("m_cols", [P, NT, 4, ML_HEADS]),
             "a_rows": nc.dram_tensor("a_rows", (2, ML_HEADS, NTOK), F32, kind="Internal").ap(),
             "f_rows": nc.dram_tensor("f_rows", (8, SEQ), F32, kind="Internal").ap(),
             "rpb_pad": nc.dram_tensor("rpb_pad", (16, RPB_H, RPB_PAD), F32, kind="Internal").ap(),
             "apart": ctx.enter_context(nc.semaphore("apart"))}
        for stage in stages(nc, a, k):
            stage()



_INS = ["x", "c", "ctx", "c_ctx", "norm_w", "w_ada", "b_ada", "w_in_ab", "b_gate_ab", "q_norm_a", "k_norm_a", "rpb_a",
        "h_norm_b", "w_out_ab", "w_in_c", "lb_c", "h_norm_c", "w_out_c", "c_2", "w_ada_2", "b_ada_2", "norm1_w_2",
        "w_in_2", "b_forget_2", "conv_w_2", "q_norm_w_2", "k_norm_w_2", "w_out_conv_2", "w_out_attn_2", "w_o_2",
        "norm2_w_2", "w_router_group_2", "b_router_group_2", "w_router_expert_2", "b_router_expert_2",
        "w_gate_2", "w_up_2", "w_down_2"]


def kernel(**inputs):
    import numpy as _np
    import concourse.bacc as _bacc
    from concourse import mybir as _mybir
    from concourse.bass_utils import run_bass_kernel_spmd as _run

    nc = _bacc.Bacc("TRN2", target_bir_lowering=False, num_devices=1)
    arrays = {n: _np.ascontiguousarray(inputs[n]) for n in _INS}
    arrays |= constants()
    a = {n: nc.dram_tensor(f"in_{n}", v.shape, _mybir.dt.from_np(v.dtype), kind="ExternalInput").ap()
         for n, v in arrays.items()}
    a["out"] = nc.dram_tensor("out_x", (1, SEQ, D), F32, kind="ExternalOutput").ap()
    program(nc, a)
    r = _run(nc, [{f"in_{n}": v for n, v in arrays.items()}], core_ids=[0])
    return r.results[0]["out_x"]
```

```python
from contextlib import ExitStack

import numpy as np

import concourse.bass as bass
from concourse import mybir

F32 = mybir.dt.float32
I32 = mybir.dt.int32
U32 = mybir.dt.uint32
ALU = mybir.AluOpType
ACT = mybir.ActivationFunctionType
AX_X = mybir.AxisListType.X

P = 128
D = 1024
KD = D // P
SEQ, CTX = 512, 256
LT, CT = SEQ // P, CTX // P
NT = LT + CT
NTOK = SEQ + CTX
EPS = 1e-6
NEG = -1e30

GRID_W, GRID_H = 64, SEQ // 64
COLS = P // GRID_H
WIN_W = 16
NA_PAIRS = 8
NA_SCALE = 64 ** -0.5
RPB_H, RPB_W = 15, 31
RPB_PAD = 64
UK = 3 * COLS

ML_HEADS, ML_DIM = 4, 256
HG_HEADS = 16
HG_LEVELS = [1, 2, 4, 8, 16, 32, 64, 128, 256]
INNER = 2048
NE, DE = 32, 256
BLOCKS = (2 * SEQ + NE * (P - 1)) // P
BLOCKS += BLOCKS % 2

VECTORS = [("c", 8), ("c_ctx", 8), ("c_2", 8), ("norm_w", 16), ("norm1_w_2", 8), ("norm2_w_2", 8),
           ("h_norm_b", 8), ("h_norm_c", 16), ("lb_c", 32),
           ("conv_w_2", 12)]
ROW = {}
for _name, _n in VECTORS:
    ROW[_name] = sum(n for k, n in VECTORS if k in ROW)
    assert _n <= 32
NVEC = sum(n for _, n in VECTORS)
MOD_L0, MOD_L1, MOD_B2, NMOD = 0, 24, 48, 96


def rows128(ap):
    names = " ".join("abcd"[:len(ap.shape)])
    flat = ap.rearrange(f"{names} -> ({names})") if len(ap.shape) > 1 else ap
    return flat.rearrange("(n p) -> n p", p=P)


class Stage:

    def __init__(self, nc, name):
        self.nc, self.name, self.stack, self.sems = nc, name, ExitStack(), []

    def __enter__(self):
        self.stack.__enter__()
        return self

    def __exit__(self, *e):
        self.nc.clear_and_free_semaphores(self.sems)
        self.nc.all_engine_barrier()
        return self.stack.__exit__(*e)

    def sb(self, name, shape, dt=F32):
        return self.stack.enter_context(self.nc.sbuf_tensor(f"{self.name}_{name}", shape, dt))

    def ps(self, name, shape=(P, 512)):
        return self.stack.enter_context(self.nc.psum_tensor(f"{self.name}_{name}", list(shape), F32))

    def sem(self, name):
        self.sems.append(self.nc.alloc_semaphore(f"{self.name}_{name}"))
        return self.sems[-1]


def stage_setup(nc, a, k):
    with Stage(nc, "setup") as s:
        vrows, brows = s.sb("vrows", [P, P]), s.sb("brows", [P, P])
        vps, bps = s.ps("vps"), s.ps("bps")
        e, u = s.sb("e", [P, 24]), s.sb("u", [P, 24])
        lb_t = s.sb("lb_t", [P, 3, 16])
        rpb_rows = s.sb("rpb_rows", [16, RPB_H, RPB_PAD])
        small_in, x_in, const_in, rpb_in = s.sem("small_in"), s.sem("x_in"), s.sem("const_in"), s.sem("rpb_in")
        zeroed, turned, cols_ready, exp_ready, padded = (
            s.sem(n) for n in ("zeroed", "turned", "cols_ready", "exp_ready", "padded"))
        lbx_ready, lbe_ready = s.sem("lbx_ready"), s.sem("lbe_ready")
        with nc.Block() as block:
            @block.sync
            def _(sp):
                for name, n in VECTORS:
                    sp.dma_start(vrows[ROW[name]:ROW[name] + n, :], rows128(a[name])).then_inc(small_in, 16)
                sp.dma_start(brows[0:48, :], rows128(a["b_ada"])).then_inc(small_in, 16)
                sp.dma_start(brows[48:96, :], rows128(a["b_ada_2"])).then_inc(small_in, 16)
                sp.dma_start(k["ident"][:, :], a["ident"]).then_inc(const_in, 16)
                sp.wait_ge(zeroed, 1)
                sp.dma_start(rpb_rows[:, :, 16:16 + RPB_W], a["rpb_a"][0]).then_inc(rpb_in, 16)
                sp.dma_start(k["xs"][:, 0:LT, :], a["x"][0].rearrange("(t p) d -> p t d", p=P)).then_inc(x_in, 16)
                sp.dma_start(k["xs"][:, LT:NT, :], a["ctx"][0].rearrange("(t p) d -> p t d", p=P)).then_inc(x_in, 16)
                sp.wait_ge(rpb_in, 16)
                sp.dma_start(k["rpb_pad"], rpb_rows[:, :, :]).then_inc(padded, 16)
                sp.wait_ge(padded, 16)
                sp.wait_ge(x_in, 32)

            @block.gpsimd
            def _(pool):
                pool.memset(rpb_rows[:, :, :], 0.0).then_inc(zeroed, 1)

            @block.tensor
            def _(pe):
                pe.wait_ge(const_in, 16)
                pe.wait_ge(small_in, 16 * (len(VECTORS) + 2))
                pe.transpose(vps[:, 0:NVEC], vrows[0:NVEC, :], k["ident"][0:NVEC, 0:NVEC]).then_inc(turned, 1)
                pe.transpose(bps[:, 0:NMOD], brows[0:NMOD, :], k["ident"][0:NMOD, 0:NMOD]).then_inc(turned, 1)

            @block.vector
            def _(dve):
                dve.wait_ge(turned, 2)
                dve.tensor_copy(k["vecT"][:, :], vps[:, 0:NVEC]).then_inc(cols_ready, 1)
                dve.tensor_copy(k["biasT"][:, :], bps[:, 0:NMOD])
                dve.wait_ge(exp_ready, 1)
                dve.tensor_scalar(u[:, :], e[:, :], 1.0, None, ALU.add)
                lb = k["vecT"][:, ROW["lb_c"]:ROW["lb_c"] + 32]
                dve.tensor_tensor(lb_t[:, 2, :], lb[:, 0:16], lb[:, 16:32], ALU.max)
                dve.drain()
                dve.tensor_tensor(lb_t[:, 0, :], lb[:, 0:16], lb_t[:, 2, :], ALU.subtract)
                dve.tensor_tensor(lb_t[:, 1, :], lb[:, 16:32], lb_t[:, 2, :], ALU.subtract)
                dve.reciprocal(e[:, :], u[:, :])
                dve.drain().then_inc(lbx_ready, 1)
                dve.tensor_tensor(k["silu_c"][:, :, :], k["vecT"][:, 0:24].rearrange("p (v k) -> p k v", v=3),
                                  e[:, :].rearrange("p (v k) -> p k v", v=3), ALU.mult)
                dve.wait_ge(lbe_ready, 1)
                dve.tensor_tensor(lb_t[:, 2, :], lb_t[:, 0, :], lb_t[:, 1, :], ALU.add)
                dve.drain()
                dve.reciprocal(lb_t[:, 0, :], lb_t[:, 2, :])
                dve.drain()
                dve.tensor_tensor(k["lbT"][:, 0, :], lb_t[:, 1, :], lb_t[:, 0, :], ALU.mult)
                dve.drain()
                dve.tensor_scalar(k["lbT"][:, 1, :], k["lbT"][:, 0, :], -1.0, 1.0, ALU.mult, ALU.add)

            @block.scalar
            def _(act):
                act.preload_act_table_set("natural_log_exp_and_others")
                act.wait_ge(cols_ready, 1)
                act.activation(e[:, :], k["vecT"][:, 0:24], ACT.Exp, scale=-1.0).then_inc(exp_ready, 1)
                act.wait_ge(lbx_ready, 1)
                act.activation(lb_t[:, 0:2, :], lb_t[:, 0:2, :], ACT.Exp).then_inc(lbe_ready, 1)


def stage_modulations(nc, a, k):
    NCH = 512
    with Stage(nc, "ada") as s:
        w = [s.sb(f"w{u}", [P, KD, NCH]) for u in range(2)]
        row = [s.sb(f"row{u}", [3, NCH]) for u in range(2)]
        ps, cols = [s.ps(f"ps{u}") for u in range(2)], [s.ps(f"cols{u}") for u in range(2)]
        w_in = [s.sem(f"w_in{u}") for u in range(2)]
        products_ready, rows_ready, turned = s.sem("products_ready"), s.sem("rows_ready"), s.sem("turned")
        stored = s.sem("stored")
        parts = [(a["w_ada"][0], 0, 3), (a["w_ada"][1], 6, 3), (a["w_ada_2"][0], 12, 6)]
        with nc.Block() as block:
            @block.sync
            def _(sp):
                srcs = [wd.rearrange("(k p) n -> p k n", p=P) for wd, _, _ in parts]
                for n, (src, (_, c0, pairs)) in enumerate(zip(srcs, parts)):
                    if n == 0:
                        for u in range(2):
                            sp.dma_start(w[u][:, :, :], src[:, :, u * NCH:(u + 1) * NCH]).then_inc(w_in[u], 16)
                    with sp.Fori(0, pairs - 1) as i:
                        for u in range(2):
                            sp.wait_ge(products_ready, i * 2 + (c0 + u + 1))
                            sp.dma_start(w[u][:, :, :], src[:, :, bass.ds(i * (2 * NCH) + (u + 2) * NCH, NCH)])\
                                .then_inc(w_in[u], 16)
                    if n + 1 < len(parts):
                        for u in range(2):
                            sp.wait_ge(products_ready, c0 + 2 * pairs - 1 + u)
                            sp.dma_start(w[u][:, :, :], srcs[n + 1][:, :, u * NCH:(u + 1) * NCH]).then_inc(w_in[u], 16)

            @block.tensor
            def _(pe):
                def turn(u, i, c):
                    pe.wait_ge(rows_ready, i * 2 + (c + 1))
                    pe.wait_ge(stored, i * 2 + (c + 1))
                    pe.sem_inc(k["apart"], 1)
                    for b in range(NCH // P):
                        tr = pe.transpose(cols[u][:, 3 * b:3 * b + 3], row[u][:, b * P:(b + 1) * P],
                                          k["ident"][0:3, 0:3])
                    tr.then_inc(turned, 1)

                for wd, c0, pairs in parts:
                    with pe.Fori(0, pairs) as i:
                        for u in range(2):
                            pe.wait_ge(w_in[u], i * 16 + (c0 // 2 + 1) * 16)
                            for kk in range(KD):
                                mm = pe.matmul(ps[u][0:3, :], k["silu_c"][:, kk, :], w[u][:, kk, :],
                                               start=kk == 0, stop=kk == KD - 1)
                            mm.then_inc(products_ready, 1)
                            if u == 1:
                                turn(0, i, c0)
                        turn(1, i, c0 + 1)

            @block.scalar
            def _(act):
                for wd, c0, pairs in parts:
                    with act.Fori(0, pairs) as i:
                        for u in range(2):
                            act.wait_ge(products_ready, i * 2 + (c0 + u + 1))
                            act.activation(row[u][:, :], ps[u][0:3, :], ACT.Copy).then_inc(rows_ready, 1)

            @block.vector
            def _(dve):
                dve.drain().then_inc(stored, 1)
                dve.drain().then_inc(stored, 1)
                for wd, c0, pairs in parts:
                    with dve.Fori(0, pairs) as i:
                        for u in range(2):
                            dve.wait_ge(turned, i * 2 + (c0 + u + 1))
                            col = bass.ds(i * 8 + (4 * (c0 + u)), 4)
                            dve.tensor_tensor(k["modT"][:, col, :], cols[u][:, 0:12].rearrange("p (b v) -> p b v", v=3),
                                              k["biasT"][:, col].unsqueeze(2).to_broadcast([P, 4, 3]), ALU.add)\
                                .then_inc(stored, 1)


def stage_norm(nc, k, name, groups, xs, hT, rows=None):
    with Stage(nc, name) as s:
        sq = [s.sb(f"sq{u}", [P, D]) for u in range(2)]
        xn = [s.sb(f"xn{u}", [P, D]) for u in range(2)]
        ss, ms, rstd = s.sb("ss", [P, 2]), s.sb("ms", [P, 2]), s.sb("rstd", [P, 2])
        gain = s.sb("gain", [P, len(groups), KD])
        half = s.sb("half", [P, 1])
        ps = [[s.ps(f"ps{u}{h}") for h in range(2)] for u in range(2)]
        sums_ready, rstd_ready, xn_ready, turned, stored = (
            s.sem(n) for n in ("sums_ready", "rstd_ready", "xn_ready", "turned", "stored"))
        mean_ready = s.sem("mean_ready")
        gain_ready = s.sem("gain_ready")
        rows_saved, xn_free = s.sem("rows_saved"), s.sem("xn_free")
        KH = KD // 2
        with nc.Block() as block:
            if rows is not None:
                @block.sync
                def _(sp):
                    sp.sem_inc(xn_free, 1)
                    sp.sem_inc(xn_free, 1)
                    for t in range(LT):
                        sp.wait_ge(xn_ready, t + 1)
                        sp.dma_start(rows[t * P:(t + 1) * P, :], xn[t % 2][:, :]).then_inc(rows_saved, 16)
                        sp.wait_ge(rows_saved, 16 * (t + 1))
                        sp.sem_inc(xn_free, 1)

            @block.vector
            def _(dve):
                for g, (_, _, nw, mod, v) in enumerate(groups):
                    dve.tensor_scalar(gain[:, g, :], k["modT"][:, mod + 8:mod + 16, v], 1.0, None, ALU.add)
                dve.drain()
                for g, (_, _, nw, mod, v) in enumerate(groups):
                    dve.tensor_tensor(gain[:, g, :], gain[:, g, :], k["vecT"][:, nw:nw + 8], ALU.mult)
                dve.drain().then_inc(gain_ready, 1)
                for g, (t0, n, nw, mod, v) in enumerate(groups):
                    with dve.Fori(0, n // 2) as i:
                        for u in range(2):
                            dve.wait_ge(sums_ready, i * 2 + (t0 + u + 1))
                            dve.tensor_scalar(ms[:, u:u + 1], ss[:, u:u + 1], 1.0 / D, EPS, ALU.mult, ALU.add)\
                                .then_inc(mean_ready, 1)
                        for u in range(2):
                            dve.wait_ge(turned, i * 2 + (t0 + u + 1))
                            for b in range(KH):
                                ev = dve.tensor_scalar(hT[:, b, bass.ds(i * 256 + (t0 + u) * P, P)], ps[u][0][:, b * P:(b + 1) * P],
                                                       gain[:, g, b:b + 1], k["modT"][:, mod + b:mod + b + 1, v],
                                                       ALU.mult, ALU.add)
                            ev.then_inc(stored, 1)

            @block.gpsimd
            def _(pool):
                pool.memset(half[:, :], -0.5)
                pool.drain()
                for g, (t0, n, nw, mod, v) in enumerate(groups):
                    with pool.Fori(0, n // 2) as i:
                        for u in range(2):
                            pool.wait_ge(mean_ready, i * 2 + (t0 + u + 1))
                            pool.tensor_tensor(rstd[:, u:u + 1], ms[:, u:u + 1], half[:, :], ALU.pow)\
                                .then_inc(rstd_ready, 1)

            @block.scalar
            def _(act):
                act.wait_ge(gain_ready, 1)
                for g, (t0, n, nw, mod, v) in enumerate(groups):
                    with act.Fori(0, n // 2) as i:
                        for u in range(2):
                            act.activation(sq[u][:, :], xs[:, bass.ds(i * 2 + (t0 + u), 1), :].squeeze(1), ACT.Square,
                                           accum_out=ss[:, u:u + 1]).then_inc(sums_ready, 1)
                        for u in range(2):
                            act.wait_ge(rstd_ready, i * 2 + (t0 + u + 1))
                            if rows is not None:
                                act.wait_ge(xn_free, i * 2 + (t0 + u + 1))
                            act.sem_inc(k["apart"], 1)
                            act.activation(xn[u][:, :], xs[:, bass.ds(i * 2 + (t0 + u), 1), :].squeeze(1), ACT.Copy,
                                           scale=rstd[:, u:u + 1]).then_inc(xn_ready, 1)
                        for u in range(2):
                            act.wait_ge(turned, i * 2 + (t0 + u + 1))
                            act.sem_inc(k["apart"], 1)
                            for b in range(KH):
                                act.activation(hT[:, KH + b, bass.ds(i * 256 + (t0 + u) * P, P)],
                                               ps[u][1][:, b * P:(b + 1) * P], ACT.Identity,
                                               scale=gain[:, g, KH + b:KH + b + 1],
                                               bias=k["modT"][:, mod + KH + b:mod + KH + b + 1, v])

            @block.tensor
            def _(pe):
                for g, (t0, n, nw, mod, v) in enumerate(groups):
                    with pe.Fori(0, n // 2) as i:
                        for u in range(2):
                            pe.wait_ge(xn_ready, i * 2 + (t0 + u + 1))
                            for b in range(KD):
                                tr = pe.transpose(ps[u][b // KH][:, (b % KH) * P:(b % KH + 1) * P],
                                                  xn[u][:, b * P:(b + 1) * P], k["ident"][:, :])
                            tr.then_inc(turned, 1)


def stage_attention_a(nc, a, k, yT):
    HD, W4 = 64, 512
    KINDS = {0: (0, 0, (1, 2)), 1: (256, 512, (0, 1, 2)), 2: (256, 512, (0, 1, 2)), 3: (640, 1152, (0, 1))}
    NBIAS = 896 + 3 * CTX
    units = [(t, h) for t in range(NT) for h in range(2)]
    NU = len(units)

    def key_tiles(t):
        near = list(range(max(0, t - 1), min(LT, t + 2))) if t < LT else []
        return near, near + list(range(LT, NT))

    with Stage(nc, "na") as s:
        w = s.sb("w", [P, KD, 4, P])
        h_cols = s.sb("h_cols", [P, KD, SEQ])
        squares, qkn = s.sb("squares", [P, 4, HD]), [s.sb(f"qkn{u}", [P, 4, HD]) for u in range(2)]
        ss, ms, rstd, half = (s.sb(n, [P, 4]) for n in ("ss", "ms", "rstd", "half"))
        qw, kw = s.sb("qw", [P, 1]), s.sb("kw", [P, 1])
        qT, kT = [s.sb(f"qT{n}", [P, NTOK]) for n in range(2)], [s.sb(f"kT{n}", [P, NTOK]) for n in range(2)]
        v, zs = [s.sb(f"v{n}", [P, NT, P]) for n in range(2)], [s.sb(f"zs{n}", [P, NT, P]) for n in range(2)]
        ez, uz, rz = s.sb("ez", [P, P]), s.sb("uz", [P, P]), s.sb("rz", [P, P])
        flip, mask = s.sb("flip", [P, P]), s.sb("mask", [P, 896])
        u_rev, bias = s.sb("u_rev", [P, 2, GRID_H, UK]), s.sb("bias", [P, 2, NBIAS])
        sc, p = [s.sb(f"sc{u}", [P, 640]) for u in range(2)], [s.sb(f"p{u}", [P, 640]) for u in range(2)]
        pT = [s.sb(f"pT{u}", [P, 640]) for u in range(2)]
        m, nm, sums, rinv = (s.sb(n, [P, NU]) for n in ("m", "nm", "sums", "rinv"))
        y = s.sb("y", [P, 2, P])
        banks = [s.ps(f"bank{n}") for n in range(6)]
        s_ps = s.ps("s_ps", (P, 1024))
        proj, qk_ps, o_ps, yT_ps, pT_ps = (*banks[0:4], banks[4:6])

        regrouped, yT_stored, z_ready = s.sem("regrouped"), s.sem("yT_stored"), s.sem("z_ready")
        w_in, u_in, const_in = s.sem("w_in"), s.sem("u_in"), s.sem("const_in")
        (proj_ready, squares_ready, means_ready, rstd_ready, qk_normed, qk_turned, qk_stored, consts_ready,
         u_flipped, bias_ready, scores_ready, max_ready, exp_ready, pT_ready, pT_stored_dve, pT_stored_act, pv_ready,
         y_ready, yT_ready) = (s.sem(n) for n in (
             "proj_ready", "squares_ready", "means_ready", "rstd_ready", "qk_normed", "qk_turned", "qk_stored",
             "consts_ready", "u_flipped", "bias_ready", "scores_ready", "max_ready", "exp_ready", "pT_ready",
             "pT_stored_dve", "pT_stored_act", "pv_ready", "y_ready", "yT_ready"))

        def bank_of(b, n):
            first = 3 if n > 3 else 1
            return (0, b * P) if b < first else (1, (b - first) * P)

        def regroup(eng, kk):
            src = k["hT"][:, kk, 0:SEQ].rearrange("p (r t c) -> p t r c", r=GRID_H, t=LT)
            for t in range(LT):
                dst = h_cols[:, kk, t * P:(t + 1) * P].rearrange("p (r c) -> p r c", r=GRID_H)
                if eng is nc.scalar:
                    ins = eng.activation(dst, src[:, t], ACT.Copy)
                else:
                    ins = eng.tensor_copy(dst, src[:, t])
            ins.then_inc(regrouped, 1)

        def token_tile(kk, j):
            if j < LT:
                return h_cols[:, kk, j * P:(j + 1) * P]
            return k["hT"][:, kk, j * P:(j + 1) * P]

        def at(g, per, n):
            i, c = g
            return i * (2 * per) + (c * per + n)

        def run(eng, turn):
            with eng.Fori(0, NA_PAIRS // 2 - 1) as i:
                turn((i, 0))
                turn((i, 1))
            turn((NA_PAIRS // 2 - 1, 0))
            turn((NA_PAIRS // 2 - 1, 1), last=True)

        def following(g):
            return (g[0], g[1] + 1)

        def turn_y(pe, g, t):
            pe.wait_ge(y_ready, at(g, NU, 2 * t + 2))
            pe.wait_ge(yT_stored, at(g, NT, t + 1))
            pe.transpose(yT_ps[:, 0:P], y[:, t % 2, :], k["ident"][:, :]).then_inc(yT_ready, 1)

        def store_yT(act, g, t):
            dst = yT[:, bass.ds(g[0] * 2 + g[1], 1), :].squeeze(1)
            if t < LT:
                dst = dst[:, 0:SEQ].rearrange("p (r c) -> p r c", c=GRID_W)[:, :, COLS * t:COLS * (t + 1)]
                act.activation(dst, yT_ps[:, 0:P].rearrange("p (r c) -> p r c", c=COLS), ACT.Copy)
            else:
                act.activation(dst[:, t * P:(t + 1) * P], yT_ps[:, 0:P], ACT.Copy)
            act.drain().then_inc(yT_stored, 1)

        with nc.Block() as block:
            @block.sync
            def _(sp):
                for dst, src in ((qw, "q_norm_a"), (kw, "k_norm_a")):
                    for h in range(2):
                        sp.dma_start(dst[h * HD:(h + 1) * HD, :], a[src].rearrange("a d -> d a")).then_inc(const_in, 16)
                sp.dma_start(flip[:, :], a["flip"]).then_inc(const_in, 16)
                sp.dma_start(mask[:, :], a["na_mask"]).then_inc(const_in, 16)
                src = a["w_in_ab"][0].rearrange("(k p) n -> p k n", p=P)

                def load(pair):
                    for seg in range(4):
                        sp.dma_start(w[:, :, seg, :], src[:, :, bass.ds(pair * P + seg * D, P)]).then_inc(w_in, 16)

                def load_bias(pair):
                    for h in range(2):
                        for r in range(GRID_H):
                            at = (pair * 2 + h) * (RPB_H * RPB_PAD) + r * RPB_PAD
                            sp.dma_start(u_rev[r * COLS:(r + 1) * COLS, h, :, :],
                                         bass.AP(k["rpb_pad"].tensor, at, [[1, COLS], [RPB_PAD, GRID_H], [1, UK]]))\
                                .then_inc(u_in, 16)

                load(0)
                load_bias(0)
                with sp.Fori(0, NA_PAIRS - 1) as i:
                    sp.wait_ge(proj_ready, i * NT + NT)
                    load(i + 1)
                    sp.wait_ge(u_flipped, i * 2 + 2)
                    load_bias(i + 1)

            @block.tensor
            def _(pe):
                pe.wait_ge(const_in, 16 * 6)
                pe.wait_ge(regrouped, KD)

                def project(g, j, half):
                    if half == 0:
                        if j == 0:
                            pe.wait_ge(w_in, at(g, 64, 64))
                        pe.wait_ge(qk_normed, at(g, NT, j + 1))
                    for kk in range(half * KD // 2, (half + 1) * KD // 2):
                        mm = pe.matmul(proj[:, :], token_tile(kk, j), w[:, kk, :, :],
                                       start=kk == 0, stop=kk == KD - 1)
                    if half == 1:
                        mm.then_inc(proj_ready, 1)

                def turn_qk(g, j):
                    pe.wait_ge(qk_normed, at(g, NT, j + 2))
                    pe.wait_ge(qk_stored, at(g, NT, j + 1))
                    for b in range(2):
                        tr = pe.transpose(qk_ps[:, b * P:(b + 1) * P], qkn[j % 2][:, 2 * b:2 * b + 2, :],
                                          k["ident"][:, :])
                    tr.then_inc(qk_turned, 1)

                for j in range(NT):
                    project((0, 0), j, 0)
                    project((0, 0), j, 1)
                    if j >= 1:
                        turn_qk((0, 0), j - 1)
                turn_qk((0, 0), NT - 1)

                def turn(g, last=False):
                    u = g[1] % 2
                    pe.wait_ge(exp_ready, at(g, NU, 1))
                    pe.wait_ge(u_in, at(g, 256, 256))
                    for h in range(2):
                        pe.matmul(s_ps[:, h * 512:h * 512 + 384], flip[:, :], u_rev[:, h, :, :], start=True, stop=True)\
                            .then_inc(u_flipped, 1)
                    if not last:
                        project(following(g), 0, 0)
                    pe.wait_ge(qk_stored, at(g, NT, NT + 1))
                    pe.wait_ge(bias_ready, at(g, 1, 1))
                    for n in range(NU + 3):
                        if n < NU:
                            t, h = units[n]
                            near, _ = key_tiles(t)
                            hs = slice(h * HD, (h + 1) * HD)
                            if n >= 1:
                                pe.wait_ge(max_ready, at(g, NU, n))
                            if near:
                                pe.matmul(s_ps[:, 512 - len(near) * P:512], qT[u][hs, t * P:(t + 1) * P],
                                          kT[u][hs, near[0] * P:(near[-1] + 1) * P], start=True, stop=True)
                            pe.matmul(s_ps[:, 512:512 + CTX], qT[u][hs, t * P:(t + 1) * P], kT[u][hs, SEQ:NTOK],
                                      start=True, stop=True).then_inc(scores_ready, 1)
                        if 1 <= n <= NU:
                            pe.wait_ge(exp_ready, at(g, NU, n + 1))
                        if n >= 2 and n - 2 < NU:
                            pe.wait_ge(pT_stored_dve, at(g, NU, n - 1))
                            pe.wait_ge(pT_stored_act, at(g, NU, n - 1))
                        if 1 <= n <= NU:
                            _, keys = key_tiles(units[n - 1][0])
                            for b in range(len(keys)):
                                bank, col = bank_of(b, len(keys))
                                tr = pe.transpose(pT_ps[bank][:, col:col + P],
                                    p[(n - 1) % 2][:, b * P:(b + 1) * P], k["ident"][:, :])
                            tr.then_inc(pT_ready, 1)
                        if n >= 2 and n - 2 < NU:
                            t, h = units[n - 2]
                            _, keys = key_tiles(t)
                            if n >= 3:
                                pe.wait_ge(y_ready, at(g, NU, n - 2))
                            for b, kt in enumerate(keys):
                                mm = pe.matmul(o_ps[:, 0:HD], pT[n % 2][:, b * P:(b + 1) * P],
                                               v[u][:, kt, h * HD:(h + 1) * HD], start=b == 0, stop=b == len(keys) - 1)
                            mm.then_inc(pv_ready, 1)
                        if not last:
                            if n < 2 * NT - 1:
                                project(following(g), (n + 1) // 2, (n + 1) % 2)
                            if n >= 2 and n % 2 == 0 and n // 2 - 1 < NT:
                                turn_qk(following(g), n // 2 - 1)
                        if n >= 4 and n % 2 == 0:
                            turn_y(pe, g, n // 2 - 2)

                run(pe, turn)

            @block.scalar
            def _(act):
                for kk in (0, 1, 2):
                    regroup(nc.scalar, kk)
                act.wait_ge(consts_ready, 1)
                act.drain().then_inc(qk_stored, 1)
                act.drain().then_inc(yT_stored, 1)
                act.drain().then_inc(exp_ready, 1)

                def store_qk(g, j):
                    u = g[1] % 2
                    act.wait_ge(qk_turned, at(g, NT, j + 1))
                    act.activation(qT[u][:, j * P:(j + 1) * P], qk_ps[:, 0:P], ACT.Copy, scale=qw[:, 0:1])
                    act.activation(kT[u][:, j * P:(j + 1) * P], qk_ps[:, P:2 * P], ACT.Copy, scale=kw[:, 0:1])\
                        .then_inc(qk_stored, 1)

                def take(g, j):
                    act.wait_ge(proj_ready, at(g, NT, j + 1))
                    act.wait_ge(qk_normed, at(g, NT, j + 1))
                    act.activation(v[g[1] % 2][:, j, :], proj[:, 256:384], ACT.Copy)
                    act.activation(ez[:, :], proj[:, 384:512], ACT.Exp, scale=-1.0)
                    act.activation(squares[:, :, :], proj[:, 0:256].rearrange("p (h d) -> p h d", d=HD),
                                   ACT.Square).then_inc(squares_ready, 1)
                    act.drain()
                    act.activation(uz[:, :], ez[:, :], ACT.Ln, bias=1.0)
                    act.drain()
                    act.activation(rz[:, :], uz[:, :], ACT.Exp, scale=-1.0).then_inc(z_ready, 1)

                for j in range(NT):
                    take((0, 0), j)
                    if j >= 1:
                        store_qk((0, 0), j - 1)
                store_qk((0, 0), NT - 1)

                def turn(g, last=False):
                    for n in range(NU + 3):
                        if n < NU:
                            t, h = units[n]
                            near, _ = key_tiles(t)
                            nw = len(near) * P
                            act.wait_ge(max_ready, at(g, NU, n + 1))
                            if n >= 2:
                                act.wait_ge(pT_ready, at(g, NU, n - 1))
                            act.activation(p[n % 2][:, 0:nw + CTX], sc[n % 2][:, 0:nw + CTX], ACT.Exp,
                                           bias=nm[:, n:n + 1], accum_out=sums[:, n:n + 1]).then_inc(exp_ready, 1)
                        if 1 <= n <= NU:
                            _, keys = key_tiles(units[n - 1][0])
                            act.wait_ge(pT_ready, at(g, NU, n))
                            if n >= 3:
                                act.wait_ge(pv_ready, at(g, NU, n - 2))
                            if len(keys) > 3:
                                st = act.activation(pT[(n - 1) % 2][:, 384:len(keys) * P],
                                                    pT_ps[1][:, 0:(len(keys) - 3) * P], ACT.Copy)
                            else:
                                st = act.activation(pT[(n - 1) % 2][:, P:2 * P], pT_ps[1][:, 0:P], ACT.Copy)
                            st.then_inc(pT_stored_act, 1)
                        if not last:
                            if n % 2 == 0 and n // 2 < NT:
                                take(following(g), n // 2)
                            if n >= 3 and n % 2 == 1 and (n - 3) // 2 < NT:
                                store_qk(following(g), (n - 3) // 2)
                        if n >= 4 and n % 2 == 0:
                            t = n // 2 - 2
                            act.wait_ge(yT_ready, at(g, NT, t + 1))
                            act.sem_inc(k["apart"], 1)
                            store_yT(act, g, t)
                    if not last:
                        for j in range((NU + 2 - 3) // 2 + 1, NT):
                            store_qk(following(g), j)

                run(act, turn)

            @block.gpsimd
            def _(pool):
                pool.memset(half[:, :], -0.5)
                for kk in (3, 4):
                    regroup(nc.gpsimd, kk)
                pool.drain()
                with pool.Fori(0, NA_PAIRS) as i:
                    for j in range(NT):
                        pool.wait_ge(means_ready, i * NT + (j + 1))
                        pool.tensor_tensor(rstd[:, :], ms[:, :], half[:, :], ALU.pow).then_inc(rstd_ready, 1)

            @block.vector
            def _(dve):
                dve.memset(bias[:, :, :], 0.0)
                for kk in (5, 6, 7):
                    regroup(nc.vector, kk)
                dve.wait_ge(const_in, 16 * 6)
                dve.tensor_scalar(qw[:, :], qw[:, :], NA_SCALE, None, ALU.mult).then_inc(consts_ready, 1)
                dve.drain().then_inc(qk_normed, 1)

                def mean(g, j):
                    dve.wait_ge(squares_ready, at(g, NT, j + 1))
                    dve.tensor_reduce(ss[:, :], squares[:, :, :], AX_X, ALU.add)
                    dve.drain()
                    dve.tensor_scalar(ms[:, :], ss[:, :], 1.0 / HD, EPS, ALU.mult, ALU.add).then_inc(means_ready, 1)

                def normalise(g, j):
                    dve.wait_ge(z_ready, at(g, NT, j + 1))
                    dve.tensor_tensor(zs[g[1] % 2][:, j, :], proj[:, 384:512], rz[:, :], ALU.mult)
                    dve.wait_ge(rstd_ready, at(g, NT, j + 1))
                    dve.tensor_tensor(qkn[j % 2][:, :, :], proj[:, 0:256].rearrange("p (h d) -> p h d", d=HD),
                                      rstd[:, :].unsqueeze(2).to_broadcast([P, 4, HD]), ALU.mult)
                    dve.drain().then_inc(qk_normed, 1)

                for j in range(NT):
                    mean((0, 0), j)
                    normalise((0, 0), j)

                def turn(g, last=False):
                    u = g[1] % 2
                    dve.wait_ge(u_flipped, at(g, 2, 2))
                    for h in range(2):
                        table = s_ps[:, h * 512:h * 512 + 384].rearrange("p (a t c) -> p t a c", a=GRID_H, t=3)
                        for t in (0, 1, 3):
                            of_mask, of_bias, tiles = KINDS[t]
                            for x, dt in enumerate(tiles):
                                src = slice(of_mask + x * P, of_mask + (x + 1) * P)
                                to = slice(of_bias + x * P, of_bias + (x + 1) * P)
                                ad = dve.tensor_tensor(
                                    bias[:, h, to].rearrange("p (a c) -> p a c", a=GRID_H), table[:, dt, :, :],
                                    mask[:, src].rearrange("p (a c) -> p a c", a=GRID_H), ALU.add)
                    ad.then_inc(bias_ready, 1)
                    dve.drain()
                    for n in range(NU + 3):
                        if n < NU:
                            t, h = units[n]
                            near, _ = key_tiles(t)
                            nw = len(near) * P
                            dve.wait_ge(scores_ready, at(g, NU, n + 1))
                            if n >= 2:
                                dve.wait_ge(exp_ready, at(g, NU, n))
                            dve.sem_inc(k["apart"], 1)
                            off = KINDS[t][1] if near else 256
                            dve.tensor_tensor_reduce(sc[n % 2][:, 0:nw + CTX], s_ps[:, 512 - nw:512 + CTX],
                                                     bias[:, h, off:off + nw + CTX], 1.0, -3e38,
                                                     ALU.add, ALU.max, m[:, n:n + 1])
                            dve.drain()
                            dve.tensor_scalar(nm[:, n:n + 1], m[:, n:n + 1], -1.0, None, ALU.mult)\
                                .then_inc(max_ready, 1)
                        if 1 <= n <= NU:
                            _, keys = key_tiles(units[n - 1][0])
                            first = 3 if len(keys) > 3 else 1
                            dve.wait_ge(pT_ready, at(g, NU, n))
                            dve.tensor_copy(pT[(n - 1) % 2][:, 0:first * P], pT_ps[0][:, 0:first * P])\
                                .then_inc(pT_stored_dve, 1)
                        if 2 <= n < NU + 2:
                            t, h = units[n - 2]
                            c = slice(n - 2, n - 1)
                            dve.reciprocal(rinv[:, c], sums[:, c])
                            dve.drain()
                            dve.wait_ge(pv_ready, at(g, NU, n - 1))
                            dve.scalar_tensor_tensor(out=y[:, t % 2, h * HD:(h + 1) * HD], in0=o_ps[:, 0:HD],
                                                     scalar=rinv[:, c], in1=zs[u][:, t, h * HD:(h + 1) * HD],
                                                     op0=ALU.mult, op1=ALU.mult).then_inc(y_ready, 1)
                        if not last:
                            if n >= 1 and n % 2 == 1 and (n - 1) // 2 < NT:
                                normalise(following(g), (n - 1) // 2)
                            if n % 2 == 0 and n // 2 < NT:
                                mean(following(g), n // 2)

                run(dve, turn)


SEQ_TILE = [j + CT if j < LT else j - LT for j in range(NT)]


def stage_gates(nc, a, k):
    with Stage(nc, "gates") as s:
        wg, bg = s.sb("wg", [P, KD, P]), s.sb("bg", [P, 1])
        g, t0, t1 = s.sb("g", [P, NTOK]), s.sb("t0", [P, NTOK]), s.sb("t1", [P, NTOK])
        r_lf, r_i, b, m, ones = (s.sb(n, [36, NTOK]) for n in ("r_lf", "r_i", "b", "m", "ones"))
        a_out, rows = s.sb("a_out", [36, NTOK]), s.sb("rows", [P, NTOK])
        ps0, ps1 = s.ps("ps0"), s.ps("ps1")
        col_ps = [s.ps(f"col_ps{n}") for n in range(2)]
        zeroed, w_in, a_saved = s.sem("zeroed"), s.sem("w_in"), s.sem("a_saved")
        (products_ready, g_ready, ef_ready, one_ready, ln_ready, a_ready, bm_ready, em_ready, rows_ready, turned,
         stored) = (s.sem(n) for n in ("products_ready", "g_ready", "ef_ready", "one_ready", "ln_ready", "a_ready",
                                       "bm_ready", "em_ready", "rows_ready", "turned", "stored"))

        def in_order(dst, src, d0, s0, back):
            for n, (at, to) in enumerate(((slice(SEQ, NTOK), slice(0, CTX)), (slice(0, SEQ), slice(CTX, NTOK)))):
                x = src[s0:s0 + 4, at]
                ins = nc.vector.tensor_copy(dst[d0:d0 + 4, to], x[:, ::-1] if back else x)
            return ins

        with nc.Block() as block:
            @block.sync
            def _(sp):
                sp.wait_ge(zeroed, 2)
                w = a["w_in_ab"][0][:, 9 * D:9 * D + 16].rearrange("(k p) n -> p k n", p=P)
                bias = a["b_gate_ab"].rearrange("a n -> n a")
                for q in range(4):
                    sp.dma_start(wg[:, :, 32 * q:32 * q + 4], w[:, :, 4 * q:4 * q + 4]).then_inc(w_in, 16)
                    sp.dma_start(bg[32 * q:32 * q + 4, :], bias[4 * q:4 * q + 4, :]).then_inc(w_in, 16)
                sp.wait_ge(a_ready, 1)
                for d in range(2):
                    sp.dma_start(k["a_rows"][d], a_out[32 * d:32 * d + 4, :]).then_inc(a_saved, 16)
                sp.wait_ge(a_saved, 32)

            @block.gpsimd
            def _(pool):
                pool.memset(wg[:, :, :], 0.0).then_inc(zeroed, 1)
                pool.memset(bg[:, :], 0.0).then_inc(zeroed, 1)
                pool.memset(ones[:, :], 1.0)
                pool.memset(r_lf[:, :], 0.0)
                pool.memset(r_i[:, :], 0.0)
                pool.memset(rows[:, :], 0.0)
                pool.drain().then_inc(zeroed, 1)

            @block.tensor
            def _(pe):
                pe.wait_ge(w_in, 16 * 8)
                for ps, c0, n in ((ps0, 0, SEQ), (ps1, SEQ, CTX)):
                    for kk in range(KD):
                        mm = pe.matmul(ps[:, 0:n], wg[:, kk, :], k["hT"][:, kk, c0:c0 + n],
                                       start=kk == 0, stop=kk == KD - 1)
                mm.then_inc(products_ready, 1)
                pe.wait_ge(rows_ready, 1)
                for t in range(NT):
                    tr = pe.transpose(col_ps[t // 3][:, t % 3 * P:t % 3 * P + P], rows[:, t * P:(t + 1) * P],
                                      k["ident"][:, :])
                tr.then_inc(turned, 1)

            @block.scalar
            def _(act):
                act.wait_ge(g_ready, 1)
                act.activation(t0[:, :], g[:, :], ACT.Abs)
                act.drain()
                act.activation(t1[:, :], t0[:, :], ACT.Exp, scale=-1.0)
                act.drain()
                act.activation(t0[:, :], t1[:, :], ACT.Ln, bias=1.0).then_inc(ln_ready, 1)
                act.wait_ge(bm_ready, 1)
                act.activation(r_i[:, :], b[:, :], ACT.Exp, scale=-1.0).then_inc(em_ready, 1)

            @block.vector
            def _(dve):
                dve.wait_ge(zeroed, 3)
                dve.wait_ge(products_ready, 1)
                dve.tensor_scalar(g[:, 0:SEQ], ps0[:, :], bg[:, 0:1], None, ALU.add)
                dve.tensor_scalar(g[:, SEQ:NTOK], ps1[:, 0:CTX], bg[:, 0:1], None, ALU.add).then_inc(g_ready, 1)
                dve.wait_ge(ln_ready, 1)
                dve.drain()
                dve.scalar_tensor_tensor(out=t1[:, :], in0=g[:, :], scalar=0.0, in1=t0[:, :], op0=ALU.min,
                                         op1=ALU.subtract)
                dve.drain()
                for d in range(2):
                    in_order(r_lf, t1, 32 * d, 32 + 64 * d, d == 1)
                    in_order(r_i, g, 32 * d, 64 * d, d == 1)
                dve.drain()
                dve.tensor_tensor_scan(b[:, :], ones[:, :], r_lf[:, :], 0.0, ALU.mult, ALU.add)
                dve.drain()
                dve.tensor_tensor(r_lf[:, :], r_i[:, :], b[:, :], ALU.subtract)
                dve.drain()
                dve.tensor_tensor_scan(m[:, :], r_lf[:, :], r_lf[:, :], 0.0, ALU.max, ALU.max)
                dve.tensor_copy(a_out[0:4, :], r_lf[0:4, :])
                for at in (slice(0, CTX), slice(CTX, NTOK)):
                    cp = dve.tensor_copy(a_out[32:36, at], r_lf[32:36, at][:, ::-1])
                cp.then_inc(a_ready, 1)
                dve.drain()
                dve.tensor_tensor(b[:, :], b[:, :], m[:, :], ALU.add)
                dve.tensor_scalar(r_lf[:, :], m[:, :], -1.0, None, ALU.mult)
                dve.drain().then_inc(bm_ready, 1)
                dve.wait_ge(em_ready, 1)
                for q, src in enumerate((r_lf, r_i)):
                    dve.tensor_copy(rows[64 * q:64 * q + 4, :], src[0:4, :])
                    for at in (slice(0, CTX), slice(CTX, NTOK)):
                        cp = dve.tensor_copy(rows[64 * q + 32:64 * q + 36, at], src[32:36, at][:, ::-1])
                cp.then_inc(rows_ready, 1)
                dve.wait_ge(turned, 1)
                for n in range(2):
                    dve.tensor_copy(k["m_cols"][:, 3 * n:3 * n + 3, :, :],
                                    col_ps[n][:, 0:3 * P].rearrange("p (t q c) -> p t q c", t=3, q=4)[:, :, :, 0:4])


def stage_mlstm(nc, a, k, yT):
    DH, KB = ML_DIM, ML_DIM // P
    NU = NT

    def fwd_range(t):
        return (0, (t + 1) * P)

    def bwd_ranges(t):
        if t < CT:
            return [(t * P, CTX)]
        return [(0, NTOK)] if t == CT else [(0, CTX), (t * P, NTOK)]

    def keys_of(t):
        return CT if t < CT else NT

    with Stage(nc, "ml") as s:
        w = [s.sb(f"w{u}", [P, KD, 512]) for u in range(2)]
        cos, sin = s.sb("cos", [P, LT, 2, 64]), s.sb("sin", [P, LT, 2, 64])
        qk, rot = [s.sb(f"qk{u}", [P, 2, DH]) for u in range(2)], s.sb("rot", [P, 2, 2, 64])
        qT, kT = s.sb("qT", [P, KB, NTOK]), s.sb("kT", [P, KB, NTOK])
        v, so, sz = s.sb("v", [P, NT, DH]), s.sb("so", [P, NT, DH]), s.sb("sz", [P, NT, DH])
        ex, rx = s.sb("ex", [P, DH]), s.sb("rx", [P, DH])
        ab = [s.sb(f"ab{d}", [P, NTOK]) for d in range(2)]
        abd = [s.sb(f"abd{d}", [P, NTOK]) for d in range(2)]
        tri = s.sb("tri", [P, 2, P])
        e = [[s.sb(f"e{u}{d}", [P, NTOK]) for d in range(2)] for u in range(2)]
        pT = [s.sb(f"pT{u}", [P, NTOK]) for u in range(2)]
        hcols, hn = s.sb("hcols", [P, NT, 4]), s.sb("hn", [P, KB])
        den, rden = s.sb("den", [P, NU, 2]), s.sb("rden", [P, NU, 2])
        gated, y = [s.sb(f"gated{u}", [P, DH]) for u in range(2)], [s.sb(f"y{u}", [P, DH]) for u in range(2)]
        ss, ms, rstd, half = (s.sb(n, [P, NU]) for n in ("ss", "ms", "rstd", "half"))
        banks = [s.ps(f"bank{n}") for n in range(5)]
        s_ps = s.ps("s_ps", (P, 1024))
        pT_ps = [s.ps("pT_ps"), banks[0]]
        proj, turn_ps, o_ps = banks[0:3], banks[3:5], banks[1:3]

        const_in, a_in = s.sem("const_in"), s.sem("a_in")
        w_in = [s.sem(f"w_in{u}") for u in range(3)]
        (proj_ready, cols_ready, rotated, qk_turned, qk_stored, vo_exp, vo_done, z_exp, z_done, diag_ready,
         scores_ready, exp_ready, den_ready, wb_scaled, w_ready, pT_ready, pT_stored_dve, pT_stored_act, pv_ready,
         gated_ready, squares_ready, means_ready, rstd_ready, y_ready, y_turned, yT_stored) = (s.sem(n) for n in (
             "proj_ready", "cols_ready", "rotated", "qk_turned", "qk_stored", "vo_exp", "vo_done",
             "z_exp", "z_done", "diag_ready", "scores_ready", "exp_ready", "den_ready", "wb_scaled", "w_ready",
             "pT_ready", "pT_stored_dve", "pT_stored_act", "pv_ready", "gated_ready", "squares_ready",
             "means_ready", "rstd_ready", "y_ready", "y_turned", "yT_stored"))

        def h_tile(kk, j):
            return k["hT"][:, kk, j * P:(j + 1) * P]

        with nc.Block() as block:
            @block.sync
            def _(sp):
                sp.dma_start(cos[:, :, :, :], a["rope_cos"]).then_inc(const_in, 16)
                sp.dma_start(sin[:, :, :, :], a["rope_sin"]).then_inc(const_in, 16)
                sp.dma_start(tri[:, :, :], a["tri"]).then_inc(const_in, 16)
                src = a["w_in_ab"][0].rearrange("(k p) n -> p k n", p=P)

                def load(head, piece):
                    parts = ((4, 5), (6, 7), (8,))[piece]
                    for n, x in enumerate(parts):
                        sp.dma_start(w[piece % 2][:, :, n * DH:(n + 1) * DH],
                                     src[:, :, bass.ds(head * DH + x * D, DH)]).then_inc(w_in[piece], 16)

                def load_a(head):
                    for d in range(2):
                        sp.dma_start(ab[d][:, :], k["a_rows"][d, bass.ds(head, 1), :].to_broadcast([P, NTOK]))\
                            .then_inc(a_in, 16)

                load(0, 0)
                load(0, 1)
                load_a(0)
                with sp.Fori(0, ML_HEADS - 1) as i:
                    sp.wait_ge(proj_ready, i * 18 + NT)
                    load(i, 2)
                    sp.wait_ge(proj_ready, i * 18 + 2 * NT)
                    load(i + 1, 1)
                    sp.wait_ge(proj_ready, i * 18 + 3 * NT)
                    load(i + 1, 0)
                    sp.wait_ge(exp_ready, i * NU + NU)
                    load_a(i + 1)
                sp.wait_ge(proj_ready, (ML_HEADS - 1) * 18 + NT)
                load(ML_HEADS - 1, 2)

            @block.tensor
            def _(pe):
                with pe.Fori(0, ML_HEADS) as i:
                    def project(j, u, width):
                        for kk in range(KD):
                            mm = pe.matmul(proj[j % 3][:, 0:width], h_tile(kk, j), w[u][:, kk, 0:width],
                                           start=kk == 0, stop=kk == KD - 1)
                        mm.then_inc(proj_ready, 1)

                    def turn_qk(j):
                        pe.wait_ge(rotated, i * NT + (j + 1))
                        if j >= 2:
                            pe.wait_ge(qk_stored, i * NT + (j - 1))
                        for x in range(2):
                            for b in range(KB):
                                tr = pe.transpose(turn_ps[j % 2][:, (2 * x + b) * P:(2 * x + b + 1) * P],
                                                  qk[j % 2][:, x, b * P:(b + 1) * P], k["ident"][:, :])
                        tr.then_inc(qk_turned, 1)

                    pe.wait_ge(w_in[0], i * 32 + 32)
                    for j in range(NT):
                        if j >= 3:
                            pe.wait_ge(rotated, i * NT + (j - 2))
                        project(j, 0, 512)
                        if j >= 2:
                            turn_qk(j - 2)
                    pe.wait_ge(w_in[1], i * 32 + 32)
                    for j in range(NT):
                        if j < 3:
                            pe.wait_ge(rotated, i * NT + (j + 4))
                        else:
                            pe.wait_ge(vo_exp, i * NT + (j - 2))
                        project(j, 1, 512)
                        if j < 2:
                            turn_qk(j + 4)
                    pe.wait_ge(w_in[2], i * 16 + 16)
                    for j in range(NT):
                        if j < 3:
                            pe.wait_ge(vo_exp, i * NT + (j + 4))
                        else:
                            pe.wait_ge(z_done, i * NT + (j - 2))
                        project(j, 0, 256)
                    pe.wait_ge(qk_stored, i * NT + NT)
                    pe.wait_ge(z_done, i * NT + NT)
                    for n in range(NU + 4):
                        if n < NU:
                            if n >= 1:
                                pe.wait_ge(den_ready, i * NU + n)
                            for c0 in range(0, keys_of(n) * P, 512):
                                c1 = min(c0 + 512, keys_of(n) * P)
                                for b in range(KB):
                                    mm = pe.matmul(s_ps[:, c0:c1], qT[:, b, n * P:(n + 1) * P], kT[:, b, c0:c1],
                                                   start=b == 0, stop=b == KB - 1)
                            mm.then_inc(scores_ready, 1)
                        if 2 <= n < NU + 2:
                            pe.wait_ge(pT_stored_dve, i * NU + (n - 1))
                            pe.wait_ge(pT_stored_act, i * NU + (n - 1))
                        if 1 <= n <= NU:
                            t = n - 1
                            pe.wait_ge(w_ready, i * NU + n)
                            for b in range(keys_of(t)):
                                src = e[t % 2][1 if b > t else 0]
                                hf = keys_of(t) // 2
                                tr = pe.transpose(pT_ps[b // hf][:, b % hf * P:b % hf * P + P],
                                                  src[:, b * P:(b + 1) * P], k["ident"][:, :])
                            tr.then_inc(pT_ready, 1)
                        if 2 <= n < NU + 2:
                            t = n - 2
                            for b in range(keys_of(t)):
                                mm = pe.matmul(o_ps[t % 2][:, 0:DH], pT[t % 2][:, b * P:(b + 1) * P], v[:, b, :],
                                               start=b == 0, stop=b == keys_of(t) - 1)
                            mm.then_inc(pv_ready, 1)
                        if n >= 4:
                            t = n - 4
                            pe.wait_ge(y_ready, i * NU + (t + 1))
                            if t >= 2:
                                pe.wait_ge(yT_stored, i * NU + (t - 1))
                            for b in range(KB):
                                tr = pe.transpose(turn_ps[t % 2][:, b * P:(b + 1) * P], y[t % 2][:, b * P:(b + 1) * P],
                                                  k["ident"][:, :])
                            tr.then_inc(y_turned, 1)
                    pe.wait_ge(yT_stored, i * NU + NU)

            @block.scalar
            def _(act):
                with act.Fori(0, ML_HEADS) as i:
                    def store_qk(j):
                        at = slice(SEQ_TILE[j] * P, SEQ_TILE[j] * P + P)
                        ps = turn_ps[j % 2][:, :].rearrange("p (x b c) -> p x b c", x=2, b=KB)
                        act.wait_ge(qk_turned, i * NT + (j + 1))
                        act.activation(qT[:, :, at], ps[:, 0], ACT.Copy)
                        act.activation(kT[:, :, at], ps[:, 1], ACT.Copy, scale=DH ** -0.5).then_inc(qk_stored, 1)

                    for j in range(NT):
                        store_qk(j)
                    for j in range(NT):
                        act.wait_ge(proj_ready, i * 18 + (NT + j + 1))
                        act.activation(v[:, SEQ_TILE[j], :], proj[j % 3][:, 0:DH], ACT.Copy)
                        if j >= 1:
                            act.wait_ge(vo_done, i * NT + j)
                        act.activation(ex[:, :], proj[j % 3][:, DH:2 * DH], ACT.Exp, scale=-1.0).then_inc(vo_exp, 1)
                    act.wait_ge(vo_done, i * NT + NT)
                    for j in range(NT):
                        act.wait_ge(proj_ready, i * 18 + (2 * NT + j + 1))
                        if j >= 1:
                            act.wait_ge(z_done, i * NT + j)
                        act.activation(ex[:, :], proj[j % 3][:, 0:DH], ACT.Exp, scale=-1.0).then_inc(z_exp, 1)
                    act.wait_ge(cols_ready, i + 1)
                    act.wait_ge(diag_ready, i * 2 + 2)
                    for n in range(NU + 4):
                        if n < NU:
                            if n >= 2:
                                act.wait_ge(pT_ready, i * NU + (n - 1))
                            st, dg = n, slice(n * P, (n + 1) * P)
                            for d, ranges in enumerate(([fwd_range(n)], bwd_ranges(n))):
                                bias = hcols[:, n, d:d + 1]
                                for lo, hi in ranges:
                                    for c0, c1, src in ((lo, min(hi, n * P), ab[d]),
                                                        (max(lo, n * P), min(hi, (n + 1) * P), abd[d]),
                                                        (max(lo, (n + 1) * P), hi, ab[d])):
                                        if c0 < c1:
                                            act.activation(e[n % 2][d][:, c0:c1], src[:, c0:c1], ACT.Exp, bias=bias)
                            act.drain().then_inc(exp_ready, 1)
                            act.wait_ge(den_ready, i * NU + (n + 1))
                            for lo, hi in bwd_ranges(n):
                                act.activation(e[n % 2][1][:, lo:hi], e[n % 2][1][:, lo:hi], ACT.Copy,
                                               scale=rden[:, n, 1:2])
                            act.drain().then_inc(wb_scaled, 1)
                        if 1 <= n <= NU:
                            t = n - 1
                            hf = keys_of(t) // 2
                            act.wait_ge(pT_ready, i * NU + n)
                            act.activation(pT[t % 2][:, hf * P:2 * hf * P], pT_ps[1][:, 0:hf * P], ACT.Copy)\
                                .then_inc(pT_stored_act, 1)
                        if 2 <= n < NU + 2:
                            t = n - 2
                            act.wait_ge(gated_ready, i * NU + (t + 1))
                            act.activation(ex[:, :], gated[t % 2][:, :], ACT.Square, accum_out=ss[:, t:t + 1])\
                                .then_inc(squares_ready, 1)
                        if n >= 4:
                            t = n - 4
                            act.wait_ge(y_turned, i * NU + (t + 1))
                            act.sem_inc(k["apart"], 1)
                            tok = (t - CT) * P if t >= CT else SEQ + t * P
                            for b in range(KB):
                                st_ = act.activation(yT[:, bass.ds(i * KB + (KD + b), 1), tok:tok + P].squeeze(1),
                                                     turn_ps[t % 2][:, b * P:(b + 1) * P], ACT.Copy,
                                                     scale=hn[:, b:b + 1])
                            st_.then_inc(yT_stored, 1)

            @block.gpsimd
            def _(pool):
                pool.memset(half[:, :], -0.5)
                pool.wait_ge(const_in, 48)
                with pool.Fori(0, ML_HEADS) as i:
                    pool.wait_ge(a_in, i * 32 + 32)
                    pool.sem_inc(k["apart"], 1)
                    for d in range(2):
                        pool.tensor_tensor(abd[d][:, :].rearrange("p (t c) -> p t c", c=P),
                                           ab[d][:, :].rearrange("p (t c) -> p t c", c=P),
                                           tri[:, d, :].unsqueeze(1).to_broadcast([P, NT, P]), ALU.add)\
                            .then_inc(diag_ready, 1)
                    for t in range(NU):
                        pool.wait_ge(means_ready, i * NU + (t + 1))
                        pool.tensor_tensor(rstd[:, t:t + 1], ms[:, t:t + 1], half[:, 0:1], ALU.pow)\
                            .then_inc(rstd_ready, 1)

            @block.vector
            def _(dve):
                dve.wait_ge(const_in, 48)
                with dve.Fori(0, ML_HEADS) as i:
                    for j in range(NT):
                        dve.wait_ge(proj_ready, i * 18 + (j + 1))
                        if j >= 2:
                            dve.wait_ge(qk_turned, i * NT + (j - 1))
                        if j >= LT:
                            dve.tensor_copy(qk[j % 2][:, :, :], proj[j % 3][:, :].rearrange("p (x d) -> p x d", x=2))\
                                .then_inc(rotated, 1)
                            continue
                        for x in range(2):
                            src = proj[j % 3][:, x * DH:(x + 1) * DH].rearrange("p (h r f) -> p h r f", h=2, r=2)
                            dst = qk[j % 2][:, x, :].rearrange("p (h r f) -> p h r f", h=2, r=2)
                            dve.tensor_tensor(dst, src, cos[:, j, :, :].unsqueeze(2).to_broadcast([P, 2, 2, 64]), ALU.mult)
                            for r in range(2):
                                dve.tensor_tensor(rot[:, :, r, :], src[:, :, 1 - r, :], sin[:, j, :, :], ALU.mult)
                            dve.drain()
                            for r, op in enumerate((ALU.subtract, ALU.add)):
                                last = dve.tensor_tensor(dst[:, :, r, :], dst[:, :, r, :], rot[:, :, r, :], op)
                            if x == 0:
                                dve.drain()
                        last.then_inc(rotated, 1)
                        dve.drain()
                    for j in range(NT):
                        dve.wait_ge(vo_exp, i * NT + (j + 1))
                        dve.tensor_scalar(rx[:, :], ex[:, :], 1.0, None, ALU.add).then_inc(vo_done, 1)
                        dve.drain()
                        dve.reciprocal(so[:, SEQ_TILE[j], :], rx[:, :])
                        dve.drain()
                    dve.tensor_copy(hcols[:, :, :], k["m_cols"][:, :, :, bass.ds(i, 1)].squeeze(3))
                    dve.tensor_copy(hn[:, :], k["vecT"][:, bass.ds(i * KB + ROW["h_norm_b"], KB)]).then_inc(cols_ready, 1)
                    for j in range(NT):
                        dve.wait_ge(z_exp, i * NT + (j + 1))
                        dve.tensor_scalar(rx[:, :], ex[:, :], 1.0, None, ALU.add)
                        dve.drain()
                        dve.reciprocal(sz[:, SEQ_TILE[j], :], rx[:, :])
                        dve.drain()
                        dve.tensor_tensor(sz[:, SEQ_TILE[j], :], proj[j % 3][:, 0:DH], sz[:, SEQ_TILE[j], :], ALU.mult)\
                            .then_inc(z_done, 1)
                    for n in range(NU + 3):
                        if n >= 3:
                            t = n - 3
                            dve.wait_ge(squares_ready, i * NU + (t + 1))
                            dve.tensor_scalar(ms[:, t:t + 1], ss[:, t:t + 1], 1.0 / DH, EPS, ALU.mult, ALU.add)\
                                .then_inc(means_ready, 1)
                        if n < NU:
                            ef, eb = e[n % 2]
                            dve.wait_ge(exp_ready, i * NU + (n + 1))
                            dve.wait_ge(scores_ready, i * NU + (n + 1))
                            lo, hi = fwd_range(n)
                            dve.tensor_tensor_reduce(ef[:, lo:hi], s_ps[:, lo:hi], ef[:, lo:hi], 1.0, 0.0, ALU.mult,
                                                     ALU.add, den[:, n, 0:1])
                            for x, (lo, hi) in enumerate(bwd_ranges(n)):
                                if x:
                                    dve.drain()
                                dve.tensor_tensor_reduce(eb[:, lo:hi], s_ps[:, lo:hi], eb[:, lo:hi], 1.0,
                                                         den[:, n, 1:2] if x else 0.0, ALU.mult, ALU.add,
                                                         den[:, n, 1:2])
                            dve.drain()
                            dve.scalar_tensor_tensor(out=den[:, n, :], in0=den[:, n, :], scalar=-1.0,
                                                     in1=den[:, n, :], op0=ALU.mult, op1=ALU.max)
                            dve.drain()
                            dve.tensor_tensor(den[:, n, :], den[:, n, :], hcols[:, n, 2:4], ALU.max)
                            dve.drain()
                            dve.reciprocal(rden[:, n, :], den[:, n, :]).then_inc(den_ready, 1)
                            dve.drain()
                            dve.wait_ge(wb_scaled, i * NU + (n + 1))
                            both = [(n * P, (n + 1) * P)] if n < CT else (
                                [(0, CTX), (n * P, (n + 1) * P)])
                            for lo, hi in both:
                                dve.scalar_tensor_tensor(out=ef[:, lo:hi], in0=ef[:, lo:hi], scalar=rden[:, n, 0:1],
                                                         in1=eb[:, lo:hi], op0=ALU.mult, op1=ALU.add)
                            lo, hi = (0, n * P) if n < CT else (CTX, n * P)
                            if lo < hi:
                                dve.tensor_scalar(ef[:, lo:hi], ef[:, lo:hi], rden[:, n, 0:1], None, ALU.mult)
                            dve.drain().then_inc(w_ready, 1)
                        if 1 <= n <= NU:
                            t = n - 1
                            hf = keys_of(t) // 2
                            dve.wait_ge(pT_ready, i * NU + n)
                            dve.tensor_copy(pT[t % 2][:, 0:hf * P], pT_ps[0][:, 0:hf * P]).then_inc(pT_stored_dve, 1)
                        if 2 <= n < NU + 2:
                            t = n - 2
                            dve.wait_ge(pv_ready, i * NU + (t + 1))
                            dve.tensor_tensor(gated[t % 2][:, :], o_ps[t % 2][:, 0:DH], so[:, t, :], ALU.mult)\
                                .then_inc(gated_ready, 1)
                        if n >= 3:
                            t = n - 3
                            if t >= 2:
                                dve.wait_ge(y_turned, i * NU + (t - 1))
                            dve.wait_ge(rstd_ready, i * NU + (t + 1))
                            dve.scalar_tensor_tensor(out=y[t % 2][:, :], in0=gated[t % 2][:, :], scalar=rstd[:, t:t + 1],
                                                     in1=sz[:, t, :], op0=ALU.mult, op1=ALU.mult).then_inc(y_ready, 1)
                            dve.drain()


def stage_output(nc, k, name, lhs, w_dram, chunks, tiles, gates, dst=None):
    NW = 256
    with Stage(nc, name) as s:
        w = [s.sb(f"w{u}", [P, chunks, NW]) for u in range(2)]
        ones, diag = s.sb("ones", [P, P]), s.sb("diag", [P, len(gates), KD, P])
        gate = s.sb("gate", [P, len(gates), D])
        t = [s.sb(f"t{u}", [P, NW]) for u in range(2)]
        banks = [s.ps(f"bank{n}") for n in range(4)]
        w_in = [s.sem(f"w_in{u}") for u in range(2)]
        diag_ready, spread, stored, products_ready, added = (
            s.sem(n) for n in ("diag_ready", "spread", "stored", "products_ready", "added"))
        n_t = len(tiles)
        half = KD // 2
        with nc.Block() as block:
            @block.sync
            def _(sp):
                src = w_dram.rearrange("(k p) n -> p k n", p=P)
                for u in range(2):
                    sp.dma_start(w[u][:, :, :], src[:, :, u * NW:(u + 1) * NW]).then_inc(w_in[u], 16)
                for u in range(2):
                    sp.wait_ge(products_ready, n_t * (u + 1))
                    sp.dma_start(w[u][:, :, :], src[:, :, (u + 2) * NW:(u + 3) * NW]).then_inc(w_in[u], 16)

            @block.tensor
            def _(pe):
                pe.wait_ge(diag_ready, 1)
                for g in range(len(gates)):
                    for h in range(2):
                        n = 2 * g + h
                        pe.matmul(banks[n % 4][:, :], ones[:, :], diag[:, g, h * half:(h + 1) * half, :],
                                  start=True, stop=True).then_inc(spread, 1)
                pe.wait_ge(stored, 2 * len(gates))
                with pe.Fori(0, 2) as i:
                    for u in range(2):
                        pe.wait_ge(w_in[u], i * 16 + 16)
                        for x, j in enumerate(tiles):
                            pe.wait_ge(added, i * (2 * n_t) + (u * n_t + x + 1))
                            bank = banks[(u * n_t + x) % 4]
                            for c in range(chunks):
                                mm = pe.matmul(bank[:, 0:NW], lhs(c, j), w[u][:, c, :],
                                               start=c == 0, stop=c == chunks - 1)
                            mm.then_inc(products_ready, 1)

            @block.vector
            def _(dve):
                dve.memset(ones[:, :], 1.0)
                for g, (mod, v, _, _) in enumerate(gates):
                    dve.tensor_tensor(diag[:, g, :, :], k["ident"][:, :].unsqueeze(1).to_broadcast([P, KD, P]),
                                      k["modT"][:, mod:mod + KD, v:v + 1].to_broadcast([P, KD, P]), ALU.mult)
                dve.drain().then_inc(diag_ready, 1)
                for n in range(2 * len(gates)):
                    dve.wait_ge(spread, n + 1)
                    dve.tensor_copy(gate[:, n // 2, (n % 2) * 512:(n % 2) * 512 + 512], banks[n % 4][:, :])\
                        .then_inc(stored, 1)
                for _ in range(4):
                    dve.drain().then_inc(added, 1)
                with dve.Fori(0, 2) as i:
                    for u in range(2):
                        for x, j in enumerate(tiles):
                            g = [n for n, (_, _, t0, nt) in enumerate(gates) if t0 <= j < t0 + nt][0]
                            at = bass.ds(i * (2 * NW) + u * NW, NW)
                            dve.wait_ge(products_ready, i * (2 * n_t) + (u * n_t + x + 1))
                            dve.tensor_tensor(t[x % 2][:, :], banks[(u * n_t + x) % 4][:, 0:NW], gate[:, g, at], ALU.mult)\
                                .then_inc(added, 1)
                            dve.drain()
                            dve.tensor_tensor(k["xs"][:, j, at], k["xs"][:, j, at], t[x % 2][:, :], ALU.add)
                            dve.drain()


def stage_gla(nc, a, k, yT):
    SMALL = [w for w in HG_LEVELS if w < P]
    NL = len(HG_LEVELS)
    with Stage(nc, "gla") as s:
        wf, w = s.sb("wf", [P, KD, 2, P]), s.sb("w", [P, KD, 3, P])
        lbh, hn, tiny, half = s.sb("lbh", [P, 2]), s.sb("hn", [P, 1]), s.sb("tiny", [P, 1]), s.sb("half", [P, LT])
        f = [s.sb("f_ctx", [P, 2, CTX]), s.sb("f_fwd", [P, SEQ]), s.sb("f_bwd", [P, SEQ])]
        u = [s.sb("u_ctx", [P, 2, CTX]), s.sb("u_fwd", [P, SEQ]), s.sb("u_bwd", [P, SEQ])]
        kk_ = [s.sb("k_ctx", [P, 2, CTX]), s.sb("k_fwd", [P, SEQ]), s.sb("k_bwd", [P, SEQ])]
        q, eq, uq, kd0 = (s.sb(n, [P, SEQ]) for n in ("q", "eq", "uq", "kd0"))
        arr = [s.sb(f"arr{d}", [P, SEQ + 1]) for d in range(2)]
        arc = [s.sb(f"arc{d}", [P, CTX + 1]) for d in range(2)]
        ones = s.sb("ones", [P, SEQ])
        xy = [s.sb(f"xy{n}", [P, 2, SEQ]) for n in range(2)]
        qk = [s.sb(f"qk{n}", [P, 2, SEQ]) for n in range(2)]
        xq, xc = s.sb("xq", [P, 2, SEQ]), s.sb("xc", [P, 2, CTX])
        masks = s.sb("masks", [P, len(SMALL), P], I32)
        own, near, far = s.sb("own", [P, SEQ]), s.sb("near", [P, SEQ]), s.sb("far", [P, LT, 2 * P])
        v, zs = s.sb("v", [P, NT, P]), s.sb("zs", [P, LT, P])
        ez, uz, rz = s.sb("ez", [P, P]), s.sb("uz", [P, P]), s.sb("rz", [P, P])
        kdT, st = s.sb("kdT", [P, 4, P]), s.sb("st", [P, 2, P])
        ss, ms, rstd = s.sb("ss", [P, LT]), s.sb("ms", [P, LT]), s.sb("rstd", [P, LT])
        sq, y = s.sb("sq", [P, P]), s.sb("y", [P, LT, P])
        b = [s.ps(f"bank{n}") for n in range(8)]
        f_ps, q_ps, iz_ps = [b[4], b[5], b[1]], b[0], [b[4], b[5], b[6], b[7]]
        IZ = [*range(LT, NT), *range(LT)]

        def iz_bank(m):
            return iz_ps[m if m < 2 else 2 + m % 2]

        wf_in, w_in, const_in, pool_consts = s.sem("wf_in"), s.sem("w_in"), s.sem("const_in"), s.sem("pool_consts")
        (f_ready, q_ready, iz_ready, ef_ready, eq_ready, iz_exp, iz_used, f_stored, k_stored, lf_stored, sums_ready,
         q_stored, xy_ready, xy_exp, qk_ready, level_ready, own_stored, near_stored, far_stored, xc_ready, xc_exp,
         kd_ready, kd_turned, kdT_stored, st_ready, st_stored, xq_ready, xq_exp, qp_ready, o_ready, squares_ready,
         means_ready, rstd_ready, y_ready, y_turned, yT_stored, k_diag) = (s.sem(n) for n in (
             "f_ready", "q_ready", "iz_ready", "ef_ready", "eq_ready", "iz_exp", "iz_used", "f_stored", "k_stored",
             "lf_stored", "sums_ready", "q_stored", "xy_ready", "xy_exp", "qk_ready", "level_ready", "own_stored",
             "near_stored", "far_stored", "xc_ready", "xc_exp", "kd_ready", "kd_turned", "kdT_stored", "st_ready",
             "st_stored", "xq_ready", "xq_exp", "qp_ready", "o_ready", "squares_ready", "means_ready", "rstd_ready",
             "y_ready", "y_turned", "yT_stored", "k_diag"))

        def halves(x, wd):
            return x.rearrange("p (n h w) -> p n h w", h=2, w=wd)

        with nc.Block() as block:
            @block.sync
            def _(sp):
                sp.dma_start(masks[:, :, :], a["level_masks"]).then_inc(const_in, 16)
                src = a["w_in_c"][0].rearrange("(k p) n -> p k n", p=P)

                def load_f(head):
                    for x in range(2):
                        sp.dma_start(wf[:, :, x, :], src[:, :, bass.ds(head * P + (1 + x) * INNER, P)])\
                            .then_inc(wf_in, 16)

                def load(head):
                    for n, x in enumerate((0, 3, 4)):
                        sp.dma_start(w[:, :, n, :], src[:, :, bass.ds(head * P + x * INNER, P)]).then_inc(w_in, 16)

                load_f(0)
                load(0)
                with sp.Fori(0, HG_HEADS - 1) as i:
                    sp.wait_ge(f_ready, i * 3 + 3)
                    sp.sem_inc(k["apart"], 1)
                    load_f(i + 1)
                    sp.wait_ge(iz_ready, i * NT + NT)
                    sp.sem_inc(k["apart"], 1)
                    load(i + 1)

            @block.tensor
            def _(pe):
                def project(out, weights, x, c0, n):
                    for c in range(KD):
                        mm = pe.matmul(out, weights[:, c, x, :], k["hT"][:, c, c0:c0 + n], start=c == 0, stop=c == KD - 1)
                    return mm

                def project_f(head, g):
                    if g == 0:
                        pe.wait_ge(wf_in, head * 32 + 32)
                        for x in range(2):
                            mm = project(f_ps[0][:, x * CTX:(x + 1) * CTX], wf, x, SEQ, CTX)
                        mm.then_inc(f_ready, 1)
                    else:
                        project(f_ps[g][:, :], wf, g - 1, 0, SEQ).then_inc(f_ready, 1)

                for g in range(3):
                    project_f(0, g)

                def turn(i, last=False):
                    pe.wait_ge(w_in, i * 48 + 48)
                    project(q_ps[:, :], w, 0, 0, SEQ).then_inc(q_ready, 1)

                    def project_iz(m):
                        j = IZ[m]
                        n = 2 * P if j < LT else P
                        if m >= 4:
                            pe.wait_ge(iz_used, i * NT + (m - 1))
                        for c in range(KD):
                            mm = pe.matmul(iz_bank(m)[:, 0:n], k["hT"][:, c, j * P:(j + 1) * P],
                                           w[:, c, 1:1 + n // P, :], start=c == 0, stop=c == KD - 1)
                        mm.then_inc(iz_ready, 1)

                    pe.wait_ge(ef_ready, i * 3 + 3)
                    project_iz(0)
                    project_iz(1)
                    pe.wait_ge(kd_ready, i * 2 + 2)
                    pe.wait_ge(iz_used, i * NT + CT)
                    for d in range(2):
                        for t in range(CT):
                            tr = pe.transpose(b[4][:, (2 * d + t) * P:(2 * d + t + 1) * P],
                                              kk_[0][:, d, t * P:(t + 1) * P], k["ident"][:, :])
                    tr.then_inc(kd_turned, 1)
                    for n in range(len(SMALL) + 1):
                        if n == 0:
                            pe.wait_ge(k_diag, i + 1)
                            pe.wait_ge(q_stored, i + 1)
                            kl, ql = kd0, q
                        else:
                            pe.wait_ge(qk_ready, i * NL + n)
                            kl, ql = qk[(n - 1) % 2][:, 1, :], qk[(n - 1) % 2][:, 0, :]
                        if n >= 2:
                            pe.wait_ge(own_stored, i * (len(SMALL) + 1) + (n - 1))
                        for t in range(LT):
                            at = slice(t * P, (t + 1) * P)
                            mm = pe.matmul(b[n % 2][:, at], kl[:, at], ql[:, at], start=True, stop=True)
                        mm.then_inc(level_ready, 1)
                        if n == 1:
                            pe.wait_ge(kdT_stored, i + 1)
                            for d in range(2):
                                for t in range(CT):
                                    mm = pe.matmul(b[5][:, d * P:(d + 1) * P], kdT[:, 2 * d + t, :], v[:, LT + t, :],
                                                   start=t == 0, stop=t == CT - 1)
                            mm.then_inc(st_ready, 1)
                        if n % 2 == 1:
                            project_iz(CT + n // 2)
                    pe.wait_ge(qk_ready, i * NL + len(SMALL) + 1)
                    x = qk[len(SMALL) % 2]
                    pe.wait_ge(own_stored, i * (len(SMALL) + 1) + len(SMALL))
                    for t in range(LT):
                        o = t ^ 1
                        mm = pe.matmul(b[0][:, t * P:(t + 1) * P], x[:, 1, o * P:(o + 1) * P], x[:, 0, t * P:(t + 1) * P],
                                       start=True, stop=True)
                    mm.then_inc(level_ready, 1)
                    pe.wait_ge(qk_ready, i * NL + len(SMALL) + 2)
                    x = qk[(len(SMALL) + 1) % 2]
                    for t in range(LT):
                        to = 2 * P if t < 2 else 0
                        mm = pe.matmul(b[2 + t // 2][:, t % 2 * 256:t % 2 * 256 + 256], x[:, 1, t * P:(t + 1) * P],
                                       x[:, 0, to:to + 256], start=True, stop=True)
                    mm.then_inc(level_ready, 1)
                    pe.wait_ge(st_stored, i + 1)
                    if not last:
                        project_f(i + 1, 0)
                    pe.wait_ge(qp_ready, i * 2 + 2)
                    pe.wait_ge(own_stored, i * (len(SMALL) + 1) + len(SMALL) + 1)
                    pe.wait_ge(near_stored, i + 1)
                    pe.wait_ge(far_stored, i + 1)
                    pe.wait_ge(iz_used, i * NT + NT)
                    for t in range(LT):
                        at = slice(t * P, (t + 1) * P)
                        s0 = 2 if t < 2 else 0
                        fc = slice(t % 2 * P, t % 2 * P + P)
                        parts = [(own[:, at], v[:, t, :]), (near[:, at], v[:, t ^ 1, :]),
                                 (far[:, s0, fc], v[:, s0, :]), (far[:, s0 + 1, fc], v[:, s0 + 1, :]),
                                 (xq[:, 0, at], st[:, 0, :]), (xq[:, 1, at], st[:, 1, :])]
                        for n, (l, r) in enumerate(parts):
                            mm = pe.matmul(b[6][:, at], l, r, start=n == 0, stop=n == len(parts) - 1)
                    mm.then_inc(o_ready, 1)
                    if not last:
                        project_f(i + 1, 1)
                    pe.wait_ge(y_ready, i + 1)
                    for t in range(LT):
                        tr = pe.transpose(b[7][:, t * P:(t + 1) * P], y[:, t, :], k["ident"][:, :])
                    tr.then_inc(y_turned, 1)
                    if not last:
                        project_f(i + 1, 2)

                with pe.Fori(0, HG_HEADS - 1) as i:
                    turn(i)
                turn(HG_HEADS - 1, last=True)

            @block.scalar
            def _(act):
                act.wait_ge(pool_consts, 1)

                def take_f(head, g):
                    act.wait_ge(f_ready, head * 3 + (g + 1))
                    act.activation(u[g][:, :, :] if g == 0 else u[g][:, :],
                                   f_ps[g][:, :].rearrange("p (d t) -> p d t", d=2) if g == 0 else f_ps[g][:, :],
                                   ACT.Exp, scale=-1.0).then_inc(ef_ready, 1)

                for g in range(3):
                    take_f(0, g)

                def turn(i, last=False):
                    act.wait_ge(q_ready, i + 1)
                    act.activation(eq[:, :], q_ps[:, :], ACT.Exp, scale=-1.0).then_inc(eq_ready, 1)
                    for g in range(3):
                        act.wait_ge(f_stored, i * 3 + (g + 1))
                        fx = f[g][:, :, :] if g == 0 else f[g][:, :]
                        ux = u[g][:, :, :] if g == 0 else u[g][:, :]
                        act.activation(ux, fx, ACT.Ln, bias=tiny[:, 0:1]).then_inc(lf_stored, 1)

                    def take_iz(m):
                        j = IZ[m]
                        act.wait_ge(iz_ready, i * NT + (m + 1))
                        cp = act.activation(v[:, j, :], iz_bank(m)[:, 0:P], ACT.Copy)
                        if j < LT:
                            if j >= 1:
                                act.wait_ge(iz_used, i * NT + m)
                            act.activation(ez[:, :], iz_bank(m)[:, P:2 * P], ACT.Exp, scale=-1.0)
                            act.drain()
                            act.activation(uz[:, :], ez[:, :], ACT.Ln, bias=1.0)
                            act.drain()
                            act.activation(rz[:, :], uz[:, :], ACT.Exp, scale=-1.0).then_inc(iz_exp, 1)
                        else:
                            cp.then_inc(iz_exp, 1)

                    take_iz(0)
                    take_iz(1)
                    act.wait_ge(xc_ready, i + 1)
                    act.activation(xc[:, :, :], xc[:, :, :], ACT.Exp).then_inc(xc_exp, 1)
                    act.wait_ge(xq_ready, i + 1)
                    act.activation(xq[:, :, :], xq[:, :, :], ACT.Exp).then_inc(xq_exp, 1)
                    for n in range(NL):
                        act.wait_ge(xy_ready, i * NL + (n + 1))
                        act.activation(xy[n % 2][:, :, :], xy[n % 2][:, :, :], ACT.Exp).then_inc(xy_exp, 1)
                        if n == 1:
                            act.wait_ge(kd_turned, i + 1)
                            act.activation(kdT[:, :, :], b[4][:, :].rearrange("p (x c) -> p x c", x=4), ACT.Copy)\
                                .then_inc(kdT_stored, 1)
                        if n >= 2 and n % 2 == 0:
                            take_iz(CT + n // 2 - 1)
                        if n == 3:
                            act.wait_ge(st_ready, i + 1)
                            act.activation(st[:, :, :], b[5][:, 0:2 * P].rearrange("p (x c) -> p x c", x=2), ACT.Copy)\
                                .then_inc(st_stored, 1)
                    act.wait_ge(level_ready, i * (NL + 1) + (NL + 1))
                    for h in range(2):
                        fs = act.activation(far[:, 2 * h:2 * h + 2, :], b[2 + h][:, :].rearrange("p (x c) -> p x c", x=2),
                                            ACT.Copy)
                    fs.then_inc(far_stored, 1)
                    if not last:
                        take_f(i + 1, 0)
                    act.wait_ge(o_ready, i + 1)
                    for t in range(LT):
                        act.activation(sq[:, :], b[6][:, t * P:(t + 1) * P], ACT.Square, accum_out=ss[:, t:t + 1])
                        act.drain()
                    act.drain().then_inc(squares_ready, 1)
                    if not last:
                        take_f(i + 1, 1)
                    act.wait_ge(y_turned, i + 1)
                    act.sem_inc(k["apart"], 1)
                    act.activation(yT[:, bass.ds(i, 1), 0:SEQ].squeeze(1), b[7][:, :], ACT.Copy, scale=hn[:, 0:1])\
                        .then_inc(yT_stored, 1)
                    if not last:
                        take_f(i + 1, 2)

                with act.Fori(0, HG_HEADS - 1) as i:
                    turn(i)
                turn(HG_HEADS - 1, last=True)

            @block.gpsimd
            def _(pool):
                pool.memset(half[:, :], -0.5)
                pool.memset(tiny[:, :], 2.0 ** -64)
                pool.memset(ones[:, :], 1.0)
                for x in (*arr, *arc):
                    pool.memset(x[:, 0:1], 0.0)
                pool.drain().then_inc(pool_consts, 1)
                with pool.Fori(0, HG_HEADS) as i:
                    for g in range(3):
                        pool.wait_ge(f_stored, i * 3 + (g + 1))
                        pool.sem_inc(k["apart"], 1)
                        fx = f[g][:, :, :] if g == 0 else f[g][:, :]
                        kx = kk_[g][:, :, :] if g == 0 else kk_[g][:, :]
                        pool.tensor_scalar(kx, fx, -1.0, 1.0, ALU.mult, ALU.add).then_inc(k_stored, 1)
                    pool.drain()
                    pool.tensor_tensor(kd0[:, :], kk_[1][:, :], kk_[2][:, :], ALU.add).then_inc(k_diag, 1)
                    pool.wait_ge(sums_ready, i * 4 + 2)
                    pool.tensor_tensor(xc[:, 0, :], arc[0][:, CTX:CTX + 1].to_broadcast([P, CTX]), arc[0][:, 1:CTX + 1],
                                       ALU.subtract)
                    pool.tensor_copy(xc[:, 1, :], arc[1][:, 0:CTX])
                    pool.drain().then_inc(xc_ready, 1)
                    pool.wait_ge(sums_ready, i * 4 + 4)
                    pool.tensor_tensor(xq[:, 1, :], arr[1][:, SEQ:SEQ + 1].to_broadcast([P, SEQ]), arr[1][:, 0:SEQ],
                                       ALU.subtract)
                    pool.tensor_copy(xq[:, 0, :], arr[0][:, 1:SEQ + 1])
                    pool.drain().then_inc(xq_ready, 1)
                    for n, wd in enumerate(HG_LEVELS):
                        if n >= 2:
                            pool.wait_ge(qk_ready, i * NL + (n - 1))
                        nb = SEQ // (2 * wd)
                        pf, ef = halves(arr[0][:, 1:SEQ + 1], wd), halves(arr[0][:, 0:SEQ], wd)
                        eb = halves(arr[1][:, 0:SEQ], wd)
                        rf, rb = (e[:, :, 1, 0:1].to_broadcast([P, nb, wd]) for e in (ef, eb))
                        x, yb = halves(xy[n % 2][:, 0, :], wd), halves(xy[n % 2][:, 1, :], wd)
                        pool.tensor_tensor(x[:, :, 0, :], rf, pf[:, :, 0, :], ALU.subtract)
                        pool.tensor_tensor(x[:, :, 1, :], pf[:, :, 1, :], rf, ALU.subtract)
                        pool.tensor_tensor(yb[:, :, 0, :], rb, eb[:, :, 0, :], ALU.subtract)
                        pool.tensor_tensor(yb[:, :, 1, :], eb[:, :, 1, :], rb, ALU.subtract)
                        pool.drain().then_inc(xy_ready, 1)
                    pool.wait_ge(means_ready, i + 1)
                    pool.tensor_tensor(rstd[:, :], ms[:, :], half[:, :], ALU.pow).then_inc(rstd_ready, 1)

            @block.vector
            def _(dve):
                dve.wait_ge(const_in, 16)
                dve.wait_ge(pool_consts, 1)
                with dve.Fori(0, HG_HEADS) as i:
                    dve.tensor_copy(lbh[:, :], k["lbT"][:, :, bass.ds(i, 1)].squeeze(2))
                    dve.drain()
                    for g in range(3):
                        ux, fx = (z[g][:, :, :] if g == 0 else z[g][:, :] for z in (u, f))
                        dve.wait_ge(ef_ready, i * 3 + (g + 1))
                        dve.tensor_scalar(fx, ux, 1.0, None, ALU.add)
                        dve.drain()
                        dve.reciprocal(fx, fx)
                        dve.drain()
                        dve.tensor_scalar(fx, fx, lbh[:, 1:2], lbh[:, 0:1], ALU.mult, ALU.add).then_inc(f_stored, 1)
                    dve.wait_ge(eq_ready, i + 1)
                    dve.tensor_scalar(uq[:, :], eq[:, :], 1.0, None, ALU.add)
                    dve.drain()
                    dve.reciprocal(uq[:, :], uq[:, :])
                    dve.drain()
                    dve.tensor_tensor(q[:, :], q_ps[:, :], uq[:, :], ALU.mult).then_inc(q_stored, 1)
                    dve.wait_ge(lf_stored, i * 3 + 1)
                    for d in range(2):
                        dve.tensor_tensor_scan(arc[d][:, 1:CTX + 1], ones[:, 0:CTX], u[0][:, d, :], 0.0, ALU.mult,
                                               ALU.add).then_inc(sums_ready, 1)
                    for d in range(2):
                        dve.wait_ge(lf_stored, i * 3 + (2 + d))
                        dve.tensor_tensor_scan(arr[d][:, 1:SEQ + 1], ones[:, :], u[1 + d][:, :], 0.0, ALU.mult, ALU.add)\
                            .then_inc(sums_ready, 1)

                    def take_iz(m):
                        j = IZ[m]
                        dve.wait_ge(iz_exp, i * NT + (m + 1))
                        dve.sem_inc(k["apart"], 1)
                        if j >= LT:
                            dve.drain().then_inc(iz_used, 1)
                        else:
                            dve.tensor_tensor(zs[:, j, :], iz_bank(m)[:, P:2 * P], rz[:, :], ALU.mult).then_inc(iz_used, 1)

                    take_iz(0)
                    take_iz(1)
                    dve.wait_ge(xc_exp, i + 1)
                    for d in range(2):
                        dve.tensor_tensor(kk_[0][:, d, :], kk_[0][:, d, :], xc[:, d, :], ALU.mult).then_inc(kd_ready, 1)
                    dve.wait_ge(xq_exp, i + 1)
                    for d in range(2):
                        dve.tensor_tensor(xq[:, d, :], xq[:, d, :], q[:, :], ALU.mult).then_inc(qp_ready, 1)

                    def collect(n):
                        dve.wait_ge(level_ready, i * (NL + 1) + (n + 1))
                        dve.sem_inc(k["apart"], 1)
                        if n == 0:
                            cp = dve.tensor_copy(own[:, :], b[0][:, :])
                        else:
                            cp = dve.copy_predicated(own[:, :].rearrange("p (t c) -> p t c", t=LT),
                                                     masks[:, n - 1, :].unsqueeze(1).to_broadcast([P, LT, P]),
                                                     b[n % 2][:, :].rearrange("p (t c) -> p t c", t=LT))
                        cp.then_inc(own_stored, 1)
                        dve.drain()

                    for n, wd in enumerate(HG_LEVELS):
                        dve.wait_ge(xy_exp, i * NL + (n + 1))
                        if n >= 2:
                            dve.wait_ge(level_ready, i * (NL + 1) + n)
                        x, yb = halves(xy[n % 2][:, 0, :], wd), halves(xy[n % 2][:, 1, :], wd)
                        ql, kl = halves(qk[n % 2][:, 0, :], wd), halves(qk[n % 2][:, 1, :], wd)
                        qh, kf, kb = halves(q[:, :], wd), halves(kk_[1][:, :], wd), halves(kk_[2][:, :], wd)
                        dve.tensor_tensor(ql[:, :, 0, :], qh[:, :, 0, :], yb[:, :, 0, :], ALU.mult)
                        dve.tensor_tensor(ql[:, :, 1, :], qh[:, :, 1, :], x[:, :, 1, :], ALU.mult)
                        dve.tensor_tensor(kl[:, :, 0, :], kf[:, :, 0, :], x[:, :, 0, :], ALU.mult)
                        dve.tensor_tensor(kl[:, :, 1, :], kb[:, :, 1, :], yb[:, :, 1, :], ALU.mult)
                        dve.drain().then_inc(qk_ready, 1)
                        if n <= len(SMALL):
                            collect(n)
                        if n >= 3 and n % 2 == 1:
                            take_iz(CT + (n - 3) // 2)
                    take_iz(NT - 1)
                    dve.wait_ge(level_ready, i * (NL + 1) + (len(SMALL) + 2))
                    dve.tensor_copy(near[:, :], b[0][:, :]).then_inc(near_stored, 1)
                    dve.wait_ge(squares_ready, i + 1)
                    dve.tensor_scalar(ms[:, :], ss[:, :], 1.0 / P, EPS, ALU.mult, ALU.add).then_inc(means_ready, 1)
                    dve.tensor_copy(hn[:, :], k["vecT"][:, bass.ds(i + ROW["h_norm_c"], 1)])
                    dve.wait_ge(rstd_ready, i + 1)
                    for t in range(LT):
                        dve.scalar_tensor_tensor(out=y[:, t, :], in0=b[6][:, t * P:(t + 1) * P], scalar=rstd[:, t:t + 1],
                                                 in1=zs[:, t, :], op0=ALU.mult, op1=ALU.mult)
                    dve.drain().then_inc(y_ready, 1)


def stage_conv(nc, a, k, yaT, f_rows):
    CH = 512 // P
    with Stage(nc, "conv") as s:
        w = [s.sb(f"w{n}", [P, KD, 3, P]) for n in range(2)]
        wf, bf = s.sb("wf", [P, KD, 8]), s.sb("bf", [8, 1])
        g, t0, t1, cum, ones = (s.sb(n, [8, SEQ]) for n in ("g", "t0", "t1", "cum", "ones"))
        c = [s.sb(f"c{n}", [P, SEQ]) for n in range(2)]
        u = s.sb("u", [P, SEQ + 2])
        taps = s.sb("taps", [P, 3, 1])
        s0, s1 = s.sb("s0", [P, SEQ]), s.sb("s1", [P, SEQ])
        ps = [[s.ps(f"ps_{n}{h}") for n in ("x", "b", "c")] for h in range(2)]
        f_ps = s.ps("f_ps")
        w_in, f_in = [s.sem(f"w_in{n}") for n in range(2)], s.sem("f_in")
        (f_ready, g_ready, ln_ready, f_rows_ready, f_saved, products_ready, c_stored, chunk_done) = (
            s.sem(n) for n in ("f_ready", "g_ready", "ln_ready", "f_rows_ready", "f_saved", "products_ready",
                               "c_stored", "chunk_done"))
        with nc.Block() as block:
            @block.sync
            def _(sp):
                src = a["w_in_2"][0].rearrange("(k p) n -> p k n", p=P)

                def load(n, col):
                    for x in range(3):
                        sp.dma_start(w[n][:, :, x, :], src[:, :, bass.ds(col + x * 512, P)]).then_inc(w_in[n], 16)

                sp.dma_start(wf[:, :, :], src[:, :, 3072:3080]).then_inc(f_in, 16)
                sp.dma_start(bf[:, :], a["b_forget_2"].rearrange("a n -> n a")).then_inc(f_in, 16)
                for n in range(2):
                    load(n, n * P)
                for n in range(2):
                    sp.wait_ge(products_ready, n + 1)
                    load(n, (n + 2) * P)
                sp.wait_ge(f_rows_ready, 1)
                sp.dma_start(f_rows, cum[:, :]).then_inc(f_saved, 16)
                sp.wait_ge(f_saved, 16)

            @block.tensor
            def _(pe):
                pe.wait_ge(f_in, 32)
                for kk in range(KD):
                    mm = pe.matmul(f_ps[0:8, :], wf[:, kk, :], k["hT"][:, kk, 0:SEQ], start=kk == 0, stop=kk == KD - 1)
                mm.then_inc(f_ready, 1)
                with pe.Fori(0, CH // 2) as i:
                    for n in range(2):
                        pe.wait_ge(w_in[n], i * 48 + 48)
                        pe.wait_ge(chunk_done, i * 2 + (n + 1))
                        for x in range(3):
                            for kk in range(KD):
                                mm = pe.matmul(ps[n][x][:, :], w[n][:, kk, x, :], k["hT"][:, kk, 0:SEQ],
                                               start=kk == 0, stop=kk == KD - 1)
                        mm.then_inc(products_ready, 1)

            @block.scalar
            def _(act):
                act.wait_ge(g_ready, 1)
                act.activation(t0[:, :], g[:, :], ACT.Abs)
                act.drain()
                act.activation(t1[:, :], t0[:, :], ACT.Exp, scale=-1.0)
                act.drain()
                act.activation(t0[:, :], t1[:, :], ACT.Ln, bias=1.0).then_inc(ln_ready, 1)
                with act.Fori(0, CH // 2) as i:
                    for n in range(2):
                        act.wait_ge(products_ready, i * 2 + (n + 1))
                        act.activation(c[n][:, :], ps[n][2][:, :], ACT.Copy).then_inc(c_stored, 1)

            @block.vector
            def _(dve):
                dve.memset(ones[:, :], 1.0)
                dve.memset(u[:, 0:2], 0.0)
                dve.drain().then_inc(chunk_done, 1)
                dve.drain().then_inc(chunk_done, 1)
                dve.wait_ge(f_ready, 1)
                dve.tensor_scalar(g[:, :], f_ps[0:8, :], bf[:, 0:1], None, ALU.add).then_inc(g_ready, 1)
                dve.wait_ge(ln_ready, 1)
                dve.drain()
                dve.tensor_scalar(t1[:, :], g[:, :], 0.0, None, ALU.min)
                dve.drain()
                dve.tensor_tensor(g[:, :], t0[:, :], t1[:, :], ALU.subtract)
                dve.drain()
                dve.tensor_tensor_scan(cum[:, :], ones[:, :], g[:, :], 0.0, ALU.mult, ALU.add).then_inc(f_rows_ready, 1)
                table = k["vecT"][:, ROW["conv_w_2"]:ROW["conv_w_2"] + 12].rearrange("p (j c) -> p j c", c=CH)
                with dve.Fori(0, CH // 2) as i:
                    for n in range(2):
                        dve.drain()
                        dve.tensor_copy(taps[:, :, :], table[:, :, bass.ds(i * 2 + n, 1)])
                        dve.wait_ge(c_stored, i * 2 + (n + 1))
                        dve.tensor_tensor(u[:, 2:SEQ + 2], ps[n][0][:, :], c[n][:, :], ALU.mult)
                        dve.drain()
                        dve.tensor_scalar(s0[:, :], u[:, 0:SEQ], taps[:, 0, :], None, ALU.mult)
                        dve.drain()
                        dve.scalar_tensor_tensor(out=s1[:, :], in0=u[:, 1:SEQ + 1], scalar=taps[:, 1, :], in1=s0[:, :],
                                                 op0=ALU.mult, op1=ALU.add)
                        dve.drain()
                        dve.scalar_tensor_tensor(out=s0[:, :], in0=u[:, 2:SEQ + 2], scalar=taps[:, 2, :], in1=s1[:, :],
                                                 op0=ALU.mult, op1=ALU.add)
                        dve.drain()
                        dve.tensor_tensor(yaT[:, bass.ds(i * 2 + n, 1), 0:SEQ].squeeze(1), s0[:, :], ps[n][1][:, :],
                                          ALU.mult).then_inc(chunk_done, 1)


def stage_attention_2(nc, a, k, ybT, f_rows):
    HD, PAIRS = 64, 4
    OFF = [0, 1, 3, 6]
    PACK = 10 * P
    units = [(t, h) for t in range(LT) for h in range(2)]
    NU = len(units)
    with Stage(nc, "att") as s:
        w = s.sb("w", [P, KD, 3, P])
        squares, qkn = s.sb("squares", [P, 4, HD]), [s.sb(f"qkn{u}", [P, 4, HD]) for u in range(2)]
        ss, ms, rstd, half = (s.sb(n, [P, 4]) for n in ("ss", "ms", "rstd", "half"))
        qw, kw = s.sb("qw", [P, 1]), s.sb("kw", [P, 1])
        qT, kT = s.sb("qT", [P, SEQ]), s.sb("kT", [P, SEQ])
        v = s.sb("v", [P, LT, P])
        mask, fb = s.sb("mask", [P, PACK]), [s.sb(f"fb{h}", [P, SEQ]) for h in range(2)]
        bias = s.sb("bias", [P, 2, PACK])
        sc, p = [s.sb(f"sc{u}", [P, SEQ]) for u in range(3)], [s.sb(f"p{u}", [P, SEQ]) for u in range(3)]
        pT = [s.sb(f"pT{u}", [P, SEQ]) for u in range(2)]
        m, nm, sums, rinv = (s.sb(n, [P, NU]) for n in ("m", "nm", "sums", "rinv"))
        y = s.sb("y", [P, 2, P])
        banks = [s.ps(f"bank{n}") for n in range(8)]
        proj, qk_ps, pT_ps = banks[0:4], banks[4:6], banks[6:8]
        s_ps, o_ps, yT_ps = banks[0:2], banks[2:4], banks[4:6]
        w_in, f_in, const_in = s.sem("w_in"), s.sem("f_in"), s.sem("const_in")
        (consts_ready, proj_ready, squares_ready, means_ready, rstd_ready, qk_normed, qk_turned, qk_stored,
         bias_ready, scores_ready, max_ready, exp_ready, pT_ready, pT_stored, pv_ready, y_ready, y_turned,
         yT_stored) = (s.sem(n) for n in (
             "consts_ready", "proj_ready", "squares_ready", "means_ready", "rstd_ready", "qk_normed", "qk_turned",
             "qk_stored", "bias_ready", "scores_ready", "max_ready", "exp_ready", "pT_ready", "pT_stored", "pv_ready",
             "y_ready", "y_turned", "yT_stored"))

        def n_keys(t):
            return (t + 1) * P

        with nc.Block() as block:
            @block.sync
            def _(sp):
                for dst, src in ((qw, "q_norm_w_2"), (kw, "k_norm_w_2")):
                    for h in range(2):
                        sp.dma_start(dst[h * HD:(h + 1) * HD, :], a[src].rearrange("a d -> d a")).then_inc(const_in, 16)
                sp.dma_start(mask[:, :], a["causal"]).then_inc(const_in, 16)
                src = a["w_in_2"][0].rearrange("(k p) n -> p k n", p=P)

                def load(pair):
                    for x in range(3):
                        sp.dma_start(w[:, :, x, :], src[:, :, bass.ds(pair * P + (1536 + x * 512), P)])\
                            .then_inc(w_in, 16)
                    for h in range(2):
                        sp.dma_start(fb[h][:, :], f_rows[bass.ds(pair * 2 + h, 1), :].to_broadcast([P, SEQ]))\
                            .then_inc(f_in, 16)

                load(0)
                with sp.Fori(0, PAIRS - 1) as i:
                    sp.wait_ge(proj_ready, i * LT + LT)
                    sp.sem_inc(k["apart"], 1)
                    sp.wait_ge(bias_ready, i + 1)
                    sp.sem_inc(k["apart"], 1)
                    load(i + 1)

            @block.tensor
            def _(pe):
                pe.wait_ge(const_in, 16 * 5)
                with pe.Fori(0, PAIRS) as i:
                    def turn_qk(j):
                        pe.wait_ge(qk_normed, i * LT + (j + 1))
                        if j >= 2:
                            pe.wait_ge(qk_stored, i * LT + (j - 1))
                        for b in range(2):
                            tr = pe.transpose(qk_ps[j % 2][:, b * P:(b + 1) * P],
                                              qkn[j % 2][:, 2 * b:2 * b + 2, :], k["ident"][:, :])
                        tr.then_inc(qk_turned, 1)

                    pe.wait_ge(w_in, i * 48 + 48)
                    for j in range(LT):
                        for kk in range(KD):
                            mm = pe.matmul(proj[j][:, 0:384], k["hT"][:, kk, j * P:(j + 1) * P], w[:, kk, :, :],
                                           start=kk == 0, stop=kk == KD - 1)
                        mm.then_inc(proj_ready, 1)
                        if j >= 1:
                            turn_qk(j - 1)
                    turn_qk(LT - 1)
                    pe.wait_ge(qk_stored, i * LT + LT)
                    for n in range(NU + 4):
                        if n < NU:
                            t, h = units[n]
                            hs = slice(h * HD, (h + 1) * HD)
                            if n >= 2:
                                pe.wait_ge(max_ready, i * NU + (n - 1))
                            pe.matmul(s_ps[n % 2][:, 0:n_keys(t)], qT[hs, t * P:(t + 1) * P], kT[hs, 0:n_keys(t)],
                                      start=True, stop=True).then_inc(scores_ready, 1)
                        if 2 <= n < NU + 2:
                            x = n - 2
                            pe.wait_ge(exp_ready, i * NU + (x + 1))
                            if x >= 2:
                                pe.wait_ge(pT_stored, i * NU + (x - 1))
                            for b in range(units[x][0] + 1):
                                tr = pe.transpose(pT_ps[x % 2][:, b * P:(b + 1) * P], p[x % 3][:, b * P:(b + 1) * P],
                                                  k["ident"][:, :])
                            tr.then_inc(pT_ready, 1)
                        if 3 <= n < NU + 3:
                            x = n - 3
                            t, h = units[x]
                            pe.wait_ge(pT_stored, i * NU + (x + 1))
                            if x >= 2:
                                pe.wait_ge(y_ready, i * NU + (x - 1))
                            for b in range(t + 1):
                                mm = pe.matmul(o_ps[x % 2][:, 0:HD], pT[x % 2][:, b * P:(b + 1) * P],
                                               v[:, b, h * HD:(h + 1) * HD], start=b == 0, stop=b == t)
                            mm.then_inc(pv_ready, 1)
                        if n >= 5 and n % 2 == 1:
                            t = (n - 5) // 2
                            pe.wait_ge(y_ready, i * NU + (2 * t + 2))
                            if t >= 2:
                                pe.wait_ge(yT_stored, i * LT + (t - 1))
                            pe.transpose(yT_ps[t % 2][:, 0:P], y[:, t % 2, :], k["ident"][:, :]).then_inc(y_turned, 1)

            @block.scalar
            def _(act):
                act.wait_ge(consts_ready, 1)
                with act.Fori(0, PAIRS) as i:
                    def store_qk(j):
                        act.wait_ge(qk_turned, i * LT + (j + 1))
                        act.activation(qT[:, j * P:(j + 1) * P], qk_ps[j % 2][:, 0:P], ACT.Copy, scale=qw[:, 0:1])
                        act.activation(kT[:, j * P:(j + 1) * P], qk_ps[j % 2][:, P:2 * P], ACT.Copy, scale=kw[:, 0:1])\
                            .then_inc(qk_stored, 1)

                    def store_y(t):
                        act.wait_ge(y_turned, i * LT + (t + 1))
                        act.sem_inc(k["apart"], 1)
                        act.activation(ybT[:, bass.ds(i, 1), t * P:(t + 1) * P].squeeze(1), yT_ps[t % 2][:, 0:P], ACT.Copy)\
                            .then_inc(yT_stored, 1)

                    for j in range(LT):
                        act.wait_ge(proj_ready, i * LT + (j + 1))
                        if j >= 1:
                            act.wait_ge(qk_normed, i * LT + j)
                        act.activation(v[:, j, :], proj[j][:, 256:384], ACT.Copy)
                        act.activation(squares[:, :, :], proj[j][:, 0:256].rearrange("p (h d) -> p h d", d=HD),
                                       ACT.Square).then_inc(squares_ready, 1)
                        if j >= 1:
                            store_qk(j - 1)
                    store_qk(LT - 1)
                    for n in range(NU + 3):
                        if n < NU:
                            nk = n_keys(units[n][0])
                            act.wait_ge(max_ready, i * NU + (n + 1))
                            if n >= 3:
                                act.wait_ge(pT_ready, i * NU + (n - 2))
                            act.activation(p[n % 3][:, 0:nk], sc[n % 3][:, 0:nk], ACT.Exp, bias=nm[:, n:n + 1],
                                           accum_out=sums[:, n:n + 1]).then_inc(exp_ready, 1)
                        if 2 <= n < NU + 2:
                            x = n - 2
                            nk = n_keys(units[x][0])
                            act.wait_ge(pT_ready, i * NU + (x + 1))
                            if x >= 2:
                                act.wait_ge(pv_ready, i * NU + (x - 1))
                            act.activation(pT[x % 2][:, 0:nk], pT_ps[x % 2][:, 0:nk], ACT.Copy).then_inc(pT_stored, 1)
                        if n >= 7 and n % 2 == 1:
                            store_y((n - 7) // 2)
                    for t in range((NU + 2 - 7) // 2 + 1, LT):
                        store_y(t)

            @block.gpsimd
            def _(pool):
                pool.memset(half[:, :], -0.5)
                pool.drain()
                pool.wait_ge(const_in, 16 * 5)
                with pool.Fori(0, PAIRS) as i:
                    for j in range(LT):
                        pool.wait_ge(means_ready, i * LT + (j + 1))
                        pool.tensor_tensor(rstd[:, :], ms[:, :], half[:, :], ALU.pow).then_inc(rstd_ready, 1)
                    pool.wait_ge(f_in, i * 32 + 32)
                    pool.sem_inc(k["apart"], 1)
                    for h in range(2):
                        for t in range(LT):
                            at = slice(OFF[t] * P, OFF[t] * P + n_keys(t))
                            pool.tensor_tensor(bias[:, h, at], mask[:, at], fb[h][:, 0:n_keys(t)], ALU.add)
                    pool.drain().then_inc(bias_ready, 1)

            @block.vector
            def _(dve):
                dve.wait_ge(const_in, 16 * 5)
                dve.tensor_scalar(qw[:, :], qw[:, :], HD ** -0.5, None, ALU.mult).then_inc(consts_ready, 1)
                with dve.Fori(0, PAIRS) as i:
                    for j in range(LT):
                        dve.wait_ge(squares_ready, i * LT + (j + 1))
                        dve.tensor_reduce(ss[:, :], squares[:, :, :], AX_X, ALU.add)
                        dve.drain()
                        dve.tensor_scalar(ms[:, :], ss[:, :], 1.0 / HD, EPS, ALU.mult, ALU.add).then_inc(means_ready, 1)
                        dve.wait_ge(rstd_ready, i * LT + (j + 1))
                        if j >= 2:
                            dve.wait_ge(qk_turned, i * LT + (j - 1))
                        dve.tensor_tensor(qkn[j % 2][:, :, :], proj[j][:, 0:256].rearrange("p (h d) -> p h d", d=HD),
                                          rstd[:, :].unsqueeze(2).to_broadcast([P, 4, HD]), ALU.mult)\
                            .then_inc(qk_normed, 1)
                    dve.wait_ge(bias_ready, i + 1)
                    dve.sem_inc(k["apart"], 1)
                    for n in range(NU + 3):
                        if n >= 3:
                            x = n - 3
                            dve.wait_ge(exp_ready, i * NU + (x + 1))
                            dve.reciprocal(rinv[:, x:x + 1], sums[:, x:x + 1])
                        if n < NU:
                            t, h = units[n]
                            nk = n_keys(t)
                            dve.wait_ge(scores_ready, i * NU + (n + 1))
                            dve.sem_inc(k["apart"], 1)
                            dve.tensor_tensor_reduce(sc[n % 3][:, 0:nk], s_ps[n % 2][:, 0:nk],
                                                     bias[:, h, OFF[t] * P:OFF[t] * P + nk], 1.0, -3e38,
                                                     ALU.add, ALU.max, m[:, n:n + 1])
                        dve.drain()
                        if n < NU:
                            dve.tensor_scalar(nm[:, n:n + 1], m[:, n:n + 1], -1.0, None, ALU.mult).then_inc(max_ready, 1)
                        if n >= 3:
                            t, h = units[x]
                            dve.wait_ge(pv_ready, i * NU + (x + 1))
                            if t >= 2 and h == 0:
                                dve.wait_ge(y_turned, i * LT + (t - 1))
                            dve.tensor_scalar(y[:, t % 2, h * HD:(h + 1) * HD], o_ps[x % 2][:, 0:HD], rinv[:, x:x + 1],
                                              None, ALU.mult).then_inc(y_ready, 1)


def stage_merge(nc, a, k, yaT, ybT, mergedT):
    with Stage(nc, "merge") as s:
        wg = [s.sb(f"wg{n}", [P, 2, KD, P]) for n in range(2)]
        wo = [s.sb(f"wo{n}", [P, 2, 4, P]) for n in range(2)]
        e, r = s.sb("e", [P, 2, SEQ]), s.sb("r", [P, 2, SEQ])
        t = s.sb("t", [P, 2, SEQ])
        ps = [[s.ps(f"{n}{h}") for n in ("gc", "ga", "pa", "pb")] for h in range(2)]
        w_in = [s.sem(f"w_in{n}") for n in range(2)]
        gates_ready, products_ready, exp_ready, e_read, merged = (
            s.sem(n) for n in ("gates_ready", "products_ready", "exp_ready", "e_read", "merged"))
        with nc.Block() as block:
            @block.sync
            def _(sp):
                src = a["w_in_2"][0].rearrange("(k p) n -> p k n", p=P)
                outs = [a[n][0].rearrange("(k p) n -> p k n", p=P) for n in ("w_out_conv_2", "w_out_attn_2")]

                def load(n, chunk):
                    for x in range(2):
                        sp.dma_start(wg[n][:, x, :, :], src[:, :, bass.ds(chunk * P + (3080 + x * D), P)])\
                            .then_inc(w_in[n], 16)
                        sp.dma_start(wo[n][:, x, :, :], outs[x][:, :, bass.ds(chunk * P, P)]).then_inc(w_in[n], 16)

                for n in range(2):
                    load(n, n)
                with sp.Fori(0, KD // 2 - 1) as i:
                    for n in range(2):
                        sp.wait_ge(products_ready, i * 2 + (n + 1))
                        load(n, i * 2 + (n + 2))

            @block.tensor
            def _(pe):
                with pe.Fori(0, KD // 2) as i:
                    for n in range(2):
                        pe.wait_ge(w_in[n], i * 64 + 64)
                        pe.wait_ge(merged, i * 2 + (n + 1))
                        for x in range(2):
                            for kk in range(KD):
                                mm = pe.matmul(ps[n][x][:, :], wg[n][:, x, kk, :], k["hT"][:, kk, 0:SEQ],
                                               start=kk == 0, stop=kk == KD - 1)
                        mm.then_inc(gates_ready, 1)
                        for x, yy in enumerate((yaT, ybT)):
                            for kk in range(4):
                                mm = pe.matmul(ps[n][2 + x][:, :], wo[n][:, x, kk, :], yy[:, kk, 0:SEQ],
                                               start=kk == 0, stop=kk == 3)
                        mm.then_inc(products_ready, 1)

            @block.scalar
            def _(act):
                with act.Fori(0, KD // 2) as i:
                    for n in range(2):
                        act.wait_ge(gates_ready, i * 2 + (n + 1))
                        act.wait_ge(e_read, i * 2 + (n + 1))
                        act.activation(e[:, 0, :], ps[n][0][:, :], ACT.Exp, scale=-1.0)
                        act.activation(e[:, 1, :], ps[n][1][:, :], ACT.Exp, scale=-1.0).then_inc(exp_ready, 1)

            @block.vector
            def _(dve):
                dve.drain().then_inc(merged, 1)
                dve.drain().then_inc(merged, 1)
                dve.drain().then_inc(e_read, 1)
                with dve.Fori(0, KD // 2) as i:
                    for n in range(2):
                        dve.wait_ge(exp_ready, i * 2 + (n + 1))
                        dve.tensor_scalar(r[:, :, :], e[:, :, :], 1.0, None, ALU.add).then_inc(e_read, 1)
                        dve.drain()
                        dve.reciprocal(r[:, :, :], r[:, :, :])
                        dve.drain()
                        dve.wait_ge(products_ready, i * 2 + (n + 1))
                        for x in range(2):
                            dve.tensor_tensor(t[:, x, :], ps[n][2 + x][:, :], r[:, x, :], ALU.mult)
                        dve.drain()
                        dve.tensor_tensor(mergedT[:, bass.ds(i * 2 + n, 1), 0:SEQ].squeeze(1), t[:, 0, :], t[:, 1, :],
                                          ALU.add).then_inc(merged, 1)


def stage_router(nc, a, k, slots, share, block_expert, slot_token):
    NG, EG = 4, 8
    NL = NG + NE
    with Stage(nc, "router") as s:
        w, bias = s.sb("w", [P, KD, NL]), s.sb("bias", [P, NL])
        lg, le = s.sb("lg", [P, LT, NG]), s.sb("le", [P, LT, NG, EG])
        picked = s.sb("picked", [P, LT, NG, EG])
        ex_g, leg, leg2 = s.sb("ex_g", [P, LT, NG]), s.sb("leg", [P, LT, EG]), s.sb("leg2", [P, LT, EG])
        iota = s.sb("iota", [P, EG])
        val, low = s.sb("val", [P, LT, EG]), s.sb("low", [P, LT])
        sel, first, second = s.sb("sel", [P, LT, NG]), s.sb("first", [P, LT, EG]), s.sb("second", [P, LT, EG])
        mg, v1, v2, dv, ex, sg, rg, w1, w2 = (s.sb(n, [P, LT]) for n in ("mg", "v1", "v2", "dv", "ex", "sg", "rg",
                                                                         "w1", "w2"))
        chosen = [s.sb(f"chosen{n}", [P, LT, NE]) for n in range(2)]
        both, place = s.sb("both", [P, LT, NE]), s.sb("place", [P, LT, NE])
        count, blocks, upto, base, ones32 = (s.sb(n, [P, NE]) for n in ("count", "blocks", "upto", "base", "ones32"))
        before, ones = s.sb("before", [P, P]), s.sb("ones", [P, P])
        passed, e_of, e_min = s.sb("passed", [1, BLOCKS, NE]), s.sb("e_of", [1, BLOCKS]), s.sb("e_min", [1, BLOCKS])
        block_ids, slots_f = s.sb("block_ids", [1, BLOCKS]), s.sb("slots_f", [P, 2, LT])
        zeros, token_ids = s.sb("zeros", [P, BLOCKS], U32), s.sb("token_ids", [P, LT], U32)
        rank_ps, count_ps = s.ps("rank_ps"), s.ps("count_ps")
        tables_in, both_ready, ranks_ready, zeroed, zeros_saved, slots_ready, tokens_saved = (s.sem(n) for n in (
            "tables_in", "both_ready", "ranks_ready", "zeroed", "zeros_saved", "slots_ready", "tokens_saved"))
        ps = s.ps("ps")
        w_in, bias_in, products_ready = s.sem("w_in"), s.sem("bias_in"), s.sem("products_ready")
        diff_ready, exp_ready, group_ready, group_exp = (
            s.sem(n) for n in ("diff_ready", "exp_ready", "group_ready", "group_exp"))
        with nc.Block() as block:
            @block.sync
            def _(sp):
                for src, c0, n in (("w_router_group_2", 0, NG), ("w_router_expert_2", NG, NE)):
                    sp.dma_start(w[:, :, c0:c0 + n], a[src][0].rearrange("(k p) n -> p k n", p=P)).then_inc(w_in, 16)
                for src, c0, n in (("b_router_group_2", 0, NG), ("b_router_expert_2", NG, NE)):
                    sp.dma_start(bias[:, c0:c0 + n], a[src].to_broadcast([P, n])).then_inc(bias_in, 16)
                sp.dma_start(iota[:, :], a["iota8"]).then_inc(bias_in, 16)
                sp.dma_start(before[:, :], a["before"]).then_inc(tables_in, 16)
                sp.dma_start(block_ids[:, :], a["block_ids"]).then_inc(tables_in, 16)
                sp.dma_start(token_ids[:, :], a["token_ids"]).then_inc(tables_in, 16)
                sp.wait_ge(zeroed, 1)
                sp.dma_start(slot_token.rearrange("(p b) o -> p (b o)", p=P), zeros[:, :]).then_inc(zeros_saved, 16)

            @block.tensor
            def _(pe):
                pe.wait_ge(w_in, 32)
                for j in range(LT):
                    for kk in range(KD):
                        mm = pe.matmul(ps[:, j * 64:j * 64 + NL], k["hT"][:, kk, j * P:(j + 1) * P], w[:, kk, :],
                                       start=kk == 0, stop=kk == KD - 1)
                mm.then_inc(products_ready, 1)
                pe.wait_ge(tables_in, 48)
                pe.wait_ge(both_ready, 1)
                for j in range(LT):
                    for n in range(j + 1):
                        mm = pe.matmul(rank_ps[:, j * NE:(j + 1) * NE], (before if n == j else ones)[:, :],
                                       both[:, n, :], start=n == 0, stop=n == j)
                for n in range(LT):
                    mm = pe.matmul(count_ps[:, 0:NE], ones[:, :], both[:, n, :], start=n == 0, stop=n == LT - 1)
                mm.then_inc(ranks_ready, 1)

            @block.gpsimd
            def _(pool):
                pool.memset(zeros[:, :], 0)
                pool.drain().then_inc(zeroed, 1)
                pool.wait_ge(tables_in, 48)
                pool.wait_ge(zeros_saved, 16)
                pool.wait_ge(slots_ready, 1)
                for n in range(2):
                    for t in range(LT):
                        pool.indirect_dma_start(slot_token, bass.IndirectOffsetOnAxis(slots[:, n, t:t + 1], 0),
                                                token_ids[:, t:t + 1], None).then_inc(tokens_saved, 16)
                pool.wait_ge(tokens_saved, 16 * 2 * LT)

            @block.scalar
            def _(act):
                act.wait_ge(group_ready, 1)
                act.activation(ex_g[:, :, :], ex_g[:, :, :], ACT.Exp).then_inc(group_exp, 1)
                act.wait_ge(diff_ready, 1)
                act.activation(ex[:, :], dv[:, :], ACT.Exp).then_inc(exp_ready, 1)

            @block.vector
            def _(dve):
                def bc(x, n):
                    return x[:, :].unsqueeze(2).to_broadcast([P, LT, n])

                def pick_first(out, x, top, n):
                    dve.tensor_tensor(out[:, :, :], x[:, :, :], bc(top, n), ALU.is_equal)
                    dve.drain()
                    dve.scalar_tensor_tensor(out=val[:, :, 0:n], in0=out[:, :, :], scalar=-100.0,
                                             in1=iota[:, 0:n].unsqueeze(1).to_broadcast([P, LT, n]),
                                             op0=ALU.mult, op1=ALU.add)
                    dve.drain()
                    dve.tensor_reduce(low[:, :], val[:, :, 0:n], AX_X, ALU.min)
                    dve.drain()
                    dve.tensor_tensor(out[:, :, :], val[:, :, 0:n], bc(low, n), ALU.is_equal)
                    dve.drain()

                dve.wait_ge(bias_in, 48)
                dve.wait_ge(products_ready, 1)
                logits = ps[:, 0:LT * 64].rearrange("p (t n) -> p t n", t=LT)
                dve.tensor_tensor(lg[:, :, :], logits[:, :, 0:NG],
                                  bias[:, 0:NG].unsqueeze(1).to_broadcast([P, LT, NG]), ALU.add)
                for t in range(LT):
                    dve.tensor_tensor(le[:, t, :, :].rearrange("p g e -> p (g e)"), logits[:, t, NG:NL],
                                      bias[:, NG:NL], ALU.add)
                dve.drain()
                dve.tensor_reduce(mg[:, :], lg[:, :, :], AX_X, ALU.max)
                dve.drain()
                dve.tensor_tensor(ex_g[:, :, :], lg[:, :, :], bc(mg, NG), ALU.subtract).then_inc(group_ready, 1)
                pick_first(sel, lg, mg, NG)
                for t in range(LT):
                    dve.tensor_tensor(picked[:, t, :, :], le[:, t, :, :],
                                      sel[:, t, :].unsqueeze(2).to_broadcast([P, NG, EG]), ALU.mult)
                dve.drain()
                for t in range(LT):
                    dve.tensor_reduce(leg[:, t, :], picked[:, t, :, :].rearrange("p g e -> p e g"), AX_X, ALU.add)
                dve.drain()
                dve.tensor_reduce(v1[:, :], leg[:, :, :], AX_X, ALU.max)
                dve.drain()
                pick_first(first, leg, v1, EG)
                dve.scalar_tensor_tensor(out=leg2[:, :, :], in0=first[:, :, :], scalar=NEG, in1=leg[:, :, :],
                                         op0=ALU.mult, op1=ALU.add)
                dve.drain()
                dve.tensor_reduce(v2[:, :], leg2[:, :, :], AX_X, ALU.max)
                dve.drain()
                dve.tensor_tensor(dv[:, :], v2[:, :], v1[:, :], ALU.subtract).then_inc(diff_ready, 1)
                pick_first(second, leg2, v2, EG)
                dve.wait_ge(group_exp, 1)
                dve.tensor_reduce(sg[:, :], ex_g[:, :, :], AX_X, ALU.add)
                dve.wait_ge(exp_ready, 1)
                dve.tensor_scalar(w1[:, :], ex[:, :], 1.0, None, ALU.add)
                dve.drain()
                dve.reciprocal(rg[:, :], sg[:, :])
                dve.reciprocal(w2[:, :], w1[:, :])
                dve.drain()
                dve.tensor_tensor(share[:, 0, :], w2[:, :], rg[:, :], ALU.mult)
                for n, mine in enumerate((first, second)):
                    for t in range(LT):
                        dve.tensor_tensor(chosen[n][:, t, :].rearrange("p (g e) -> p g e", g=NG),
                                          mine[:, t, :].unsqueeze(1).to_broadcast([P, NG, EG]),
                                          sel[:, t, :].unsqueeze(2).to_broadcast([P, NG, EG]), ALU.mult)
                dve.memset(ones[:, :], 1.0)
                dve.memset(ones32[:, :], 1.0)
                dve.drain()
                dve.tensor_tensor(share[:, 1, :], share[:, 0, :], ex[:, :], ALU.mult)
                dve.tensor_tensor(both[:, :, :], chosen[0][:, :, :], chosen[1][:, :, :], ALU.add)
                dve.drain().then_inc(both_ready, 1)
                dve.wait_ge(ranks_ready, 1)
                dve.tensor_copy(count[:, :], count_ps[:, 0:NE])
                dve.drain()
                dve.tensor_scalar(blocks[:, :], count[:, :], 0.0, None, ALU.is_gt)
                dve.drain()
                for n in range(1, LT):
                    dve.scalar_tensor_tensor(out=blocks[:, :], in0=count[:, :], scalar=float(n * P), in1=blocks[:, :],
                                             op0=ALU.is_gt, op1=ALU.add)
                    dve.drain()
                dve.tensor_tensor_scan(upto[:, :], ones32[:, :], blocks[:, :], 0.0, ALU.mult, ALU.add)
                dve.drain()
                dve.tensor_tensor(base[:, :], upto[:, :], blocks[:, :], ALU.subtract)
                dve.wait_ge(tables_in, 48)
                dve.tensor_tensor(passed[:, :, :], upto[0:1, :].unsqueeze(1).to_broadcast([1, BLOCKS, NE]),
                                  block_ids[:, :].unsqueeze(2).to_broadcast([1, BLOCKS, NE]), ALU.is_le)
                dve.drain()
                dve.tensor_reduce(e_of[:, :], passed[:, :, :], AX_X, ALU.add)
                for t in range(LT):
                    dve.scalar_tensor_tensor(out=place[:, t, :], in0=base[:, :], scalar=float(P),
                                             in1=rank_ps[:, t * NE:(t + 1) * NE], op0=ALU.mult, op1=ALU.add)
                dve.drain()
                dve.tensor_scalar(e_min[:, :], e_of[:, :], float(NE - 1), None, ALU.min)
                for n in range(2):
                    dve.tensor_tensor(chosen[n][:, :, :], chosen[n][:, :, :], place[:, :, :], ALU.mult)
                dve.drain()
                dve.tensor_copy(block_expert[:, :], e_min[:, :])
                for n in range(2):
                    dve.tensor_reduce(slots_f[:, n, :], chosen[n][:, :, :], AX_X, ALU.add)
                dve.drain()
                dve.tensor_copy(slots[:, :, :], slots_f[:, :, :])
                dve.drain().then_inc(slots_ready, 1)


def stage_moe(nc, a, k):
    with Stage(nc, "routes") as s:
        slots, share = s.sb("slots", [P, 2, LT], U32), s.sb("share", [P, 2, LT])
        block_expert = s.sb("block_expert", [1, BLOCKS], I32)
        stage_router(nc, a, k, slots, share, block_expert, k["slot_token"])
        stage_experts(nc, a, k, slots, share, block_expert, k["slot_token"])


def stage_experts(nc, a, k, slots, share, block_expert, slot_token):
    FC = DE // P
    KH = KD // 2
    mod, nw = MOD_B2 + 24, ROW["norm2_w_2"]
    with Stage(nc, "moe") as s:
        wgu = [s.sb(f"wgu{n}", [P, KD, 2, DE]) for n in range(2)]
        wd = [s.sb(f"wd{n}", [P, FC, D]) for n in range(2)]
        tokens = s.sb("tokens", [P, BLOCKS], U32)
        token = [s.sb(f"token{n}", [P, 1], U32) for n in range(2)]
        x = [s.sb(f"x{n}", [P, D]) for n in range(2)]
        gain = s.sb("gain", [P, KD])
        h = [s.sb(f"h{n}", [P, KD, P]) for n in range(2)]
        silu = [s.sb(f"silu{n}", [P, DE]) for n in range(2)]
        act_out = [s.sb(f"a{n}", [P, DE]) for n in range(2)]
        aT = [s.sb(f"aT{n}", [P, FC, P]) for n in range(2)]
        y = [s.sb(f"y{n}", [P, D]) for n in range(2)]
        ones, diag, gate = s.sb("ones", [P, P]), s.sb("diag", [P, KD, P]), s.sb("gate", [P, D])
        mine = [[s.sb(f"mine{n}{t}", [P, D]) for t in range(2)] for n in range(2)]
        x_ps, gu_ps = [s.ps(f"x_ps{n}") for n in range(2)], [s.ps(f"gu_ps{n}") for n in range(2)]
        aT_ps, y_ps = s.ps("aT_ps"), [s.ps(f"y_ps{n}") for n in range(2)]
        gu_in, d_in, x_in, y_saved = ([s.sem(f"{n}{u}") for u in range(2)] for n in ("gu_in", "d_in", "x_in",
                                                                                     "y_saved"))
        mine_in = [s.sem(f"mine_in{t}") for t in range(2)]
        (tokens_in, diag_ready, spread, gate_ready, x_turned, h_act, h_dve, gu_ready, silu_ready, a_ready, a_turned,
         aT_stored, down_ready, y_act, y_dve, out_ready, out_saved) = (s.sem(n) for n in (
             "tokens_in", "diag_ready", "spread", "gate_ready", "x_turned", "h_act", "h_dve", "gu_ready",
             "silu_ready", "a_ready", "a_turned", "aT_stored", "down_ready", "y_act", "y_dve", "out_ready",
             "out_saved"))

        def run(eng, step):
            for c in range(4):
                step(0, c)
            with eng.Fori(0, BLOCKS // 2 - 3) as i:
                step(i, 4)
                step(i, 5)
            step(0, BLOCKS - 2)
            step(0, BLOCKS - 1)
            step(0, BLOCKS)

        def upto(i, c, n=0):
            return i * 2 + (c - n + 1)

        with nc.Block() as block:
            @block.sync
            def _(sp):
                sp.dma_start(tokens[:, :], slot_token.rearrange("(b p) o -> p (b o)", p=P),
                             allow_slow_non_contiguous=True).then_inc(tokens_in, 16)

                def load(i, c, wait):
                    u = c % 2
                    if wait:
                        sp.wait_ge(gu_ready, upto(i, c, 2))
                        sp.sem_inc(k["apart"], 1)
                    e = sp.value_load(block_expert[0:1, bass.ds(i * 2 + c, 1)], min_val=0, max_val=NE - 1)
                    for n, name in enumerate(("w_gate_2", "w_up_2")):
                        sp.dma_start(wgu[u][:, :, n, :],
                                     a[name][0, bass.ds(e, 1), :, :].squeeze(0).rearrange("(k p) n -> p k n", p=P))\
                            .then_inc(gu_in[u], 16)
                    if wait:
                        sp.wait_ge(down_ready, upto(i, c, 2))
                        sp.sem_inc(k["apart"], 1)
                    sp.dma_start(wd[u][:, :, :],
                                 a["w_down_2"][0, bass.ds(e, 1), :, :].squeeze(0).rearrange("(k p) n -> p k n", p=P))\
                        .then_inc(d_in[u], 16)

                load(0, 0, False)
                load(0, 1, False)
                with sp.Fori(0, BLOCKS // 2 - 1) as i:
                    load(i, 2, True)
                    load(i, 3, True)
                for t in range(LT):
                    sp.wait_ge(out_ready, t + 1)
                    sp.dma_start(a["out"][0, t * P:(t + 1) * P, :], k["xs"][:, t, :]).then_inc(out_saved, 16)
                sp.wait_ge(out_saved, 16 * LT)

            @block.gpsimd
            def _(pool):
                pool.wait_ge(tokens_in, 16)

                def gather(i, c, wait):
                    u = c % 2
                    if wait:
                        pool.wait_ge(x_turned, upto(i, c, 2))
                        pool.sem_inc(k["apart"], 1)
                    pool.tensor_copy(token[u][:, :], tokens[:, bass.ds(i * 2 + c, 1)])
                    pool.drain()
                    pool.indirect_dma_start(x[u][:, :], None, k["xn_rows"], bass.IndirectOffsetOnAxis(token[u][:, :], 0))\
                        .then_inc(x_in[u], 16)

                gather(0, 0, False)
                gather(0, 1, False)
                with pool.Fori(0, BLOCKS // 2 - 1) as i:
                    gather(i, 2, True)
                    gather(i, 3, True)
                for u in range(2):
                    pool.wait_ge(y_saved[u], 16 * (BLOCKS // 2))
                for t in range(LT):
                    if t >= 2:
                        pool.wait_ge(out_ready, t - 1)
                    for n in range(2):
                        pool.indirect_dma_start(mine[n][t % 2][:, :], None, k["y_rows"],
                                                bass.IndirectOffsetOnAxis(slots[:, n, t:t + 1], 0))\
                            .then_inc(mine_in[t % 2], 16)

            @block.tensor
            def _(pe):
                pe.wait_ge(diag_ready, 1)
                for n in range(2):
                    mm = pe.matmul(y_ps[n][:, :], ones[:, :], diag[:, n * 4:n * 4 + 4, :], start=True, stop=True)
                mm.then_inc(spread, 1)
                pe.wait_ge(gate_ready, 1)

                def turn_x(i, c, first=False):
                    pe.wait_ge(x_in[c % 2], i * 16 + (c // 2 + 1) * 16)
                    if not first:
                        pe.wait_ge(h_act, upto(i, c, 1))
                        pe.wait_ge(h_dve, upto(i, c, 1))
                    for n in range(KD):
                        tr = pe.transpose(x_ps[n // KH][:, n % KH * P:n % KH * P + P],
                                          x[c % 2][:, n * P:(n + 1) * P], k["ident"][:, :])
                    tr.then_inc(x_turned, 1)

                turn_x(0, 0, True)

                def step(i, c):
                    u = c % 2
                    if c + 1 < BLOCKS:
                        turn_x(i, c + 1)
                    if c < BLOCKS:
                        pe.wait_ge(gu_in[u], i * 32 + (c // 2 + 1) * 32)
                        pe.wait_ge(h_act, upto(i, c))
                        pe.wait_ge(h_dve, upto(i, c))
                        if c >= 2:
                            pe.wait_ge(a_ready, upto(i, c, 2))
                    for n in range(KD):
                        if n == KH and c >= 1:
                            pe.wait_ge(a_ready, upto(i, c, 1))
                            if c >= 2:
                                pe.wait_ge(aT_stored, upto(i, c, 2))
                            for f in range(FC):
                                tr = pe.transpose(aT_ps[:, f * P:(f + 1) * P], act_out[1 - u][:, f * P:(f + 1) * P],
                                                  k["ident"][:, :])
                            tr.then_inc(a_turned, 1)
                        if c < BLOCKS:
                            mm = pe.matmul(gu_ps[u][:, :], h[u][:, n, :], wgu[u][:, n, :, :], start=n == 0,
                                           stop=n == KD - 1)
                    if c < BLOCKS:
                        mm.then_inc(gu_ready, 1)
                    if c >= 1:
                        pe.wait_ge(d_in[1 - u], i * 16 + ((c - 1) // 2 + 1) * 16)
                        pe.wait_ge(aT_stored, upto(i, c, 1))
                        if c >= 2:
                            pe.wait_ge(y_act, upto(i, c, 2))
                            pe.wait_ge(y_dve, upto(i, c, 2))
                        for n in range(2):
                            for f in range(FC):
                                mm = pe.matmul(y_ps[n][:, :], aT[1 - u][:, f, :],
                                               wd[1 - u][:, f, n * 512:(n + 1) * 512], start=f == 0, stop=f == FC - 1)
                        mm.then_inc(down_ready, 1)

                run(pe, step)

            @block.scalar
            def _(act):
                act.wait_ge(gate_ready, 1)

                def modulate(i, c):
                    act.wait_ge(x_turned, upto(i, c))
                    if c >= 2:
                        act.wait_ge(gu_ready, upto(i, c, 2))
                    for n in range(KH):
                        ev = act.activation(h[c % 2][:, n, :], x_ps[0][:, n * P:(n + 1) * P], ACT.Identity,
                                            scale=gain[:, n:n + 1], bias=k["modT"][:, mod + n:mod + n + 1, 2])
                    ev.then_inc(h_act, 1)

                def store_y(i, c):
                    u = c % 2
                    act.wait_ge(down_ready, upto(i, c))
                    if c >= 2:
                        act.wait_ge(y_saved[u], i * 16 + (c // 2) * 16)
                    act.activation(y[u][:, 0:512], y_ps[0][:, :], ACT.Copy).then_inc(y_act, 1)
                    act.wait_ge(y_act, upto(i, c))
                    act.wait_ge(y_dve, upto(i, c))
                    act.sem_inc(k["apart"], 1)
                    act.dma_start(k["y_rows"][bass.ds(i * (2 * P) + c * P, P), :], y[u][:, :]).then_inc(y_saved[u], 16)

                modulate(0, 0)

                def step(i, c):
                    if c + 1 < BLOCKS:
                        modulate(i, c + 1)
                    if c < BLOCKS:
                        act.wait_ge(gu_ready, upto(i, c))
                        if c >= 2:
                            act.wait_ge(a_ready, upto(i, c, 2))
                        act.activation(silu[c % 2][:, :], gu_ps[c % 2][:, 0:DE], ACT.Silu).then_inc(silu_ready, 1)
                    if c >= 1:
                        store_y(i, c - 1)

                run(act, step)

            @block.vector
            def _(dve):
                dve.memset(ones[:, :], 1.0)
                dve.tensor_tensor(diag[:, :, :], k["ident"][:, :].unsqueeze(1).to_broadcast([P, KD, P]),
                                  k["modT"][:, MOD_B2 + 40:MOD_B2 + 48, 2:3].to_broadcast([P, KD, P]), ALU.mult)
                dve.drain().then_inc(diag_ready, 1)
                dve.tensor_scalar(gain[:, :], k["modT"][:, mod + 8:mod + 16, 2], 1.0, None, ALU.add)
                dve.drain()
                dve.tensor_tensor(gain[:, :], gain[:, :], k["vecT"][:, nw:nw + 8], ALU.mult)
                dve.wait_ge(spread, 1)
                for n in range(2):
                    dve.tensor_copy(gate[:, n * 512:(n + 1) * 512], y_ps[n][:, :])
                dve.drain().then_inc(gate_ready, 1)

                def modulate(i, c):
                    dve.wait_ge(x_turned, upto(i, c))
                    if c >= 2:
                        dve.wait_ge(gu_ready, upto(i, c, 2))
                    for n in range(KH, KD):
                        ev = dve.tensor_scalar(h[c % 2][:, n, :], x_ps[1][:, (n - KH) * P:(n - KH + 1) * P],
                                               gain[:, n:n + 1], k["modT"][:, mod + n:mod + n + 1, 2], ALU.mult, ALU.add)
                    ev.then_inc(h_dve, 1)

                modulate(0, 0)

                def step(i, c):
                    u = c % 2
                    if c + 1 < BLOCKS:
                        modulate(i, c + 1)
                    if c >= 1:
                        dve.wait_ge(a_turned, upto(i, c, 1))
                        if c >= 3:
                            dve.wait_ge(down_ready, upto(i, c, 3))
                        dve.sem_inc(k["apart"], 1)
                        dve.tensor_copy(aT[1 - u][:, :, :], aT_ps[:, 0:FC * P].rearrange("p (f c) -> p f c", f=FC))\
                            .then_inc(aT_stored, 1)
                    if c < BLOCKS:
                        dve.wait_ge(silu_ready, upto(i, c))
                        if c >= 2:
                            dve.wait_ge(a_turned, upto(i, c, 2))
                        dve.tensor_tensor(act_out[u][:, :], silu[u][:, :], gu_ps[u][:, DE:2 * DE], ALU.mult)\
                            .then_inc(a_ready, 1)
                    if c >= 1:
                        dve.wait_ge(down_ready, upto(i, c, 1))
                        if c >= 3:
                            dve.wait_ge(y_saved[1 - u], i * 16 + ((c - 1) // 2) * 16)
                        dve.sem_inc(k["apart"], 1)
                        dve.tensor_copy(y[1 - u][:, 512:D], y_ps[1][:, :]).then_inc(y_dve, 1)

                run(dve, step)
                for t in range(LT):
                    m0, m1 = mine[0][t % 2], mine[1][t % 2]
                    dve.wait_ge(mine_in[t % 2], 32 * (t // 2 + 1))
                    dve.tensor_scalar(m0[:, :], m0[:, :], share[:, 0, t:t + 1], None, ALU.mult)
                    dve.drain()
                    dve.scalar_tensor_tensor(out=m0[:, :], in0=m1[:, :], scalar=share[:, 1, t:t + 1], in1=m0[:, :],
                                             op0=ALU.mult, op1=ALU.add)
                    dve.drain()
                    dve.tensor_tensor(m0[:, :], m0[:, :], gate[:, :], ALU.mult)
                    dve.drain()
                    dve.tensor_tensor(k["xs"][:, t, :], k["xs"][:, t, :], m0[:, :], ALU.add).then_inc(out_ready, 1)


def stages(nc, a, k):
    norm = lambda name, groups, rows=None: stage_norm(nc, k, name, groups, k["xs"], k["hT"], rows)
    y_tile = lambda c, j: k["yT"][:, c, j * P:(j + 1) * P]
    return [
        lambda: stage_setup(nc, a, k),
        lambda: stage_modulations(nc, a, k),
        lambda: norm("norm_a", [(0, LT, ROW["norm_w"], MOD_L0, 0), (LT, CT, ROW["norm_w"], MOD_L0, 1)]),
        lambda: stage_attention_a(nc, a, k, k["yT"]),
        lambda: stage_gates(nc, a, k),
        lambda: stage_mlstm(nc, a, k, k["yT"]),
        lambda: stage_output(nc, k, "out_a", y_tile, a["w_out_ab"][0], INNER // P, range(NT),
                             [(MOD_L0 + 16, 0, 0, LT), (MOD_L0 + 16, 1, LT, CT)]),
        lambda: norm("norm_c", [(0, LT, ROW["norm_w"] + KD, MOD_L1, 0), (LT, CT, ROW["norm_w"] + KD, MOD_L1, 1)]),
        lambda: stage_gla(nc, a, k, k["yT"]),
        lambda: stage_output(nc, k, "out_c", y_tile, a["w_out_c"][0], INNER // P, range(LT),
                             [(MOD_L1 + 16, 0, 0, LT)]),
        lambda: norm("norm_1", [(0, LT, ROW["norm1_w_2"], MOD_B2, 2)]),
        lambda: stage_conv(nc, a, k, k["yT"][:, 0:4, :], k["f_rows"]),
        lambda: stage_attention_2(nc, a, k, k["yT"][:, 4:8, :], k["f_rows"]),
        lambda: stage_merge(nc, a, k, k["yT"][:, 0:4, :], k["yT"][:, 4:8, :], k["yT"][:, 8:16, :]),
        lambda: stage_output(nc, k, "out_2", lambda c, j: y_tile(8 + c, j), a["w_o_2"][0], KD, range(LT),
                             [(MOD_B2 + 16, 2, 0, LT)]),
        lambda: norm("norm_2", [(0, LT, ROW["norm2_w_2"], MOD_B2 + 24, 2)], k["xn_rows"]),
        lambda: stage_moe(nc, a, k),
    ]


def constants():
    f = np.float32
    c = {"ident": np.eye(P, dtype=f), "flip": np.ascontiguousarray(np.eye(P, dtype=f)[::-1])}
    col = np.arange(GRID_W)
    start = np.clip(col - WIN_W // 2, 0, GRID_W - WIN_W)
    kinds = []
    for t in (0, 1, 3):
        keys = range(max(0, t - 1), min(LT, t + 2))
        m = np.zeros((GRID_H, COLS, len(keys), GRID_H, COLS), f)
        for ci in range(COLS):
            q = COLS * t + ci
            for n, kt in enumerate(keys):
                kc = COLS * kt + np.arange(COLS)
                ok = (kc >= start[q]) & (kc < start[q] + WIN_W)
                m[:, ci, n, :, ~ok] = NEG
        kinds.append(m.reshape(P, -1))
    c["na_mask"] = np.concatenate(kinds, axis=1)
    freqs = (f(10000.0) ** (-np.arange(64, dtype=f) / f(64))).astype(f)
    t = np.arange(SEQ)
    ang = np.stack([(t // GRID_W).astype(f)[:, None] * freqs, (t % GRID_W).astype(f)[:, None] * freqs], axis=1)
    tiles = ang.reshape(LT, P, 2, 64).transpose(1, 0, 2, 3)
    c["rope_cos"] = np.cos(tiles).astype(f)
    c["rope_sin"] = np.sin(tiles).astype(f)
    i = np.arange(P)
    c["tri"] = np.stack([np.where(i[None] > i[:, None], NEG, 0), np.where(i[None] < i[:, None], NEG, 0)], axis=1).astype(f)
    d = i[:, None] ^ i[None]
    c["level_masks"] = np.stack([(d >= w) & (d < 2 * w) for w in HG_LEVELS if w < P], axis=1).astype(np.int32)
    c["causal"] = np.concatenate([np.where(np.arange((n + 1) * P)[None] > n * P + i[:, None], NEG, 0)
                                  for n in range(LT)], axis=1).astype(f)
    c["before"] = (i[:, None] < i[None]).astype(f)
    c["block_ids"] = np.arange(BLOCKS, dtype=f)[None]
    c["token_ids"] = (i[:, None] + P * np.arange(LT)[None]).astype(np.uint32)
    c["iota8"] = np.tile(np.arange(8, dtype=f), (P, 1))
    return c


def program(nc, a):
    with ExitStack() as ctx:
        def sb(name, shape, dt=F32):
            return ctx.enter_context(nc.sbuf_tensor(name, shape, dt))

        k = {"xs": sb("xs", [P, NT, D]), "hT": sb("hT", [P, KD, NTOK]), "ident": sb("ident", [P, P]),
             "vecT": sb("vecT", [P, NVEC]), "biasT": sb("biasT", [P, NMOD]), "modT": sb("modT", [P, NMOD, 3]),
             "silu_c": sb("silu_c", [P, KD, 3]), "lbT": sb("lbT", [P, 2, HG_HEADS]),
             "yT": sb("yT", [P, INNER // P, NTOK]),
             "m_cols": sb("m_cols", [P, NT, 4, ML_HEADS]),
             "a_rows": nc.dram_tensor("a_rows", (2, ML_HEADS, NTOK), F32, kind="Internal").ap(),
             "xn_rows": nc.dram_tensor("xn_rows", (SEQ, D), F32, kind="Internal").ap(),
             "y_rows": nc.dram_tensor("y_rows", (BLOCKS * P, D), F32, kind="Internal").ap(),
             "slot_token": nc.dram_tensor("slot_token", (BLOCKS * P, 1), U32, kind="Internal").ap(),
             "f_rows": nc.dram_tensor("f_rows", (8, SEQ), F32, kind="Internal").ap(),
             "rpb_pad": nc.dram_tensor("rpb_pad", (16, RPB_H, RPB_PAD), F32, kind="Internal").ap(),
             "apart": ctx.enter_context(nc.semaphore("apart"))}
        for stage in stages(nc, a, k):
            stage()



_INS = ["x", "c", "ctx", "c_ctx", "norm_w", "w_ada", "b_ada", "w_in_ab", "b_gate_ab", "q_norm_a", "k_norm_a", "rpb_a",
        "h_norm_b", "w_out_ab", "w_in_c", "lb_c", "h_norm_c", "w_out_c", "c_2", "w_ada_2", "b_ada_2", "norm1_w_2",
        "w_in_2", "b_forget_2", "conv_w_2", "q_norm_w_2", "k_norm_w_2", "w_out_conv_2", "w_out_attn_2", "w_o_2",
        "norm2_w_2", "w_router_group_2", "b_router_group_2", "w_router_expert_2", "b_router_expert_2",
        "w_gate_2", "w_up_2", "w_down_2"]


def kernel(**inputs):
    import numpy as _np
    import concourse.bacc as _bacc
    from concourse import mybir as _mybir
    from concourse.bass_utils import run_bass_kernel_spmd as _run

    nc = _bacc.Bacc("TRN2", target_bir_lowering=False, num_devices=1)
    arrays = {n: _np.ascontiguousarray(inputs[n]) for n in _INS}
    arrays |= constants()
    a = {n: nc.dram_tensor(f"in_{n}", v.shape, _mybir.dt.from_np(v.dtype), kind="ExternalInput").ap()
         for n, v in arrays.items()}
    a["out"] = nc.dram_tensor("out_x", (1, SEQ, D), F32, kind="ExternalOutput").ap()
    program(nc, a)
    r = _run(nc, [{f"in_{n}": v for n, v in arrays.items()}], core_ids=[0])
    return r.results[0]["out_x"]
```
